# Optimizing a Trainium2 kernel written in Bass

```python
import math
import jax, jax.numpy as jnp
from jax import lax
import numpy as np

D_MODEL = 1024
BATCH = 1
SEQ = 256
DEPTH = 2

N_A_LAYERS = DEPTH // 2
N_B_LAYERS = DEPTH - N_A_LAYERS

A_CHUNK = 128
A_GROUPS = 8
A_WIDTH = 2 * D_MODEL
A_GROUP_DIM = A_WIDTH // A_GROUPS

B_HEADS = 16
B_HEAD_DIM = D_MODEL // B_HEADS
B_BLOCK = 256
B_TOPK = 3
B_QCHUNK = 32

N_EXPERTS = 64
TOP_K = 8
N_GROUPS = 8
TOPK_GROUPS = 4
EXPERT_DIM = 256
SHARED_DIM = 256
ROUTED_SCALE = 2.5
MOE_ROW_BLOCK = 128

RMS_EPS = 1e-6
LN_EPS = 1e-5
NEG_INF = -1e30


def rmsnorm(x, g):
    xf = x.astype(jnp.float32)
    y = xf * lax.rsqrt(jnp.mean(xf * xf, axis=-1, keepdims=True) + RMS_EPS)
    return y.astype(x.dtype) * g

def layernorm(x, g, b):
    xf = x.astype(jnp.float32)
    mu = jnp.mean(xf, axis=-1, keepdims=True)
    var = jnp.mean(jnp.square(xf - mu), axis=-1, keepdims=True)
    y = (xf - mu) * lax.rsqrt(var + LN_EPS)
    return y.astype(x.dtype) * g + b

def ada(c, w, b, n):
    m = jax.nn.silu(c) @ w + b
    return [t[:, None, :] for t in jnp.split(m, n, axis=-1)]

def modulate(h, shift, scale):
    return h * (1 + scale) + shift

def swiglu(x, wg, wu, wd):
    return (jax.nn.silu(x @ wg) * (x @ wu)) @ wd

def gmlp_mixer(h, w_in, b_in, ln_g, ln_b, w_s, b_s, w_out):
    B, S, _ = h.shape
    z = jax.nn.gelu(h @ w_in + b_in)
    u, v = jnp.split(z, 2, axis=-1)
    v = layernorm(v, ln_g, ln_b)
    nc = S // A_CHUNK
    v = v.reshape(B, nc, A_CHUNK, A_GROUPS, A_GROUP_DIM)
    causal = jnp.tril(jnp.ones((A_CHUNK, A_CHUNK), dtype=bool))
    w = jnp.where(causal[None], w_s, 0)
    sv = jnp.einsum('gts,bcsgd->bctgd', w, v) + b_s.T[None, None, :, :, None]
    y = u * sv.reshape(B, S, A_WIDTH)
    return y @ w_out

def shared_kv(x, c, g, w_ada, b_ada, w_k, w_v):
    shift, scale = ada(c, w_ada, b_ada, 2)
    h = modulate(rmsnorm(x, g), shift, scale)
    B, S, _ = h.shape
    k = (h @ w_k).reshape(B, S, B_HEADS, B_HEAD_DIM).transpose(0, 2, 1, 3)
    v = (h @ w_v).reshape(B, S, B_HEADS, B_HEAD_DIM).transpose(0, 2, 1, 3)
    nb = -(-S // B_BLOCK)
    pad = nb * B_BLOCK - S
    k = jnp.pad(k, ((0, 0), (0, 0), (0, pad), (0, 0)))
    v = jnp.pad(v, ((0, 0), (0, 0), (0, pad), (0, 0)))
    kb = k.reshape(B, B_HEADS, nb, B_BLOCK, B_HEAD_DIM)
    vb = v.reshape(B, B_HEADS, nb, B_BLOCK, B_HEAD_DIM)
    kmean = jnp.mean(kb, axis=3)
    return kb, vb, kmean

def moba_attention(q, kb, vb, kmean):
    B, H, S, dh = q.shape
    nb = kb.shape[2]
    n_sel = min(B_TOPK, nb - 1)
    scale = dh ** -0.5
    nqc = S // B_QCHUNK
    qc = q.reshape(B, H, nqc, B_QCHUNK, dh).transpose(0, 2, 1, 3, 4)
    head_idx = jnp.arange(H)[:, None, None]

    def one_seq(args):
        q_s, kb_s, vb_s, km_s = args

        def one_chunk(args2):
            ci, q_c = args2
            start = ci * B_QCHUNK
            own = start // B_BLOCK
            qpos = start + jnp.arange(B_QCHUNK)
            kpos = own * B_BLOCK + jnp.arange(B_BLOCK)
            k_own = lax.dynamic_index_in_dim(kb_s, own, axis=1, keepdims=False)
            v_own = lax.dynamic_index_in_dim(vb_s, own, axis=1, keepdims=False)
            s_own = jnp.einsum('hqd,hjd->hqj', q_c, k_own).astype(jnp.float32) * scale
            s_own = jnp.where((kpos[None, :] <= qpos[:, None])[None], s_own, NEG_INF)
            if n_sel > 0:
                gate = jnp.einsum('hqd,hnd->hqn', q_c, km_s).astype(jnp.float32)
                past = jnp.arange(nb) < own
                gate = jnp.where(past[None, None, :], gate, NEG_INF)
                _, idx = lax.top_k(gate, n_sel)
                valid = idx < own
                k_sel = kb_s[head_idx, idx]
                v_sel = vb_s[head_idx, idx]
                s_sel = jnp.einsum('hqd,hqnjd->hqnj', q_c, k_sel).astype(jnp.float32) * scale
                s_sel = jnp.where(valid[..., None], s_sel, NEG_INF)
                s = jnp.concatenate([s_sel.reshape(H, B_QCHUNK, n_sel * B_BLOCK), s_own], axis=-1)
                p = jax.nn.softmax(s, axis=-1).astype(v_own.dtype)
                p_sel = p[..., :n_sel * B_BLOCK].reshape(H, B_QCHUNK, n_sel, B_BLOCK)
                p_own = p[..., n_sel * B_BLOCK:]
                o = (jnp.einsum('hqnj,hqnjd->hqd', p_sel, v_sel)
                     + jnp.einsum('hqj,hjd->hqd', p_own, v_own))
            else:
                p = jax.nn.softmax(s_own, axis=-1).astype(v_own.dtype)
                o = jnp.einsum('hqj,hjd->hqd', p, v_own)
            return o

        return lax.map(one_chunk, (jnp.arange(nqc), q_s))

    o = lax.map(one_seq, (qc, kb, vb, kmean))
    return o.transpose(0, 2, 1, 3, 4).reshape(B, H, S, dh)

def moba_mixer(h, w_q, w_o, kb, vb, kmean):
    B, S, D = h.shape
    q = (h @ w_q).reshape(B, S, B_HEADS, B_HEAD_DIM).transpose(0, 2, 1, 3)
    o = moba_attention(q, kb, vb, kmean)
    return o.transpose(0, 2, 1, 3).reshape(B, S, D) @ w_o

def grouped_experts(xt, eidx, w, w_gate, w_up, w_down):
    T, D = xt.shape
    K = eidx.shape[1]
    E, M = N_EXPERTS, MOE_ROW_BLOCK
    TK = T * K
    e_flat = eidx.reshape(TK)
    tok_flat = jnp.arange(TK, dtype=jnp.int32) // K
    w_flat = w.reshape(TK)
    order = jnp.argsort(e_flat)
    e_sorted = e_flat[order]
    tok_sorted = tok_flat[order]
    w_sorted = w_flat[order]
    counts = jnp.zeros((E,), jnp.int32).at[e_flat].add(1)
    starts = jnp.cumsum(counts) - counts
    padded = ((counts + M - 1) // M) * M
    pad_ends = jnp.cumsum(padded)
    pad_starts = pad_ends - padded
    rank = jnp.arange(TK, dtype=jnp.int32) - starts[e_sorted]
    dest = pad_starts[e_sorted] + rank
    n_blocks = -(-(TK + E * (M - 1)) // M)
    R = n_blocks * M
    x_pad = jnp.zeros((R, D), xt.dtype).at[dest].set(xt[tok_sorted])
    block_start = jnp.arange(n_blocks, dtype=jnp.int32) * M
    block_expert = jnp.minimum(jnp.sum(pad_ends[None, :] <= block_start[:, None], axis=1), E - 1)

    def run_block(args):
        xb, e = args
        return swiglu(xb, w_gate[e], w_up[e], w_down[e])

    y_pad = lax.map(run_block, (x_pad.reshape(n_blocks, M, D), block_expert)).reshape(R, D)
    y = y_pad[dest] * w_sorted[:, None].astype(xt.dtype)
    return jax.ops.segment_sum(y, tok_sorted, num_segments=T)

def moe(h, w_router, e_bias, w_gate, w_up, w_down, ws_gate, ws_up, ws_down):
    B, S, D = h.shape
    T = B * S
    xt = h.reshape(T, D)
    scores = jax.nn.sigmoid((xt @ w_router).astype(jnp.float32))
    choice = scores + e_bias.astype(jnp.float32)
    grp = choice.reshape(T, N_GROUPS, N_EXPERTS // N_GROUPS)
    grp_score = jnp.sum(lax.top_k(grp, 2)[0], axis=-1)
    _, gidx = lax.top_k(grp_score, TOPK_GROUPS)
    gmask = jnp.sum(jax.nn.one_hot(gidx, N_GROUPS, dtype=jnp.float32), axis=1) > 0
    emask = jnp.repeat(gmask, N_EXPERTS // N_GROUPS, axis=1)
    choice = jnp.where(emask, choice, NEG_INF)
    _, eidx = lax.top_k(choice, TOP_K)
    w = jnp.take_along_axis(scores, eidx, axis=1)
    w = w / jnp.sum(w, axis=-1, keepdims=True) * ROUTED_SCALE
    routed = grouped_experts(xt, eidx, w, w_gate, w_up, w_down)
    shared = swiglu(xt, ws_gate, ws_up, ws_down)
    return (routed + shared).reshape(B, S, D)

def first_inputs(seed: int = 0) -> dict:
    key = jax.random.key(seed)
    ks = jax.random.split(key, 32)
    f32 = jnp.float32

    def nrm(k, shape, s):
        return jax.random.normal(k, shape, f32) * s

    D = D_MODEL
    return {
        'x': nrm(ks[0], (BATCH, SEQ, D), 1.0),
        'c': nrm(ks[1], (BATCH, D), 1.0),
        'ada_w': nrm(ks[2], (DEPTH, D, 6 * D), 0.2 * D ** -0.5),
        'ada_b': nrm(ks[3], (DEPTH, 6 * D), 0.02),
        'norm_mix': 1.0 + nrm(ks[4], (DEPTH, D), 0.02),
        'norm_ffn': 1.0 + nrm(ks[5], (DEPTH, D), 0.02),
        'a_w_in': nrm(ks[6], (N_A_LAYERS, D, 2 * A_WIDTH), D ** -0.5),
        'a_b_in': nrm(ks[7], (N_A_LAYERS, 2 * A_WIDTH), 0.02),
        'a_ln_g': 1.0 + nrm(ks[8], (N_A_LAYERS, A_WIDTH), 0.02),
        'a_ln_b': nrm(ks[9], (N_A_LAYERS, A_WIDTH), 0.02),
        'a_w_s': nrm(ks[10], (N_A_LAYERS, A_GROUPS, A_CHUNK, A_CHUNK), 0.5 * A_CHUNK ** -0.5),
        'a_b_s': 1.0 + nrm(ks[11], (N_A_LAYERS, A_GROUPS, A_CHUNK), 0.02),
        'a_w_out': nrm(ks[12], (N_A_LAYERS, A_WIDTH, D), A_WIDTH ** -0.5),
        'kv_norm': 1.0 + nrm(ks[13], (D,), 0.02),
        'kv_ada_w': nrm(ks[14], (D, 2 * D), 0.2 * D ** -0.5),
        'kv_ada_b': nrm(ks[15], (2 * D,), 0.02),
        'kv_w_k': nrm(ks[16], (D, D), D ** -0.5),
        'kv_w_v': nrm(ks[17], (D, D), D ** -0.5),
        'b_w_q': nrm(ks[18], (N_B_LAYERS, D, D), D ** -0.5),
        'b_w_o': nrm(ks[19], (N_B_LAYERS, D, D), D ** -0.5),
        'moe_router': nrm(ks[20], (DEPTH, D, N_EXPERTS), D ** -0.5),
        'moe_bias': nrm(ks[21], (DEPTH, N_EXPERTS), 0.01),
        'moe_w_gate': nrm(ks[22], (DEPTH, N_EXPERTS, D, EXPERT_DIM), D ** -0.5),
        'moe_w_up': nrm(ks[23], (DEPTH, N_EXPERTS, D, EXPERT_DIM), D ** -0.5),
        'moe_w_down': nrm(ks[24], (DEPTH, N_EXPERTS, EXPERT_DIM, D), EXPERT_DIM ** -0.5),
        'sh_w_gate': nrm(ks[25], (DEPTH, D, SHARED_DIM), D ** -0.5),
        'sh_w_up': nrm(ks[26], (DEPTH, D, SHARED_DIM), D ** -0.5),
        'sh_w_down': nrm(ks[27], (DEPTH, SHARED_DIM, D), SHARED_DIM ** -0.5),
        'final_norm': 1.0 + nrm(ks[28], (D,), 0.02),
    }

def first_block(x, c, ada_w, ada_b, norm_mix, norm_ffn, a_w_in, a_b_in, a_ln_g, a_ln_b,
              a_w_s, a_b_s, a_w_out, kv_norm, kv_ada_w, kv_ada_b, kv_w_k, kv_w_v,
              b_w_q, b_w_o, moe_router, moe_bias, moe_w_gate, moe_w_up, moe_w_down,
              sh_w_gate, sh_w_up, sh_w_down, final_norm):
    kv = None
    for i in range(DEPTH):
        sh1, sc1, g1, sh2, sc2, g2 = ada(c, ada_w[i], ada_b[i], 6)
        h = modulate(rmsnorm(x, norm_mix[i]), sh1, sc1)
        if i < N_A_LAYERS:
            y = gmlp_mixer(h, a_w_in[i], a_b_in[i], a_ln_g[i], a_ln_b[i],
                           a_w_s[i], a_b_s[i], a_w_out[i])
        else:
            if kv is None:
                kv = shared_kv(x, c, kv_norm, kv_ada_w, kv_ada_b, kv_w_k, kv_w_v)
            j = i - N_A_LAYERS
            y = moba_mixer(h, b_w_q[j], b_w_o[j], kv[0], kv[1], kv[2])
        x = x + g1 * y
        h = modulate(rmsnorm(x, norm_ffn[i]), sh2, sc2)
        x = x + g2 * moe(h, moe_router[i], moe_bias[i], moe_w_gate[i], moe_w_up[i],
                         moe_w_down[i], sh_w_gate[i], sh_w_up[i], sh_w_down[i])
    return rmsnorm(x, final_norm)


DEPTH_2 = 4

N_MIXERS = 3
BLOCK = 128
ROPE_THETA = 10000.0
NORM_EPS = 1e-6

A_HEADS = 8
A_HEAD_DIM = D_MODEL // (2 * A_HEADS)
A_V_DIM = 2 * A_HEAD_DIM
A_IN = 4 * A_HEADS * A_HEAD_DIM + A_HEADS * A_V_DIM

B_HEAD_DIM_2 = D_MODEL // B_HEADS
B_IN = 3 * B_HEADS * B_HEAD_DIM_2

C_HEADS = 16
C_KV_HEADS = 2
C_GROUP = C_HEADS // C_KV_HEADS
C_HEAD_DIM = 64
WINDOW = 128
C_IN = (C_HEADS + 2 * C_KV_HEADS) * C_HEAD_DIM

ROPE_DIM = 64

FFN_HIDDEN = -(-8 * D_MODEL // (3 * 256)) * 256

N_A = (DEPTH_2 + 2) // 3
N_B = (DEPTH_2 + 1) // 3
N_C = DEPTH_2 // 3


def rms_norm(x, g):
    xf = x.astype(jnp.float32)
    y = xf * lax.rsqrt(jnp.mean(xf * xf, axis=-1, keepdims=True) + NORM_EPS)
    return (y * g.astype(jnp.float32)).astype(x.dtype)

def rope_tables(positions):
    inv = ROPE_THETA ** (-jnp.arange(0, ROPE_DIM, 2, dtype=jnp.float32) / ROPE_DIM)
    ang = positions.astype(jnp.float32)[..., None] * inv
    return jnp.cos(ang), jnp.sin(ang)

def apply_rope(x, cos, sin):
    xf = x.astype(jnp.float32)
    x1, x2 = jnp.split(xf, 2, axis=-1)
    c = cos[:, :, None, :]
    s = sin[:, :, None, :]
    return jnp.concatenate([x1 * c - x2 * s, x2 * c + x1 * s], axis=-1).astype(x.dtype)

def diff_attention(h, w_in, w_out, lam_params, subln_g, cos, sin, layer_idx):
    b, s, _ = h.shape
    nblk = s // BLOCK
    qkv = h @ w_in
    nq = 2 * A_HEADS * A_HEAD_DIM
    q, k, v = jnp.split(qkv, [nq, 2 * nq], axis=-1)
    q = apply_rope(q.reshape(b, s, 2 * A_HEADS, A_HEAD_DIM), cos, sin).reshape(b, s, A_HEADS, 2, A_HEAD_DIM)
    k = apply_rope(k.reshape(b, s, 2 * A_HEADS, A_HEAD_DIM), cos, sin).reshape(b, s, A_HEADS, 2, A_HEAD_DIM)
    v = v.reshape(b, s, A_HEADS, A_V_DIM)
    lam_init = 0.8 - 0.6 * math.exp(-0.3 * layer_idx)
    lp = lam_params.astype(jnp.float32)
    lam = jnp.exp(jnp.sum(lp[0] * lp[1])) - jnp.exp(jnp.sum(lp[2] * lp[3])) + lam_init
    scale = A_HEAD_DIM ** -0.5
    kpos = jnp.arange(s)
    q_blocks = jnp.moveaxis(q.reshape(b, nblk, BLOCK, A_HEADS, 2, A_HEAD_DIM), 1, 0)

    def block(args):
        qb, i = args
        sc = jnp.einsum('bqhcd,bkhcd->bhcqk', qb, k).astype(jnp.float32) * scale
        qpos = i * BLOCK + jnp.arange(BLOCK)
        causal = kpos[None, :] <= qpos[:, None]
        p = jax.nn.softmax(jnp.where(causal, sc, -jnp.inf), axis=-1)
        wts = p[:, :, 0] - lam * p[:, :, 1]
        return jnp.einsum('bhqk,bkhe->bqhe', wts.astype(v.dtype), v)

    o = lax.map(block, (q_blocks, jnp.arange(nblk)))
    o = jnp.moveaxis(o, 0, 1).reshape(b, s, A_HEADS, A_V_DIM)
    o = rms_norm(o, subln_g) * (1.0 - lam_init)
    return o.reshape(b, s, A_HEADS * A_V_DIM) @ w_out

def stick_breaking_attention(h, w_in, w_out):
    b, s, _ = h.shape
    nblk = s // BLOCK
    qkv = h @ w_in
    q, k, v = jnp.split(qkv, 3, axis=-1)
    q = q.reshape(b, s, B_HEADS, B_HEAD_DIM_2)
    k = k.reshape(b, s, B_HEADS, B_HEAD_DIM_2)
    v = v.reshape(b, s, B_HEADS, B_HEAD_DIM_2)
    scale = B_HEAD_DIM_2 ** -0.5
    kpos = jnp.arange(s)
    q_blocks = jnp.moveaxis(q.reshape(b, nblk, BLOCK, B_HEADS, B_HEAD_DIM_2), 1, 0)

    def block(args):
        qb, i = args
        z = jnp.einsum('bqhd,bkhd->bhqk', qb, k).astype(jnp.float32) * scale
        qpos = i * BLOCK + jnp.arange(BLOCK)
        strict = kpos[None, :] < qpos[:, None]
        log_beta = jax.nn.log_sigmoid(z)
        log_1m_beta = jnp.where(strict, jax.nn.log_sigmoid(-z), 0.0)
        suffix = lax.cumsum(log_1m_beta, axis=3, reverse=True) - log_1m_beta
        a = jnp.where(strict, jnp.exp(log_beta + suffix), 0.0)
        return jnp.einsum('bhqk,bkhd->bqhd', a.astype(v.dtype), v)

    o = lax.map(block, (q_blocks, jnp.arange(nblk)))
    o = jnp.moveaxis(o, 0, 1).reshape(b, s, B_HEADS * B_HEAD_DIM_2)
    return o @ w_out

def sliding_window_sink_attention(h, w_in, w_out, sinks, cos, sin):
    b, s, _ = h.shape
    nblk = s // WINDOW
    qkv = h @ w_in
    nq = C_HEADS * C_HEAD_DIM
    nkv = C_KV_HEADS * C_HEAD_DIM
    q, k, v = jnp.split(qkv, [nq, nq + nkv], axis=-1)
    q = apply_rope(q.reshape(b, s, C_HEADS, C_HEAD_DIM), cos, sin)
    k = apply_rope(k.reshape(b, s, C_KV_HEADS, C_HEAD_DIM), cos, sin)
    v = v.reshape(b, s, C_KV_HEADS, C_HEAD_DIM)
    qb = q.reshape(b, nblk, WINDOW, C_KV_HEADS, C_GROUP, C_HEAD_DIM)
    kb = k.reshape(b, nblk, WINDOW, C_KV_HEADS, C_HEAD_DIM)
    vb = v.reshape(b, nblk, WINDOW, C_KV_HEADS, C_HEAD_DIM)
    pad = ((0, 0), (1, 0), (0, 0), (0, 0), (0, 0))
    kwin = jnp.concatenate([jnp.pad(kb[:, :-1], pad), kb], axis=2)
    vwin = jnp.concatenate([jnp.pad(vb[:, :-1], pad), vb], axis=2)
    sc = jnp.einsum('bnqcgd,bnkcd->bncgqk', qb, kwin).astype(jnp.float32) * (C_HEAD_DIM ** -0.5)
    qi = jnp.arange(WINDOW)[:, None]
    ki = jnp.arange(2 * WINDOW)[None, :]
    rel = WINDOW + qi - ki
    band = (rel >= 0) & (rel < WINDOW)
    in_seq = (jnp.arange(nblk)[:, None] * WINDOW + jnp.arange(2 * WINDOW)[None, :] - WINDOW) >= 0
    mask = band[None] & in_seq[:, None, :]
    sc = jnp.where(mask[None, :, None, None], sc, -jnp.inf)
    sink = sinks.astype(jnp.float32).reshape(C_KV_HEADS, C_GROUP)[None, None, :, :, None, None]
    m = jnp.maximum(jnp.max(sc, axis=-1, keepdims=True), sink)
    p = jnp.exp(sc - m)
    probs = p / (jnp.sum(p, axis=-1, keepdims=True) + jnp.exp(sink - m))
    o = jnp.einsum('bncgqk,bnkcd->bnqcgd', probs.astype(v.dtype), vwin)
    return o.reshape(b, s, C_HEADS * C_HEAD_DIM) @ w_out

def swiglu_2(h, w_gate, w_up, w_down):
    return (jax.nn.silu(h @ w_gate) * (h @ w_up)) @ w_down

def second_inputs(seed: int = 0) -> dict:
    key = jax.random.key(seed)
    ks = jax.random.split(key, 16)
    f32 = jnp.float32

    def dense(k, shape, fan_in):
        return jax.random.normal(k, shape, f32) * (fan_in ** -0.5)

    x = jax.random.normal(ks[0], (BATCH, SEQ, D_MODEL), f32)
    positions = jnp.broadcast_to(jnp.arange(SEQ, dtype=jnp.int32)[None, :], (BATCH, SEQ))
    norm_gains = 1.0 + 0.02 * jax.random.normal(ks[1], (DEPTH_2, 4, D_MODEL), f32)
    a_w_in = dense(ks[2], (N_A, D_MODEL, A_IN), D_MODEL)
    a_w_out = dense(ks[3], (N_A, A_HEADS * A_V_DIM, D_MODEL), A_HEADS * A_V_DIM)
    a_lambda = 0.1 * jax.random.normal(ks[4], (N_A, 4, A_HEAD_DIM), f32)
    a_subln = 1.0 + 0.02 * jax.random.normal(ks[5], (N_A, A_V_DIM), f32)
    b_w_in = dense(ks[6], (N_B, D_MODEL, B_IN), D_MODEL)
    b_w_out = dense(ks[7], (N_B, B_HEADS * B_HEAD_DIM_2, D_MODEL), B_HEADS * B_HEAD_DIM_2)
    c_w_in = dense(ks[8], (N_C, D_MODEL, C_IN), D_MODEL)
    c_w_out = dense(ks[9], (N_C, C_HEADS * C_HEAD_DIM, D_MODEL), C_HEADS * C_HEAD_DIM)
    c_sinks = 0.5 * jax.random.normal(ks[10], (N_C, C_HEADS), f32)
    ffn_w_gate = dense(ks[11], (DEPTH_2, D_MODEL, FFN_HIDDEN), D_MODEL)
    ffn_w_up = dense(ks[12], (DEPTH_2, D_MODEL, FFN_HIDDEN), D_MODEL)
    ffn_w_down = dense(ks[13], (DEPTH_2, FFN_HIDDEN, D_MODEL), FFN_HIDDEN)
    return {"x": x, "positions": positions, "norm_gains": norm_gains,
            "a_w_in": a_w_in, "a_w_out": a_w_out, "a_lambda": a_lambda, "a_subln": a_subln,
            "b_w_in": b_w_in, "b_w_out": b_w_out,
            "c_w_in": c_w_in, "c_w_out": c_w_out, "c_sinks": c_sinks,
            "ffn_w_gate": ffn_w_gate, "ffn_w_up": ffn_w_up, "ffn_w_down": ffn_w_down}

def second_block(x, positions, norm_gains, a_w_in, a_w_out, a_lambda, a_subln,
              b_w_in, b_w_out, c_w_in, c_w_out, c_sinks,
              ffn_w_gate, ffn_w_up, ffn_w_down):
    cos, sin = rope_tables(positions)
    for i in range(DEPTH_2):
        kind = i % N_MIXERS
        inst = i // N_MIXERS
        hn = rms_norm(x, norm_gains[i, 0])
        if kind == 0:
            m = diff_attention(hn, a_w_in[inst], a_w_out[inst], a_lambda[inst], a_subln[inst], cos, sin, i)
        elif kind == 1:
            m = stick_breaking_attention(hn, b_w_in[inst], b_w_out[inst])
        else:
            m = sliding_window_sink_attention(hn, c_w_in[inst], c_w_out[inst], c_sinks[inst], cos, sin)
        x = x + rms_norm(m, norm_gains[i, 1])
        f = swiglu_2(rms_norm(x, norm_gains[i, 2]), ffn_w_gate[i], ffn_w_up[i], ffn_w_down[i])
        x = x + rms_norm(f, norm_gains[i, 3])
    return x


def setup_inputs(seed=0):
    out = dict(first_inputs(seed))
    for name, value in second_inputs(seed + 1).items():
        if name != "x":
            out[name + "_2"] = value
    return out


def reference(
    x, c, ada_w, ada_b, norm_mix, norm_ffn, a_w_in, a_b_in, a_ln_g, a_ln_b, a_w_s, a_b_s,
    a_w_out, kv_norm, kv_ada_w, kv_ada_b, kv_w_k, kv_w_v, b_w_q, b_w_o, moe_router, moe_bias,
    moe_w_gate, moe_w_up, moe_w_down, sh_w_gate, sh_w_up, sh_w_down, final_norm, positions_2,
    norm_gains_2, a_w_in_2, a_w_out_2, a_lambda_2, a_subln_2, b_w_in_2, b_w_out_2, c_w_in_2,
    c_w_out_2, c_sinks_2, ffn_w_gate_2, ffn_w_up_2, ffn_w_down_2,
):
    x = first_block(
        x, c, ada_w, ada_b, norm_mix, norm_ffn, a_w_in, a_b_in, a_ln_g, a_ln_b, a_w_s, a_b_s,
        a_w_out, kv_norm, kv_ada_w, kv_ada_b, kv_w_k, kv_w_v, b_w_q, b_w_o, moe_router,
        moe_bias, moe_w_gate, moe_w_up, moe_w_down, sh_w_gate, sh_w_up, sh_w_down, final_norm,
    )
    return second_block(
        x, positions_2, norm_gains_2, a_w_in_2, a_w_out_2, a_lambda_2, a_subln_2, b_w_in_2,
        b_w_out_2, c_w_in_2, c_w_out_2, c_sinks_2, ffn_w_gate_2, ffn_w_up_2, ffn_w_down_2,
    )


_drawn_inputs = setup_inputs


def setup_inputs(seed=0):
    import zlib

    import numpy as np

    out = dict(_drawn_inputs(seed))
    spreads = {}
    factors = {'norm_mix': 6.261,
     'a_b_in': 4.754,
     'a_ln_g': 8.0,
     'a_ln_b': 8.0,
     'a_b_s': 5.034,
     'kv_norm': 8.0,
     'kv_ada_b': 2.694,
     'c_sinks_2': 4.524,
     'norm_ffn': 5.451,
     'moe_bias': 4.111}
    for name, (base, spread) in spreads.items():
        noise = np.random.default_rng([zlib.crc32(name.encode()), seed]).standard_normal(out[name].shape)
        drawn = base * np.exp(spread * noise) if base else spread * noise
        out[name] = __import__('jax').numpy.asarray(drawn.astype(out[name].dtype))
    for name, factor in factors.items():
        out[name] = (out[name] * factor).astype(out[name].dtype)
    return out
```

```python
import math
from contextlib import ExitStack

import concourse.bass as bass
from concourse import mybir

F32 = mybir.dt.float32
F32R = mybir.dt.float32r
I32 = mybir.dt.int32
ALU = mybir.AluOpType
ACT = mybir.ActivationFunctionType
AX = mybir.AxisListType.X

P = 128
NEG = -1e30
RMS_EPS = 1e-6
LN_EPS = 1e-5
ROUTED_SCALE = 2.5
ROPE_THETA = 10000.0
HD = 64
ATT_SCALE = HD ** -0.5


def at(base, i, step):
    return base if i is None else base + i * step


class Sem:

    def __init__(self, ctx, nc, name):
        self.h = ctx.enter_context(nc.semaphore(name))
        self.n = 0


class Chain:

    def __init__(self, eng, sem):
        self.eng, self.sem, self.i, self.step = eng, sem, None, 0

    def __call__(self, ins):
        self.sem.n += 1
        ins.then_inc(self.sem.h, 1)
        self.eng.wait_ge(self.sem.h, at(self.sem.n, self.i, self.step))


def build(nc, a, out, stop=None):
    S, D = a["x"].shape[1:]
    M = S // P
    K8 = D // P
    NB = 512
    HALF = K8 // 2
    E = a["moe_router"].shape[2]
    EH = a["moe_w_gate"].shape[3]
    AW = a["a_w_out"].shape[1]
    NG = a["a_w_s"].shape[1]
    FFN = a["ffn_w_gate_2"].shape[2]
    assert M == 2 and K8 == 8 and EH == 2 * P and FFN % EH == 0

    with ExitStack() as top:
        names = {}

        def sb(ctx, name, shape, dt=F32):
            names[name] = names.get(name, 0) + 1
            return ctx.enter_context(nc.sbuf_tensor(f"{name}_{names[name]}", shape, dt))

        sems = {}

        def sem(name):
            if name not in sems:
                sems[name] = Sem(top, nc, name)
            return sems[name]

        x = sb(top, "x", [P, M, D])
        gu_raw = sb(top, "gu_raw", [P, 2, K8, NB])
        gu_hi = sb(top, "gu_hi", [P, K8, NB], F32R)
        gu_lo = sb(top, "gu_lo", [P, K8, NB], F32R)
        dn_raw = sb(top, "dn_raw", [P, 2, 2, D])
        dn_hi = sb(top, "dn_hi", [P, 2, D], F32R)
        dn_lo = sb(top, "dn_lo", [P, 2, D], F32R)
        hT_hi = sb(top, "hT_hi", [P, K8, S], F32R)
        hT_lo = sb(top, "hT_lo", [P, K8, S], F32R)
        ident = sb(top, "ident", [P, P])
        ones = sb(top, "ones", [P, P])
        featA = sb(top, "featA", [P, P])
        featB = sb(top, "featB", [P, P])
        featC = sb(top, "featC", [P, P])
        mods = sb(top, "mods", [P, P])
        cs = sb(top, "cs", [P, K8])
        gates = sb(top, "gates", [P, 2, D])
        gateval = sb(top, "gateval", [P, M, E + 1])
        aff = sb(top, "aff", [P, 2, K8])
        actout = sb(top, "actout", [P, D])
        consts = sb(top, "eps", [P, 2])
        eps_of = {RMS_EPS: consts[:, 0:1], LN_EPS: consts[:, 1:2]}

        psA = top.enter_context(nc.psum_tensor("psA", [P, 4, NB], F32))
        psG = top.enter_context(nc.psum_tensor("psG", [P, 2, NB], F32))
        psT = top.enter_context(nc.psum_tensor("psT", [P, 2, NB], F32))

        COL_C, COL_KVB = 112, 96

        landed = [[sem(f"gu_landed_{s}{h}") for h in range(2)] for s in range(2)]
        dn_landed = [sem(f"dn_landed_{s}") for s in range(2)]
        gu_hi_ready, gu_lo_ready, gu_used = sem("gu_hi_ready"), sem("gu_lo_ready"), sem("gu_used")
        dn_hi_ready, dn_lo_ready, dn_used = sem("dn_hi_ready"), sem("dn_lo_ready"), sem("dn_used")
        dve_step, pool_step, act_step = sem("dve_step"), sem("pool_step"), sem("act_step")

        count = {"g": 0, "d": 0}

        class Stream:

            def __init__(self, n, src, dn_src=None):
                self.n, self.src, self.dn_src = n, src, dn_src
                self.g, self.d = count["g"], count["d"]
                count["g"] += n
                if dn_src:
                    count["d"] += n

            def load_gu(self, sp, c, i=None):
                g, step = self.g + c, 0 if i is None else 2
                for h in range(2):
                    if g >= 2:
                        sp.wait_ge(gu_lo_ready.h, at(2 * g + h - 3, i, 4))
                    for q in range(2):
                        sp.dma_start(gu_raw[:, g % 2, h * HALF:(h + 1) * HALF, q * 256:(q + 1) * 256],
                                     self.src(at(c, i, step), h, q)).then_inc(landed[g % 2][h].h, 16)

            def load_dn(self, sp, c, i=None):
                d = self.d + c
                if d >= 2:
                    sp.wait_ge(dn_lo_ready.h, at(d - 1, i, 2))
                sp.dma_start(dn_raw[:, d % 2], self.dn_src(at(c, i, 2))).then_inc(dn_landed[d % 2].h, 16)

            def first_loads(self, sp):
                for c in range(min(2, self.n)):
                    self.load_gu(sp, c)
                    if self.dn_src:
                        self.load_dn(sp, c)

            def hi(self, act, c, h, i=None):
                g = self.g + c
                act.wait_ge(landed[g % 2][h].h, at(32 * (g // 2 + 1), i, 32))
                if g >= 1:
                    act.wait_ge(gu_used.h, at(2 * g + h - 1, i, 4))
                nc.scalar.activation(gu_hi[:, h * HALF:(h + 1) * HALF], gu_raw[:, g % 2, h * HALF:(h + 1) * HALF],
                                     ACT.Copy).then_inc(gu_hi_ready.h, 1)

            def lo(self, dve, c, h, i=None):
                g = self.g + c
                dve.wait_ge(gu_hi_ready.h, at(2 * g + h + 1, i, 4))
                sl = slice(h * HALF, (h + 1) * HALF)
                nc.vector.tensor_tensor(gu_lo[:, sl], gu_raw[:, g % 2, sl], gu_hi[:, sl].bitcast(F32),
                                        ALU.subtract).then_inc(gu_lo_ready.h, 1)

            def dhi(self, act, c, i=None):
                d = self.d + c
                act.wait_ge(dn_landed[d % 2].h, at(16 * (d // 2 + 1), i, 16))
                if d >= 1:
                    act.wait_ge(dn_used.h, at(d, i, 2))
                nc.scalar.activation(dn_hi[:], dn_raw[:, d % 2], ACT.Copy).then_inc(dn_hi_ready.h, 1)

            def dlo(self, dve, c, i=None):
                d = self.d + c
                dve.wait_ge(dn_hi_ready.h, at(d + 1, i, 2))
                nc.vector.tensor_tensor(dn_lo[:], dn_raw[:, d % 2], dn_hi[:].bitcast(F32),
                                        ALU.subtract).then_inc(dn_lo_ready.h, 1)

        def cols(w):
            v = w.rearrange("(k p) n -> p k n", p=P)
            last = w.shape[1] // NB if w.shape[1] % NB else -1

            def src(c, h, q):
                if isinstance(c, int) and c == last:
                    q = 0
                return v[:, h * HALF:(h + 1) * HALF, bass.ds(c * NB + q * 256, 256)]
            return Stream(-(-w.shape[1] // NB), src)

        def cols_deep(w):
            v = w.rearrange("(k p) n -> p k n", p=P)
            deep = w.shape[0] // D

            def src(c, h, q):
                k0 = (c % deep) * K8 + h * HALF
                return v[:, k0:k0 + HALF, (c // deep) * NB + q * 256:(c // deep) * NB + q * 256 + 256]
            return Stream(deep * w.shape[1] // NB, src)

        def experts(layer):
            def src(c, h, q):
                one = isinstance(c, int) and c == 0
                name = ("gate", "up")[q]
                w = a[f"sh_w_{name}"][layer] if one else \
                    a[f"moe_w_{name}"][layer, bass.ds(c - 1, 1)].rearrange("e r n -> (e r) n")
                return w.rearrange("(k p) n -> p k n", p=P)[:, h * HALF:(h + 1) * HALF]

            def dn_src(c):
                one = isinstance(c, int) and c == 0
                w = a["sh_w_down"][layer] if one else \
                    a["moe_w_down"][layer, bass.ds(c - 1, 1)].rearrange("e r n -> (e r) n")
                return w.rearrange("(k p) n -> p k n", p=P)
            return Stream(E + 1, src, dn_src)

        def ffn(layer):
            def src(c, h, q):
                w = a[("ffn_w_gate_2", "ffn_w_up_2")[q]][layer].rearrange("(k p) n -> p k n", p=P)
                return w[:, h * HALF:(h + 1) * HALF, bass.ds(c * EH, EH)]

            def dn_src(c):
                return a["ffn_w_down_2"][layer].rearrange("(c k p) n -> c p k n", p=P, k=2)[bass.ds(c, 1)] \
                    .rearrange("c p k n -> (c p) k n")
            return Stream(FFN // EH, src, dn_src)

        s_in = cols(a["a_w_in"][0])
        s_out = cols_deep(a["a_w_out"][0])
        s_moe = [experts(0)]
        s_k, s_v = cols(a["kv_w_k"]), cols(a["kv_w_v"])
        s_q, s_o = cols(a["b_w_q"][0]), cols(a["b_w_o"][0])
        s_moe.append(experts(1))
        second = []
        for layer in range(4):
            kind, inst = layer % 3, layer // 3
            n = "abc"[kind]
            second.append((cols(a[f"{n}_w_in_2"][inst]), cols(a[f"{n}_w_out_2"][inst]), ffn(layer)))
        order = [s_in, s_out, s_moe[0], s_k, s_v, s_q, s_o, s_moe[1]] + [s for t in second for s in t]

        def following(stream):
            k = order.index(stream) + 1
            return order[k] if k < len(order) else None

        def first_halves(stream):
            return range(0 if stream is order[0] else 1, 2)

        def start_act(act, stream, pre):
            def split():
                for h in first_halves(stream):
                    stream.hi(act, 0, h)
            if pre:
                pre.act(act, split)
            else:
                split()

        def start_dve(dve, stream, pre):
            def split():
                for h in first_halves(stream):
                    stream.lo(dve, 0, h)
            if pre:
                pre.dve(dve, split)
            else:
                split()

        def mm3(ps, lhs, rhs, start, stop):
            (ah, al), (bh, bl) = lhs, rhs
            nc.tensor.matmul(ps, ah, bh, start=start, stop=False)
            nc.tensor.matmul(ps, ah, bl, start=False, stop=False)
            return nc.tensor.matmul(ps, al, bh, start=False, stop=stop)

        out_free = sem("out_free")

        def project(stream, lhs, evac_act=None, evac_dve=None, deep=1, keep=False, beside=None,
                    pre=None):
            n = stream.n
            pairs = 0 if deep > 1 or keep else (n - 1) // 2
            if pairs < 2:
                pairs = 0
            free0 = out_free.n
            with nc.Block() as block:
                if beside:
                    block.gpsimd(beside)

                def turns(eng, body):
                    if pairs:
                        with eng.Fori(0, pairs) as i:
                            body(0, i)
                            body(1, i)
                    for c in range(2 * pairs, n):
                        body(c, None)

                @block.sync
                def _(sp):
                    if pre:
                        pre.sp(sp)

                    def body(c, i):
                        if i is not None or c + 2 < n:
                            stream.load_gu(sp, c + 2, i)
                    if pairs:
                        done = 2 * pairs + 2 > n
                        turns_n = pairs - 1 if done else pairs
                        with sp.Fori(0, turns_n) as i:
                            body(0, i)
                            body(1, i)
                        for c in range(2 * turns_n, n):
                            body(c, None)
                    else:
                        for c in range(n):
                            body(c, None)
                    nxt = following(stream)
                    if nxt:
                        nxt.first_loads(sp)

                @block.tensor
                def _(pe):
                    def body(c, i):
                        g, o = stream.g + c, c // deep
                        bank = 2 * (o % 2)
                        for h in range(2):
                            pe.wait_ge(gu_lo_ready.h, at(2 * g + h + 1, i, 4))
                            if h == 0 and c % deep == 0 and (o >= 2 or i is not None) and not keep:
                                pe.wait_ge(out_free.h, at(free0 + 2 * (o - 1), i, 4))
                            for k in range(h * HALF, (h + 1) * HALF):
                                if pre and c < deep and i is None:
                                    pre.wait_turned(pe, c * K8 + k)
                                for m in range(M):
                                    hi, lo = lhs(m, (c % deep) * K8 + k)
                                    dst = psA[:, 2 * m + o % 2] if keep else psA[:, bank + m]
                                    last = mm3(dst, (hi, lo), (gu_hi[:, k], gu_lo[:, k]),
                                               k == 0 and c % deep == 0, k == K8 - 1 and c % deep == deep - 1)
                            last.then_inc(gu_used.h, 1)
                    if pre:
                        pre.pe(pe)
                    if pairs:
                        body(0, None)
                        body(1, None)
                        with pe.Fori(1, pairs) as i:
                            body(0, i)
                            body(1, i)
                    for c in range(2 * pairs, n):
                        body(c, None)

                @block.scalar
                def _(act):
                    start_act(act, stream, pre)

                    def body(c, i):
                        if i is not None or c + 1 < n:
                            for h in range(2):
                                stream.hi(act, c + 1, h, i)
                        elif following(stream):
                            following(stream).hi(act, 0, 0)
                        if evac_act and c % deep == deep - 1:
                            act.wait_ge(gu_used.h, at(2 * (stream.g + c) + 2, i, 4))
                            for ins in evac_act(c // deep, i, 2 * (c // deep % 2)):
                                ins.then_inc(out_free.h, 1)
                    turns(act, body)

                @block.vector
                def _(dve):
                    start_dve(dve, stream, pre)

                    def body(c, i):
                        if i is not None or c + 1 < n:
                            for h in range(2):
                                stream.lo(dve, c + 1, h, i)
                        elif following(stream):
                            following(stream).lo(dve, 0, 0)
                        if evac_dve and c % deep == deep - 1:
                            dve.wait_ge(gu_used.h, at(2 * (stream.g + c) + 2, i, 4))
                            for ins in evac_dve(c // deep, i, 2 * (c // deep % 2)):
                                ins.then_inc(out_free.h, 1)
                    turns(dve, body)
            if not keep:
                out_free.n += 2 * (n // deep)

        def to_sbuf(dst, n_cols):
            def evac(c, i, bank):
                w = min(NB, n_cols - c * NB) if i is None else NB
                for m in range(M):
                    yield nc.scalar.activation(dst[:, m, bass.ds(at(c, i, 2) * NB, w)], psA[:, bank + m, 0:w],
                                               ACT.Copy)
            return evac

        def hT(m, k):
            return hT_hi[:, k, m * P:(m + 1) * P], hT_lo[:, k, m * P:(m + 1) * P]

        ss_ready, root_ready, gain_landed = sem("ss_ready"), sem("root_ready"), sem("gain_landed")
        x_added, diag_ready = sem("x_added"), sem("diag_ready")
        turned, turned_out, turned_hi, turned_lo = sem("turned"), sem("turned_out"), sem("turned_hi"), sem("turned_lo")

        def as_banks(ap):
            return ap.rearrange("p (c n) -> p c n", c=2)

        acc = psA[:].rearrange("p (m c) n -> p m c n", m=M)

        def root_parts(sums, src, n, eps, ready=None):
            s0, r0 = ss_ready.n, root_ready.n
            ss_ready.n += M
            root_ready.n += M

            def act_part(act):
                for m in range(M):
                    if ready is not None:
                        act.wait_ge(x_added.h, ready + m + 1)
                    sink = actout[:] if len(src(m).shape) == 2 else as_banks(actout[:])
                    nc.scalar.activation(sink, src(m), ACT.Square, accum_out=sums[:, 0, m:m + 1]) \
                        .then_inc(ss_ready.h, 1)
                    act.wait_ge(ss_ready.h, s0 + m + 1)
                    nc.scalar.activation(sums[:, 1, m:m + 1], sums[:, 0, m:m + 1], ACT.Sqrt, scale=1.0 / n,
                                         bias=eps_of[eps]).then_inc(root_ready.h, 1)

            def reciprocal(dve, step, m):
                dve.wait_ge(root_ready.h, r0 + m + 1)
                step(nc.vector.reciprocal(sums[:, 2, m:m + 1], sums[:, 1, m:m + 1]))
                return sums[:, 2, m:m + 1]
            return act_part, reciprocal

        class Pre:

            def __init__(self, ctx):
                self.ctx, self.sps, self.acts, self.dves, self.pes = ctx, [], [], [], []
                self.x_from, self.lo_from = None, None

            def sp(self, sp):
                for part in self.sps:
                    part(sp)

            def pe(self, pe):
                for part in self.pes:
                    part(pe)

            def act(self, act, split):
                if len(self.acts) > 1:
                    self.acts[0](act)
                split()
                for part in self.acts[1 if len(self.acts) > 1 else 0:]:
                    part(act)

            def dve(self, dve, split):
                for part in self.dves[:-1]:
                    part(dve)
                if self.lo_from is None:
                    self.dves[-1](dve)
                    split()
                else:
                    self.dves[-1](dve, split)

            def wait_turned(self, pe, k):
                if k % 2 == 0:
                    pe.wait_ge(turned_lo.h, self.lo_from + k // 2 + 1)

            def alone(self):
                with nc.Block() as block:
                    block.sync(self.sp)
                    block.tensor(self.pe)
                    block.scalar(lambda act: self.act(act, lambda: None))
                    block.vector(lambda dve: self.dve(dve, lambda: None))

            def add_gated(self, gate):
                t = sb(self.ctx, "gated", [P, M, D])
                self.x_from = x_added.n
                x_added.n += M

                def dve_part(dve):
                    step = Chain(dve, dve_step)
                    for m in range(M):
                        step(nc.vector.tensor_tensor(as_banks(t[:, m]), acc[:, m], as_banks(gates[:, gate]),
                                                     ALU.mult))
                        nc.vector.tensor_tensor(x[:, m], x[:, m], t[:, m], ALU.add).then_inc(x_added.h, 1)
                self.dves.append(dve_part)

            def add_normed(self, row):
                t = sb(self.ctx, "normed", [P, M, D])
                gain = sb(self.ctx, "gain", [P, D])
                sums = sb(self.ctx, "out_sums", [P, 3, M])
                g0 = gain_landed.n
                gain_landed.n += 16
                self.x_from = x_added.n
                x_added.n += M
                act_part, reciprocal = root_parts(sums, lambda m: acc[:, m], D, RMS_EPS)

                def sp_part(sp):
                    sp.dma_start(gain[:], a["norm_gains_2"][row[0], row[1]:row[1] + 1].broadcast_to([P, D])) \
                        .then_inc(gain_landed.h, 16)

                def dve_part(dve):
                    step = Chain(dve, dve_step)
                    dve.wait_ge(gain_landed.h, g0 + 16)
                    for m in range(M):
                        r = reciprocal(dve, step, m)
                        step(nc.vector.scalar_tensor_tensor(as_banks(t[:, m]), acc[:, m], r, as_banks(gain[:]),
                                                            ALU.mult, ALU.mult))
                        nc.vector.tensor_tensor(x[:, m], x[:, m], t[:, m], ALU.add).then_inc(x_added.h, 1)
                self.sps.append(sp_part)
                self.acts.append(act_part)
                self.dves.append(dve_part)

            def turn(self, src, kt, hi, lo, scale=None, shift=None, moving=None):
                tmp = sb(self.ctx, "turned_full", [P, 2, 2, S])
                R = kt // 2
                b0 = turned.n
                for s in (turned, turned_out, turned_hi, turned_lo):
                    s.n += R
                self.lo_from = b0

                def pe_part(pe):
                    for r in range(R):
                        if r >= 2:
                            pe.wait_ge(turned_out.h, b0 + r - 1)
                        for k in range(2):
                            for m in range(M):
                                dst = psT[:, r % 2, k * S + m * P:k * S + (m + 1) * P]
                                if moving:
                                    last = nc.tensor.matmul(dst, src(m, 2 * r + k), moving(m), start=True, stop=True)
                                else:
                                    last = nc.tensor.transpose(dst, src(m, 2 * r + k), ident[:])
                        last.then_inc(turned.h, 1)

                def act_part(act):
                    for r in range(R):
                        act.wait_ge(turned_out.h, b0 + r + 1)
                        nc.scalar.activation(hi[:, 2 * r:2 * r + 2], tmp[:, r % 2], ACT.Copy).then_inc(turned_hi.h, 1)

                def dve_part(dve, split):
                    def out(r):
                        dve.wait_ge(turned.h, b0 + r + 1)
                        if r >= 2:
                            dve.wait_ge(turned_lo.h, b0 + r - 1)
                        if scale is None:
                            ins = nc.vector.tensor_copy(tmp[:, r % 2].rearrange("p k s -> p (k s)"), psT[:, r % 2])
                        for k in range(0 if scale is None else 2):
                            f, part, dst = 2 * r + k, psT[:, r % 2, k * S:(k + 1) * S], tmp[:, r % 2, k]
                            if shift is None:
                                ins = nc.vector.tensor_scalar(dst, part, scale(f), None, ALU.mult)
                            else:
                                ins = nc.vector.tensor_scalar(dst, part, scale(f), shift(f), ALU.mult, ALU.add)
                        ins.then_inc(turned_out.h, 1)

                    def low(r):
                        dve.wait_ge(turned_hi.h, b0 + r + 1)
                        nc.vector.tensor_tensor(lo[:, 2 * r:2 * r + 2], tmp[:, r % 2],
                                                hi[:, 2 * r:2 * r + 2].bitcast(F32),
                                                ALU.subtract).then_inc(turned_lo.h, 1)
                    for r in range(R + 1):
                        if r < R:
                            out(r)
                        if r >= 1:
                            low(r - 1)
                        if r == 2:
                            split()
                self.pes.append(pe_part)
                self.acts.append(act_part)
                self.dves.append(dve_part)

            def norm(self, scale, shift=None, before_dve=None):
                sums = sb(self.ctx, "x_sums", [P, 3, M])
                diag = sb(self.ctx, "diag", [P, M, P])
                act_part, reciprocal = root_parts(sums, lambda m: x[:, m], D, RMS_EPS, self.x_from)
                d0 = diag_ready.n
                diag_ready.n += M

                def dve_part(dve):
                    step = Chain(dve, dve_step)
                    if before_dve:
                        before_dve(step)
                    for m in range(M):
                        r = reciprocal(dve, step, m)
                        nc.vector.tensor_scalar(diag[:, m], ident[:], r, None, ALU.mult).then_inc(diag_ready.h, 1)
                self.acts.append(act_part)
                self.dves.append(dve_part)
                self.pes.append(lambda pe: pe.wait_ge(diag_ready.h, d0 + M))
                self.turn(lambda m, k: x[:, m, k * P:(k + 1) * P], K8, hT_hi, hT_lo, scale, shift,
                          lambda m: diag[:, m])

            def modulate(self, norm_col, shift_col, scale_col):
                def before(step):
                    step(nc.vector.scalar_tensor_tensor(aff[:, 0], mods[:, scale_col:scale_col + K8], 1.0,
                                                        featB[:, norm_col:norm_col + K8], ALU.add, ALU.mult))
                self.norm(lambda k: aff[:, 0, k:k + 1], lambda k: mods[:, shift_col + k:shift_col + k + 1], before)

        h_ready, h_turned = sem("unit_h_ready"), sem("unit_h_turned")
        silu_ready, hu_hi_ready, hu_lo_ready = sem("unit_silu_ready"), sem("unit_hT_hi"), sem("unit_hT_lo")

        def gated_units(stream, weight=None, beside=None, pre=None):
            U = stream.n
            n = (U - 1) // 2 - 1
            assert U == 2 * n + 3
            q = {s: s.n for s in (h_ready, h_turned, silu_ready, hu_hi_ready, hu_lo_ready)}
            g0, d0 = stream.g, stream.d
            with ExitStack() as ctx:
                sg = sb(ctx, "silu_g", [P, M, EH])
                hh = sb(ctx, "unit_h", [P, M, EH])
                huh = sb(ctx, "unit_hT_h", [P, 2, S], F32R)
                hul = sb(ctx, "unit_hT_l", [P, 2, S], F32R)
                with nc.Block() as block:
                    if beside:
                        block.gpsimd(beside)

                    def turns(eng, body):
                        for j in range(3):
                            body(j, None)
                        with eng.Fori(1, n) as i:
                            body(1, i)
                            body(2, i)
                        body(U - 2, None)
                        body(U - 1, None)

                    @block.sync
                    def _(sp):
                        if pre:
                            pre.sp(sp)

                        def body(j, i):
                            if i is not None or j + 2 < U:
                                stream.load_gu(sp, j + 2, i)
                                stream.load_dn(sp, j + 2, i)
                        turns(sp, body)
                        nxt = following(stream)
                        if nxt:
                            nxt.first_loads(sp)

                    @block.tensor
                    def _(pe):
                        if pre:
                            pre.pe(pe)

                        def turn(j, i):
                            pe.wait_ge(h_ready.h, at(q[h_ready] + 2 * j + 2, i, 4))
                            for k in range(2):
                                for m in range(M):
                                    last = nc.tensor.transpose(psT[:, j % 2, k * S + m * P:k * S + (m + 1) * P],
                                                               hh[:, m, k * P:(k + 1) * P], ident[:])
                            last.then_inc(h_turned.h, 1)

                        def down(j, i):
                            pe.wait_ge(dn_lo_ready.h, at(d0 + j + 1, i, 2))
                            pe.wait_ge(hu_lo_ready.h, at(q[hu_lo_ready] + j + 1, i, 2))
                            for k in range(2):
                                for m in range(M):
                                    lhs = huh[:, k, m * P:(m + 1) * P], hul[:, k, m * P:(m + 1) * P]
                                    for c in range(2):
                                        first = j == 0 and i is None and k == 0
                                        final = j == U - 1 and k == 1
                                        cs_ = slice(c * NB, (c + 1) * NB)
                                        last = mm3(psA[:, 2 * m + c], lhs, (dn_hi[:, k, cs_], dn_lo[:, k, cs_]),
                                                   first, final)
                            last.then_inc(dn_used.h, 1)

                        def body(j, i):
                            if j > 0:
                                turn(j - 1, i)
                            for h in range(2):
                                pe.wait_ge(gu_lo_ready.h, at(2 * (g0 + j) + h + 1, i, 4))
                                for k in range(h * HALF, (h + 1) * HALF):
                                    if pre and j == 0:
                                        pre.wait_turned(pe, k)
                                    for m in range(M):
                                        last = mm3(psG[:, m], hT(m, k), (gu_hi[:, k], gu_lo[:, k]),
                                                   k == 0, k == K8 - 1)
                                last.then_inc(gu_used.h, 1)
                            if j > 0:
                                down(j - 1, i)
                        turns(pe, body)
                        turn(U - 1, None)
                        down(U - 1, None)

                    @block.scalar
                    def _(act):
                        start_act(act, stream, pre)

                        def body(j, i):
                            if j < U - 1:
                                stream.hi(act, j + 1, 0, i)
                            elif following(stream):
                                following(stream).hi(act, 0, 0)
                            act.wait_ge(gu_used.h, at(2 * (g0 + j) + 2, i, 4))
                            if j > 0:
                                act.wait_ge(h_ready.h, at(q[h_ready] + 2 * j, i, 4))
                            for m in range(M):
                                nc.scalar.activation(sg[:, m], psG[:, m, 0:EH], ACT.Silu).then_inc(silu_ready.h, 1)
                            if j < U - 1:
                                stream.hi(act, j + 1, 1, i)
                            act.wait_ge(h_turned.h, at(q[h_turned] + j + 1, i, 2))
                            if d0 + j > 0:
                                act.wait_ge(dn_used.h, at(d0 + j, i, 2))
                            nc.scalar.activation(huh[:].rearrange("p k s -> p (k s)"), psT[:, j % 2], ACT.Copy) \
                                .then_inc(hu_hi_ready.h, 1)
                            stream.dhi(act, j, i)
                        turns(act, body)

                    @block.vector
                    def _(dve):
                        start_dve(dve, stream, pre)

                        def body(j, i):
                            if j < U - 1:
                                stream.lo(dve, j + 1, 0, i)
                            elif following(stream):
                                following(stream).lo(dve, 0, 0)
                            if j > 0:
                                dve.wait_ge(h_turned.h, at(q[h_turned] + j, i, 2))
                            for m in range(M):
                                dve.wait_ge(silu_ready.h, at(q[silu_ready] + 2 * j + m + 1, i, 4))
                                w = 1.0
                                if weight is not None:
                                    w = weight[:, m, j:j + 1] if i is None else weight[:, m, bass.ds(j + i * 2, 1)]
                                nc.vector.scalar_tensor_tensor(hh[:, m], sg[:, m], w, psG[:, m, EH:2 * EH],
                                                               ALU.mult, ALU.mult).then_inc(h_ready.h, 1)
                            if j < U - 1:
                                stream.lo(dve, j + 1, 1, i)
                            dve.wait_ge(hu_hi_ready.h, at(q[hu_hi_ready] + j + 1, i, 2))
                            nc.vector.tensor_tensor(hul[:].rearrange("p k s -> p (k s)"), psT[:, j % 2],
                                                    huh[:].rearrange("p k s -> p (k s)").bitcast(F32),
                                                    ALU.subtract).then_inc(hu_lo_ready.h, 1)
                            stream.dlo(dve, j, i)
                        turns(dve, body)
            h_ready.n += 2 * U
            silu_ready.n += 2 * U
            for s in (h_turned, hu_hi_ready, hu_lo_ready):
                s.n += U

        x_landed, vec_landed = sem("x_landed"), sem("vec_landed")
        const_ready, vec_turned, vec_ready = sem("const_ready"), sem("vec_turned"), sem("vec_ready")

        def rows(ap):
            return ap.rearrange("(r p) -> r p", p=P)

        B_MIX, B_FFN, B_KV, B_BS, B_SUB = 0, 16, 32, 40, 48
        with ExitStack() as ctx:
            stage = sb(ctx, "vec_rows", [P, 3, P])
            with nc.Block() as block:
                @block.sync
                def _(sp):
                    sp.dma_start(x[:], a["x"][0].rearrange("(m p) d -> p m d", p=P)).then_inc(x_landed.h, 16)
                    vecs = [(0, 0, a["ada_b"].rearrange("l (r p) -> (l r) p", p=P)), (0, COL_KVB, rows(a["kv_ada_b"])),
                            (0, COL_C, rows(a["c"][0])),
                            (1, B_MIX, a["norm_mix"].rearrange("l (r p) -> (l r) p", p=P)),
                            (1, B_FFN, a["norm_ffn"].rearrange("l (r p) -> (l r) p", p=P)),
                            (1, B_KV, rows(a["kv_norm"])), (1, B_BS, a["a_b_s"][0]), (1, B_SUB, a["a_subln_2"]),
                            (2, 0, a["norm_gains_2"].rearrange("l g (r p) -> (l g r) p", p=P))]
                    sp.wait_ge(const_ready.h, 1)
                    for t, r, src in vecs:
                        sp.dma_start(stage[r:r + src.shape[0], t], src).then_inc(vec_landed.h, 16)
                    vec_landed.n = 16 * len(vecs)
                    sp.wait_ge(x_landed.h, 16)

                @block.gpsimd
                def _(pool):
                    step = Chain(pool, pool_step)
                    nc.gpsimd.memset(stage[:], 0.0).then_inc(const_ready.h, 1)
                    nc.gpsimd.memset(gateval[:], 1.0)
                    nc.gpsimd.memset(consts[:, 0:1], RMS_EPS)
                    nc.gpsimd.memset(consts[:, 1:2], LN_EPS)
                    step(nc.gpsimd.memset(ones[:], 1.0))
                    step(nc.gpsimd.memset(ident[:], 0.0))
                    nc.gpsimd.affine_select(out=ident[:], in_=ident[:], compare_op=ALU.not_equal, fill=1.0, base=0,
                                            pattern=[[-1, P]], channel_multiplier=1).then_inc(const_ready.h, 1)

                @block.tensor
                def _(pe):
                    pe.wait_ge(const_ready.h, 2)
                    pe.wait_ge(vec_landed.h, vec_landed.n)
                    for t in range(3):
                        last = nc.tensor.transpose(psT[:, 0, t * P:(t + 1) * P], stage[:, t], ident[:])
                    last.then_inc(vec_turned.h, 1)

                @block.vector
                def _(dve):
                    step = Chain(dve, dve_step)
                    dve.wait_ge(vec_turned.h, 1)
                    for t, dst in enumerate((featA, featB, featC)):
                        step(nc.vector.tensor_copy(dst[:], psT[:, 0, t * P:(t + 1) * P]))
                    nc.vector.tensor_copy(featA[:], featA[:]).then_inc(vec_ready.h, 1)

                @block.scalar
                def _(act):
                    act.wait_ge(vec_ready.h, 1)
                    nc.scalar.activation(cs[:], featA[:, COL_C:COL_C + K8], ACT.Silu)

        ada_landed = [sem(f"ada_landed_{s}") for s in range(4)]
        side_landed = [sem("side_landed_0"), sem("side_landed_1")]
        ada_used, ada_mm, gate_out = sem("ada_used"), sem("ada_mm"), sem("gate_out")
        gate_landed = sem("gate_landed")
        AC = 256

        def ada_view(w):
            return w.rearrange("(k p) n -> p k n", p=P)

        def ada_now(w, n, row):
            wv = ada_view(w)
            R = len(ada_landed)
            assert n % R == 0
            with ExitStack() as ctx:
                ring = sb(ctx, "ada_ring", [P, R, K8, AC])
                with nc.Block() as block:
                    @block.sync
                    def _(sp):
                        for s in range(R):
                            sp.dma_start(ring[:, s], wv[:, :, s * AC:(s + 1) * AC]).then_inc(ada_landed[s].h, 16)
                        with sp.Fori(0, n // R - 1) as i:
                            for s in range(R):
                                sp.wait_ge(ada_used.h, at(s + 1, i, R))
                                sp.dma_start(ring[:, s], wv[:, :, bass.ds(i * (R * AC) + (R + s) * AC, AC)]) \
                                    .then_inc(ada_landed[s].h, 16)
                        s_in.first_loads(sp)

                    @block.vector
                    def _(dve):
                        step0 = dve_step.n
                        with dve.Fori(0, n // R) as i:
                            step = Chain(dve, dve_step)
                            step.i, step.step = i, R * (K8 - 1)
                            for s in range(R):
                                dve.wait_ge(ada_landed[s].h, at(16, i, 16))
                                dst = row[:, bass.ds(i * (R * AC) + s * AC, AC)]
                                for k in range(K8):
                                    if k == 0:
                                        ins = nc.vector.tensor_scalar(dst, ring[:, s, k], cs[:, k:k + 1], None, ALU.mult)
                                    else:
                                        ins = nc.vector.scalar_tensor_tensor(dst, ring[:, s, k], cs[:, k:k + 1], dst,
                                                                             ALU.mult, ALU.add)
                                    if k < K8 - 1:
                                        step(ins)
                                    else:
                                        ins.then_inc(ada_used.h, 1)
                        dve_step.n = step0 + (K8 - 1) * n

        def ada_beside(pool, w, first, n, row, ring):
            wv = ada_view(w)
            step0 = pool_step.n
            l0 = [s.n for s in side_landed]

            def load(s, col):
                pool.dma_start(ring(s), wv[:, :, col]).then_inc(side_landed[s].h, 16)
            for s in range(2):
                load(s, slice((first + s) * AC, (first + s + 1) * AC))

            def piece(s, i, more):
                step = Chain(pool, pool_step)
                if i is not None:
                    step.i, step.step = i, 8
                r = ring(s)
                pool.wait_ge(side_landed[s].h, at(l0[s] + 16, i, 16))
                step(nc.gpsimd.tensor_tensor(r, r, cs[:].unsqueeze(2).broadcast_to([P, K8, AC]), ALU.mult))
                step(nc.gpsimd.tensor_tensor(r[:, 0:4], r[:, 0:4], r[:, 4:8], ALU.add))
                step(nc.gpsimd.tensor_tensor(r[:, 0:2], r[:, 0:2], r[:, 2:4], ALU.add))
                base = 0 if i is None else i * (2 * AC)
                step(nc.gpsimd.tensor_tensor(row[:, bass.ds(base + s * AC, AC)], r[:, 0], r[:, 1], ALU.add))
                if more:
                    load(s, bass.ds(base + (first + 2 + s) * AC, AC))
            with pool.Fori(0, n // 2 - 1) as i:
                for s in range(2):
                    piece(s, i, True)
            pool_step.n = step0 + 4 * (n - 2)
            for s in range(2):
                l0[s] += 16 * (n // 2 - 1)
            last = row[:, (n - 2) * AC:n * AC]
            for s in range(2):
                step = Chain(pool, pool_step)
                r = ring(s)
                pool.wait_ge(side_landed[s].h, l0[s] + 16)
                step(nc.gpsimd.tensor_tensor(r, r, cs[:].unsqueeze(2).broadcast_to([P, K8, AC]), ALU.mult))
                step(nc.gpsimd.tensor_tensor(r[:, 0:4], r[:, 0:4], r[:, 4:8], ALU.add))
                step(nc.gpsimd.tensor_tensor(r[:, 0:2], r[:, 0:2], r[:, 2:4], ALU.add))
                step(nc.gpsimd.tensor_tensor(last[:, s * AC:(s + 1) * AC], r[:, 0], r[:, 1], ALU.add))
            for s in range(2):
                side_landed[s].n += 16 * (n // 2)

        def ada_finish(row, bias_col, mods_col, gates_at=None, layer=0):
            nt = row.shape[1] // P
            with nc.Block() as block:
                @block.sync
                def _(sp):
                    if gates_at:
                        for k in gates_at:
                            sp.dma_start(gates[:, k], a["ada_b"][layer:layer + 1, (2 + 3 * k) * D:(3 + 3 * k) * D]
                                         .broadcast_to([P, D])).then_inc(gate_landed.h, 16)

                @block.tensor
                def _(pe):
                    for t in range(nt):
                        last = nc.tensor.matmul(psT[:, 0, t:t + 1], row[:, t * P:(t + 1) * P], ones[:, 0:1],
                                                start=True, stop=True)
                    last.then_inc(ada_mm.h, 1)
                    if gates_at:
                        for j, k in enumerate(gates_at):
                            if j:
                                pe.wait_ge(gate_out.h, gate_out.n + j)
                            for c in range(2):
                                o = gates_at[k] + c * NB
                                last = nc.tensor.matmul(psG[:, c], ones[:], row[:, o:o + NB], start=True, stop=True)
                            last.then_inc(ada_mm.h, 1)

                @block.vector
                def _(dve):
                    dve.wait_ge(ada_mm.h, ada_mm.n + 1)
                    nc.vector.tensor_tensor(mods[:, mods_col:mods_col + nt], psT[:, 0, 0:nt],
                                            featA[:, bias_col:bias_col + nt], ALU.add)
                    if gates_at:
                        dve.wait_ge(gate_landed.h, gate_landed.n + 16 * len(gates_at))
                        for j, k in enumerate(gates_at):
                            dve.wait_ge(ada_mm.h, ada_mm.n + 2 + j)
                            nc.vector.tensor_tensor(as_banks(gates[:, k]), psG[:], as_banks(gates[:, k]),
                                                    ALU.add).then_inc(gate_out.h, 1)
            ada_mm.n += 1
            if gates_at:
                gate_landed.n += 16 * len(gates_at)
                gate_out.n += len(gates_at)
                ada_mm.n += len(gates_at)

        def finish():
            stored = sem("stored")
            with nc.Block() as block:
                @block.sync
                def _(sp):
                    sp.dma_start(out[0].rearrange("(m p) d -> p m d", p=P), x[:]).then_inc(stored.h, 16)
                    sp.wait_ge(stored.h, 16)

        with ExitStack() as ctx:
            row = sb(ctx, "ada_row", [P, 2 * D])
            ada_now(a["ada_w"][0], 2 * D // AC, row)
            ada_finish(row, 0, 0)
        bias_landed, ws_masked = sem("bias_landed"), sem("ws_masked")
        zg, v_ready, ws_turned, ws_ready = sem("gelu_done"), sem("v_ready"), sem("ws_turned"), sem("ws_ready")
        sv_ready, y_ready, mu_ready = sem("sv_ready"), sem("y_ready"), sem("mu_ready")
        with ExitStack() as ctx:
            z = sb(ctx, "z", [P, M, 2 * AW])
            with ExitStack() as ctx2:
                brow = sb(ctx2, "b_in", [P, 2 * AW])
                row = sb(ctx2, "ada_row", [P, 2 * D])
                with nc.Block() as block:
                    @block.sync
                    def _(sp):
                        sp.dma_start(brow[:], a["a_b_in"].broadcast_to([P, 2 * AW])).then_inc(bias_landed.h, 16)
                        sp.wait_ge(bias_landed.h, 16)

                def evac_z(c, i, bank):
                    for m in range(M):
                        o = at(c, i, 2) * NB
                        yield nc.vector.tensor_tensor(z[:, m, bass.ds(o, NB)], psA[:, bank + m],
                                                      brow[:, bass.ds(o, NB)], ALU.add)
                pre = Pre(ctx2)
                pre.modulate(B_MIX, 0, 8)
                project(s_in, hT, evac_dve=evac_z, pre=pre, beside=lambda pool: ada_beside(
                    pool, a["ada_w"][0], 3 * D // AC, 2 * D // AC, row,
                    lambda s: dn_raw[:, s].rearrange("p a (b n) -> p (a b) n", n=AC)))
                ada_finish(row, 24, 24)
            with ExitStack() as ctx2:
                lng = sb(ctx2, "ln_g", [P, AW])
                lnb = sb(ctx2, "ln_b", [P, AW])
                ws = sb(ctx2, "w_s", [P, NG, P])
                wsT = sb(ctx2, "w_sT", [P, NG, P])
                st = sb(ctx2, "ln_stats", [P, 4, M])
                sink = sb(ctx2, "ln_sink", [P, AW])
                with nc.Block() as block:
                    @block.sync
                    def _(sp):
                        sp.dma_start(ws[:], a["a_w_s"][0].rearrange("g t s -> t g s")).then_inc(bias_landed.h, 16)
                        sp.wait_ge(bias_landed.h, 32)
                        sp.dma_start(lng[:], a["a_ln_g"].broadcast_to([P, AW])).then_inc(bias_landed.h, 16)
                        sp.dma_start(lnb[:], a["a_ln_b"].broadcast_to([P, AW])).then_inc(bias_landed.h, 16)

                    @block.gpsimd
                    def _(pool):
                        pool.wait_ge(bias_landed.h, 32)
                        nc.gpsimd.affine_select(out=ws[:], in_=ws[:], compare_op=ALU.is_ge, fill=0.0, base=0,
                                                pattern=[[0, NG], [-1, P]], channel_multiplier=1) \
                            .then_inc(ws_masked.h, 1)
                        pool.wait_ge(mu_ready.h, 2)
                        nc.gpsimd.tensor_scalar(st[:, 1], st[:, 0], -1.0 / AW, None, ALU.mult) \
                            .then_inc(mu_ready.h, 1)

                    @block.scalar
                    def _(act):
                        for m in range(M):
                            nc.scalar.activation(z[:, m, AW:], z[:, m, AW:], ACT.Gelu_apprx_tanh).then_inc(zg.h, 1)
                        for m in range(M):
                            act.wait_ge(zg.h, m + 1)
                            nc.scalar.activation(sink[:], z[:, m, AW:], ACT.Copy,
                                                 accum_out=st[:, 0, m:m + 1]).then_inc(mu_ready.h, 1)
                            act.wait_ge(mu_ready.h, m + 1)
                        act.wait_ge(mu_ready.h, 3)
                        for m in range(M):
                            nc.scalar.activation(sink[:], z[:, m, AW:], ACT.Square, bias=st[:, 1, m:m + 1],
                                                 accum_out=st[:, 2, m:m + 1]).then_inc(mu_ready.h, 1)
                            act.wait_ge(mu_ready.h, m + 4)
                        nc.scalar.activation(st[:, 3], st[:, 2], ACT.Sqrt, scale=1.0 / AW, bias=eps_of[LN_EPS]) \
                            .then_inc(mu_ready.h, 1)
                        for m in range(M):
                            nc.scalar.activation(z[:, m, 0:AW], z[:, m, 0:AW], ACT.Gelu_apprx_tanh).then_inc(zg.h, 1)

                    @block.tensor
                    def _(pe):
                        pe.wait_ge(ws_masked.h, 1)
                        for g in range(NG):
                            last = nc.tensor.transpose(psT[:, g // 4, (g % 4) * P:(g % 4 + 1) * P], ws[:, g], ident[:])
                        last.then_inc(ws_turned.h, 1)
                        pe.wait_ge(ws_ready.h, 1)
                        W = AW // NG
                        for m in range(M):
                            pe.wait_ge(v_ready.h, m + 1)
                            for g in range(NG):
                                r = m * NG + g
                                if r >= 8 and r % 2 == 0:
                                    pe.wait_ge(y_ready.h, r - 6)
                                last = nc.tensor.matmul(psA[:, (r // 2) % 4, (r % 2) * W:(r % 2 + 1) * W], wsT[:, g],
                                                        z[:, m, AW + g * W:AW + (g + 1) * W], start=True, stop=True)
                                if r % 2:
                                    last.then_inc(sv_ready.h, 1)

                    @block.vector
                    def _(dve):
                        step = Chain(dve, dve_step)
                        dve.wait_ge(ws_turned.h, 1)
                        nc.vector.tensor_copy(wsT[:].rearrange("p (b g) t -> p b (g t)", b=2), psT[:]) \
                            .then_inc(ws_ready.h, 1)
                        dve.wait_ge(bias_landed.h, 64)
                        dve.wait_ge(mu_ready.h, 6)
                        step(nc.vector.reciprocal(st[:, 2], st[:, 3]))
                        for m in range(M):
                            v = z[:, m, AW:]
                            step(nc.vector.tensor_scalar(v, v, st[:, 1, m:m + 1], st[:, 2, m:m + 1], ALU.add, ALU.mult))
                            step(nc.vector.tensor_tensor(v, v, lng[:], ALU.mult))
                            nc.vector.tensor_tensor(v, v, lnb[:], ALU.add).then_inc(v_ready.h, 1)
                        W = AW // NG
                        dve.wait_ge(zg.h, 4)
                        for m in range(M):
                            for g in range(NG):
                                r = m * NG + g
                                dve.wait_ge(sv_ready.h, r // 2 + 1)
                                u = z[:, m, g * W:(g + 1) * W]
                                nc.vector.scalar_tensor_tensor(u, psA[:, (r // 2) % 4, (r % 2) * W:(r % 2 + 1) * W],
                                                               featB[:, B_BS + g:B_BS + g + 1], u, ALU.add, ALU.mult) \
                                    .then_inc(y_ready.h, 1)
            yT_hi = sb(ctx, "yT_hi", [P, AW // P, S], F32R)
            yT_lo = sb(ctx, "yT_lo", [P, AW // P, S], F32R)
            ring = z[:, :, AW:AW + K8 * AC].rearrange("p s (k n) -> p s k n", n=AC)
            g1_row = sb(ctx, "g1_row", [P, D])
            pre = Pre(ctx)
            pre.turn(lambda m, k: z[:, m, k * P:(k + 1) * P], AW // P, yT_hi, yT_lo)
            project(s_out, lambda m, k: (yT_hi[:, k, m * P:(m + 1) * P], yT_lo[:, k, m * P:(m + 1) * P]),
                    deep=AW // D, keep=True, pre=pre, beside=lambda pool: ada_beside(
                        pool, a["ada_w"][0], 2 * D // AC, D // AC, g1_row,
                        lambda s: ring[:, s]))
            ada_finish(g1_row, 16, 16, {0: 0}, 0)

        def add_alone(add):
            with ExitStack() as ctx:
                pre = Pre(ctx)
                add(pre)
                pre.alone()

        if stop == "gmlp":
            add_alone(lambda pre: pre.add_gated(0))
        if stop == "gmlp":
            return finish()

        router_landed, router_mm, router_sig = sem("router_landed"), sem("router_mm"), sem("router_sig")
        G8 = 8
        GE = E // G8

        def moe(layer):
            with ExitStack() as ctx:
                pre = Pre(ctx)
                pre.add_gated(0)
                pre.modulate(B_FFN + 8 * layer, 48 * layer + 24, 48 * layer + 32)
                pre.alone()
            with ExitStack() as ctx:
                wr = sb(ctx, "w_router", [P, K8, E])
                hf = sb(ctx, "hT_full", [P, K8, S])
                eb = sb(ctx, "e_bias", [P, E])
                sc = sb(ctx, "scores", [P, M, E])
                ch = sb(ctx, "choice", [P, M, E])
                ch2 = sb(ctx, "choice_cut", [P, M, E])
                t8 = sb(ctx, "group_top", [P, M, G8, 8])
                gs = sb(ctx, "group_score", [P, M, G8])
                c1 = sb(ctx, "better", [P, M, G8, G8])
                c2 = sb(ctx, "equal_before", [P, M, G8, G8])
                tri = sb(ctx, "before", [P, G8, G8])
                rk = sb(ctx, "group_rank", [P, M, G8])
                em = sb(ctx, "group_mask", [P, M, G8])
                sm = sb(ctx, "weight_sum", [P, M])
                with nc.Block() as block:
                    @block.sync
                    def _(sp):
                        sp.dma_start(wr[:], a["moe_router"][layer].rearrange("(k p) e -> p k e", p=P)) \
                            .then_inc(router_landed.h, 16)
                        sp.dma_start(eb[:], a["moe_bias"][layer:layer + 1].broadcast_to([P, E])) \
                            .then_inc(router_landed.h, 16)

                    @block.gpsimd
                    def _(pool):
                        step = Chain(pool, pool_step)
                        step(nc.gpsimd.memset(tri[:], 1.0))
                        step(nc.gpsimd.affine_select(out=tri[:], in_=tri[:], compare_op=ALU.is_gt, fill=0.0, base=0,
                                                     pattern=[[1, G8], [-1, G8]], channel_multiplier=0))

                    @block.tensor
                    def _(pe):
                        pe.wait_ge(router_landed.h, router_landed.n + 32)
                        pe.wait_ge(router_sig.h, router_sig.n + 1)
                        for m in range(M):
                            for k in range(K8):
                                last = nc.tensor.matmul(psT[:, m, 0:E], hf[:, k, m * P:(m + 1) * P], wr[:, k],
                                                        start=k == 0, stop=k == K8 - 1)
                        last.then_inc(router_mm.h, 1)

                    @block.scalar
                    def _(act):
                        act.wait_ge(router_mm.h, router_mm.n + 1)
                        nc.scalar.activation(sc[:], psT[:, :, 0:E], ACT.Sigmoid).then_inc(router_sig.h, 1)

                    pool_steps = pool_step.n

                    @block.vector
                    def _(dve):
                        step = Chain(dve, dve_step)
                        nc.vector.tensor_tensor(hf[:], hT_hi[:].bitcast(F32), hT_lo[:].bitcast(F32), ALU.add) \
                            .then_inc(router_sig.h, 1)
                        dve.wait_ge(router_sig.h, router_sig.n + 2)
                        dve.wait_ge(pool_step.h, pool_steps)
                        for m in range(M):
                            step(nc.vector.tensor_tensor(ch[:, m], sc[:, m], eb[:], ALU.add))
                        for m in range(M):
                            for g in range(G8):
                                step(nc.vector.max(t8[:, m, g], ch[:, m, g * GE:(g + 1) * GE]))
                        step(nc.vector.tensor_tensor(gs[:], t8[:, :, :, 0], t8[:, :, :, 1], ALU.add))
                        for m in range(M):
                            other = gs[:, m].unsqueeze(1).broadcast_to([P, G8, G8])
                            own = gs[:, m].unsqueeze(2).broadcast_to([P, G8, G8])
                            step(nc.vector.tensor_tensor(c1[:, m], other, own, ALU.is_gt))
                            step(nc.vector.tensor_tensor(c2[:, m], other, own, ALU.is_equal))
                            step(nc.vector.tensor_tensor(c2[:, m], c2[:, m], tri[:], ALU.mult))
                            step(nc.vector.tensor_tensor(c1[:, m], c1[:, m], c2[:, m], ALU.add))
                        step(nc.vector.reduce_sum(rk[:], c1[:], AX))
                        step(nc.vector.tensor_scalar(em[:], rk[:], 4.0, None, ALU.is_lt))
                        for m in range(M):
                            v = ch[:, m].rearrange("p (g e) -> p g e", g=G8)
                            mask = em[:, m].unsqueeze(2).broadcast_to([P, G8, GE])
                            step(nc.vector.tensor_tensor(v, v, mask, ALU.mult))
                            step(nc.vector.tensor_scalar(rk[:, m], em[:, m], -1.0, -NEG, ALU.add, ALU.mult))
                            low = rk[:, m].unsqueeze(2).broadcast_to([P, G8, GE])
                            step(nc.vector.tensor_tensor(v, v, low, ALU.add))
                            step(nc.vector.max(t8[:, m, 0], ch[:, m]))
                            step(nc.vector.match_replace(ch2[:, m], t8[:, m, 0], ch[:, m], 4 * NEG))
                            step(nc.vector.tensor_tensor(ch2[:, m], ch2[:, m], ch[:, m], ALU.not_equal))
                            step(nc.vector.tensor_tensor(ch2[:, m], ch2[:, m], sc[:, m], ALU.mult))
                        step(nc.vector.reduce_sum(sm[:], ch2[:], AX))
                        step(nc.vector.reciprocal(sm[:], sm[:]))
                        for m in range(M):
                            step(nc.vector.tensor_scalar(gateval[:, m, 1:E + 1], ch2[:, m], sm[:, m:m + 1],
                                                         ROUTED_SCALE, ALU.mult, ALU.mult))
                router_landed.n += 32
                router_mm.n += 1
                router_sig.n += 2
            if layer == 0:
                with ExitStack() as ctx:
                    rows_ = [sb(ctx, "ada_row", [P, 6 * D]), sb(ctx, "ada_row", [P, 2 * D])]
                    row_g2 = sb(ctx, "ada_row", [P, D])
                    ring = sb(ctx, "ada_ring", [P, 2, K8, AC])

                    def beside(pool):
                        ada_beside(pool, a["ada_w"][0], 5 * D // AC, D // AC, row_g2, lambda s: ring[:, s])
                        ada_beside(pool, a["ada_w"][1], 0, 6 * D // AC, rows_[0], lambda s: ring[:, s])
                        ada_beside(pool, a["kv_ada_w"], 0, 2 * D // AC, rows_[1], lambda s: ring[:, s])
                    gated_units(s_moe[layer], gateval, beside)
                    ada_finish(row_g2, 40, 40, {1: 0}, 0)
                    add_alone(lambda pre: pre.add_gated(1))
                    ada_finish(rows_[0], 48, 48, {0: 2 * D, 1: 5 * D}, 1)
                    ada_finish(rows_[1], COL_KVB, 96)
            else:
                gated_units(s_moe[layer], gateval)
                add_alone(lambda pre: pre.add_gated(1))

        moe(0)
        if stop == "moe0":
            return finish()

        masks_ready = sem("masks_ready")

        def make_masks(ctx, window):
            mk = sb(ctx, "mask", [P, 2 * P])

            def pool_part(pool):
                step = Chain(pool, pool_step)
                step(nc.gpsimd.memset(mk[:], 0.0))
                if window:
                    step(nc.gpsimd.affine_select(out=mk[:, 0:P], in_=mk[:, 0:P], compare_op=ALU.is_gt, fill=NEG,
                                                 base=0, pattern=[[1, P]], channel_multiplier=-1))
                nc.gpsimd.affine_select(out=mk[:, P:2 * P], in_=mk[:, P:2 * P], compare_op=ALU.is_ge, fill=NEG, base=0,
                                        pattern=[[-1, P]], channel_multiplier=1).then_inc(masks_ready.h, 1)
            return mk, pool_part

        qk_turned, qk_copied = sem("qk_turned"), sem("qk_copied")

        def heads_to_feature(pairs):
            n0 = qk_copied.n
            R = len(pairs) // 2

            def pe_part(pe):
                for r in range(R):
                    if r >= 2:
                        pe.wait_ge(qk_copied.h, n0 + r - 1)
                    for k in range(2):
                        for m in range(M):
                            last = nc.tensor.transpose(psT[:, r % 2, k * S + m * P:k * S + (m + 1) * P],
                                                       pairs[2 * r + k][1](m), ident[:])
                    last.then_inc(qk_turned.h, 1)

            def act_part(act):
                for r in range(R):
                    act.wait_ge(qk_turned.h, n0 + r + 1)
                    for k in range(2):
                        ins = nc.scalar.activation(pairs[2 * r + k][0], psT[:, r % 2, k * S:(k + 1) * S], ACT.Copy)
                    ins.then_inc(qk_copied.h, 1)
            qk_copied.n += R
            return pe_part, act_part

        scores_ready, s_taken, bias_ready, p_ready = (sem(n) for n in
                                                      ("scores_ready", "scores_taken", "bias_ready", "probs_ready"))
        w_ready, p_turned, p_copied, o_ready, o_taken = (sem(n) for n in
                                                         ("weights_ready", "probs_turned", "probs_copied",
                                                          "o_ready", "o_taken"))

        def softmax_attention(qT, kT, v, o, mask, window=False, lam=None, sink=None, vw=HD):
            items = [(t, m) for t in range(K8) for m in range(M)]
            q = {s: s.n for s in (scores_ready, s_taken, bias_ready, p_ready, w_ready, p_turned, p_copied,
                                  o_ready, o_taken)}
            nh = 1 if lam is not None else 2
            banks = (psG[:, 0:2], psA[:, 2:4])
            with ExitStack() as ctx:
                sm = sb(ctx, "scores_m", [P, 2, 2, 2 * P])
                pr = sb(ctx, "probs", [P, 2, 2, 2 * P])
                pT = sb(ctx, "probsT", [P, 2, 4, P])
                mx = sb(ctx, "row_max", [P, 2, 2])
                nm = sb(ctx, "neg_max", [P, 2, 2])
                su = sb(ctx, "row_sum", [P, 2, 2])
                rc = sb(ctx, "row_rec", [P, 2, 2])
                es = sb(ctx, "sink_term", [P, 2, 2])
                with nc.Block() as block:
                    @block.tensor
                    def _(pe):
                        def scores(n):
                            t, m = items[n]
                            b, L = n % 2, (m + 1) * P
                            if n >= 2:
                                pe.wait_ge(s_taken.h, q[s_taken] + n - 1)
                            for c in range(2):
                                r = slice(HD * c, HD * (c + 1))
                                last = nc.tensor.matmul(banks[b][:, c, 0:L], qT[r, t, m * P:(m + 1) * P],
                                                        kT(t)[r, 0:L], start=True, stop=True)
                            last.then_inc(scores_ready.h, 1)

                        def turn(n):
                            t, m = items[n]
                            b = n % 2
                            pe.wait_ge((w_ready if lam is not None else p_ready).h,
                                       q[w_ready] + n + 1 if lam is not None else q[p_ready] + 2 * n + 2)
                            for c in range(nh):
                                for j in range(m + 1):
                                    last = nc.tensor.transpose(psT[:, b, (2 * c + j) * P:(2 * c + j + 1) * P],
                                                               pr[:, b, c, j * P:(j + 1) * P], ident[:])
                            last.then_inc(p_turned.h, 1)

                        def values(n):
                            t, m = items[n]
                            b = n % 2
                            pe.wait_ge(p_copied.h, q[p_copied] + n + 1)
                            if n >= 2:
                                pe.wait_ge(o_taken.h, q[o_taken] + n - 1)
                            for c in range(nh):
                                for j in range(m + 1):
                                    last = nc.tensor.matmul(psA[:, b, c * vw:(c + 1) * vw], pT[:, b, 2 * c + j],
                                                            v(t, c, j), start=j == 0, stop=j == m)
                            last.then_inc(o_ready.h, 1)
                        N = len(items)
                        scores(0)
                        for n in range(N + 2):
                            if n + 1 < N:
                                scores(n + 1)
                            if n >= 2:
                                values(n - 2)
                            if 1 <= n <= N:
                                turn(n - 1)

                    @block.vector
                    def _(dve):
                        def mark(ins):
                            dve_step.n += 1
                            ins.then_inc(dve_step.h, 1)
                            return dve_step.n

                        def after(count):
                            dve.wait_ge(dve_step.h, count)

                        def masked(n):
                            t, m = items[n]
                            b, L = n % 2, (m + 1) * P
                            dve.wait_ge(scores_ready.h, q[scores_ready] + n + 1)
                            if n >= 2:
                                dve.wait_ge(p_ready.h, q[p_ready] + 2 * (n - 1))
                            mk = mask[:, 2 * P - L:].unsqueeze(1).broadcast_to([P, 2, L])
                            nc.vector.tensor_tensor(sm[:, b, :, 0:L], banks[b][:, :, 0:L], mk, ALU.add) \
                                .then_inc(s_taken.h, 1)

                        def maximum(n):
                            b, L = n % 2, (items[n][1] + 1) * P
                            dve.wait_ge(s_taken.h, q[s_taken] + n + 1)
                            return mark(nc.vector.reduce_max(mx[:, b], sm[:, b, :, 0:L], AX))

                        def bias(n, done):
                            t, b = items[n][0], n % 2
                            after(done)
                            if sink is None:
                                nc.vector.tensor_scalar(nm[:, b], mx[:, b], -ATT_SCALE, None, ALU.mult) \
                                    .then_inc(bias_ready.h, 1)
                                return
                            after(mark(nc.vector.scalar_tensor_tensor(mx[:, b], mx[:, b], ATT_SCALE,
                                                                      sink[:, 2 * t:2 * t + 2], ALU.mult, ALU.max)))
                            nc.vector.tensor_tensor(es[:, b], sink[:, 2 * t:2 * t + 2], mx[:, b], ALU.subtract)
                            nc.vector.tensor_scalar(nm[:, b], mx[:, b], -1.0, None, ALU.mult).then_inc(bias_ready.h, 1)

                        def total(n):
                            b = n % 2
                            dve.wait_ge(p_ready.h, q[p_ready] + 2 * n + 2)
                            if n >= 2:
                                dve.wait_ge(o_taken.h, q[o_taken] + n - 1)
                            if sink is not None:
                                after(mark(nc.vector.tensor_tensor(su[:, b], su[:, b], es[:, b], ALU.add)))
                            return mark(nc.vector.reciprocal(rc[:, b], su[:, b]))

                        def times_lambda(n, done):
                            b = n % 2
                            after(done)
                            return mark(nc.vector.tensor_tensor(rc[:, b, 1:2], rc[:, b, 1:2], lam, ALU.mult))

                        def first_weights(n):
                            b, L = n % 2, (items[n][1] + 1) * P
                            return mark(nc.vector.tensor_scalar(pr[:, b, 0, 0:L], pr[:, b, 0, 0:L], rc[:, b, 0:1], None,
                                                                ALU.mult))

                        def both_weights(n, done):
                            b, L = n % 2, (items[n][1] + 1) * P
                            after(done)
                            nc.vector.scalar_tensor_tensor(pr[:, b, 0, 0:L], pr[:, b, 1, 0:L], rc[:, b, 1:2],
                                                           pr[:, b, 0, 0:L], ALU.mult, ALU.add).then_inc(w_ready.h, 1)

                        reciprocal_done = {}

                        def back(n):
                            t, m = items[n]
                            b = n % 2
                            after(reciprocal_done[n])
                            dve.wait_ge(o_ready.h, q[o_ready] + n + 1)
                            w = nh * vw
                            dst = o[:, m, t * w:(t + 1) * w]
                            if lam is not None:
                                nc.vector.tensor_copy(dst, psA[:, b, 0:w]).then_inc(o_taken.h, 1)
                            else:
                                r = rc[:, b].unsqueeze(2).broadcast_to([P, 2, vw])
                                nc.vector.tensor_tensor(dst.rearrange("p (c e) -> p c e", c=2),
                                                        psA[:, b, 0:w].rearrange("p (c e) -> p c e", c=2), r,
                                                        ALU.mult).then_inc(o_taken.h, 1)
                        N = len(items)
                        for n in range(N + 2):
                            if n < N:
                                masked(n)
                            if 1 <= n <= N:
                                done = reciprocal_done[n - 1] = total(n - 1)
                            if n < N:
                                max_done = maximum(n)
                            if lam is not None and 1 <= n <= N:
                                done = times_lambda(n - 1, done)
                                weights_done = first_weights(n - 1)
                            if n < N:
                                bias(n, max_done)
                            if lam is not None and 1 <= n <= N:
                                after(done)
                                both_weights(n - 1, weights_done)
                            if n >= 2:
                                back(n - 2)

                    @block.scalar
                    def _(act):
                        def exps(n):
                            t, m = items[n]
                            b, L = n % 2, (m + 1) * P
                            act.wait_ge(bias_ready.h, q[bias_ready] + n + 1)
                            if n >= 2:
                                act.wait_ge(p_turned.h, q[p_turned] + n - 1)
                            for c in range(2):
                                nc.scalar.activation(pr[:, b, c, 0:L], sm[:, b, c, 0:L], ACT.Exp,
                                                     bias=nm[:, b, c:c + 1], scale=ATT_SCALE,
                                                     accum_out=su[:, b, c:c + 1]).then_inc(p_ready.h, 1)

                        def copy(n):
                            t, m = items[n]
                            b = n % 2
                            act.wait_ge(p_turned.h, q[p_turned] + n + 1)
                            if n >= 2:
                                act.wait_ge(o_ready.h, q[o_ready] + n - 1)
                            src = psT[:, b].rearrange("p (c j k) -> p c j k", c=2, j=2)[:, 0:nh, 0:m + 1]
                            dst = pT[:, b].rearrange("p (c j) k -> p c j k", c=2)[:, 0:nh, 0:m + 1]
                            nc.scalar.activation(dst, src, ACT.Copy).then_inc(p_copied.h, 1)
                        N = len(items)
                        for n in range(N + 1):
                            if n < N:
                                if sink is not None:
                                    act.wait_ge(bias_ready.h, q[bias_ready] + n + 1)
                                    nc.scalar.activation(es[:, n % 2], es[:, n % 2], ACT.Exp)
                                exps(n)
                            if n >= 1:
                                copy(n - 1)
            N = len(items)
            for s in (scores_ready, s_taken, bias_ready, p_turned, p_copied, o_ready, o_taken):
                s.n += N
            p_ready.n += 2 * N
            if lam is not None:
                w_ready.n += N

        def out_projection(stream, o, scale=None):
            with ExitStack() as ctx:
                pre = Pre(ctx)
                pre.turn(lambda m, k: o[:, m, k * P:(k + 1) * P], K8, hT_hi, hT_lo, scale)
                project(stream, hT, keep=True, pre=pre)

        with ExitStack() as ctx:
            qkv = sb(ctx, "qkv", [P, M, 3 * D])
            with ExitStack() as ctx2:
                pre = Pre(ctx2)
                pre.modulate(B_KV, 96, 104)
                project(s_k, hT, evac_act=to_sbuf(qkv[:, :, D:2 * D], D), pre=pre)
            project(s_v, hT, evac_act=to_sbuf(qkv[:, :, 2 * D:], D))
            with ExitStack() as ctx2:
                pre = Pre(ctx2)
                pre.modulate(B_MIX + 8, 48, 56)
                project(s_q, hT, evac_act=to_sbuf(qkv[:, :, 0:D], D), pre=pre)
            o = sb(ctx, "o", [P, M, D])
            qT = sb(ctx, "qT", [P, K8, S])
            kT = sb(ctx, "kT", [P, K8, S])
            mask, mask_pool = make_masks(ctx, False)
            pe_part, act_part = heads_to_feature(
                [(qT[:, t], lambda m, t=t: qkv[:, m, t * P:(t + 1) * P]) for t in range(K8)] +
                [(kT[:, t], lambda m, t=t: qkv[:, m, D + t * P:D + (t + 1) * P]) for t in range(K8)])
            with nc.Block() as block:
                block.tensor(pe_part)
                block.scalar(act_part)
                block.gpsimd(mask_pool)
            softmax_attention(qT, lambda t: kT[:, t],
                              lambda t, c, j: qkv[:, j, 2 * D + (2 * t + c) * HD:2 * D + (2 * t + c + 1) * HD], o, mask)
            out_projection(s_o, o)
        if stop == "moba":
            add_alone(lambda pre: pre.add_gated(0))
            return finish()
        moe(1)
        if stop == "moe1":
            return finish()
        final_landed = sem("final_gain_landed")

        def norm_x():
            with ExitStack() as ctx:
                gain = sb(ctx, "final_gain", [P, D])
                sums = sb(ctx, "final_sums", [P, 3, M])
                act_part, reciprocal = root_parts(sums, lambda m: x[:, m], D, RMS_EPS)
                with nc.Block() as block:
                    @block.sync
                    def _(sp):
                        sp.dma_start(gain[:], a["final_norm"].rearrange("(o d) -> o d", o=1).broadcast_to([P, D])) \
                            .then_inc(final_landed.h, 16)
                    block.scalar(act_part)

                    @block.vector
                    def _(dve):
                        step = Chain(dve, dve_step)
                        dve.wait_ge(final_landed.h, 16)
                        for m in range(M):
                            r = reciprocal(dve, step, m)
                            nc.vector.scalar_tensor_tensor(x[:, m], x[:, m], r, gain[:], ALU.mult, ALU.mult)
        norm_x()
        if stop == "first":
            return finish()

        trig = sb(top, "trig", [P, 2, M, 32])
        with ExitStack() as ctx:
            pos = sb(ctx, "pos", [P, M], I32)
            posf = sb(ctx, "posf", [P, M])
            fr = sb(ctx, "freq", [P, 32])
            an = sb(ctx, "angle", [P, 2, M, 32])
            tn = sb(ctx, "turns", [P, 2, M, 32])
            ti = sb(ctx, "turns_i", [P, 2, M, 32], I32)
            pos_landed, an_ready = sem("pos_landed"), sem("angle_ready")
            with nc.Block() as block:
                @block.sync
                def _(sp):
                    for m in range(M):
                        sp.dma_start(pos[:, m:m + 1], a["positions_2"][0:1, m * P:(m + 1) * P]
                                     .rearrange("o (p q) -> (o p) q", q=1)).then_inc(pos_landed.h, 16)
                    sp.dma_start(fr[:], a["rope_freq"].broadcast_to([P, 32])).then_inc(pos_landed.h, 16)

                @block.vector
                def _(dve):
                    step = Chain(dve, dve_step)
                    dve.wait_ge(pos_landed.h, 48)
                    step(nc.vector.tensor_copy(posf[:], pos[:]))
                    for m in range(M):
                        step(nc.vector.tensor_scalar(an[:, 1, m], fr[:], posf[:, m:m + 1], None, ALU.mult))
                    TWO_PI = 2 * math.pi
                    step(nc.vector.tensor_scalar(tn[:, 1], an[:, 1], 1 / TWO_PI, None, ALU.mult))
                    step(nc.vector.tensor_scalar(tn[:, 0], an[:, 1], 1 / TWO_PI, 0.25, ALU.mult, ALU.add))
                    step(nc.vector.tensor_copy(ti[:], tn[:]))
                    step(nc.vector.tensor_copy(tn[:], ti[:]))
                    c1 = 6.28125
                    c2 = math.floor((TWO_PI - c1) * 2 ** 21) / 2 ** 21
                    c3 = TWO_PI - c1 - c2
                    step(nc.vector.scalar_tensor_tensor(an[:, 0], tn[:, 0], -c1, an[:, 1], ALU.mult, ALU.add))
                    step(nc.vector.scalar_tensor_tensor(an[:, 1], tn[:, 1], -c1, an[:, 1], ALU.mult, ALU.add))
                    step(nc.vector.scalar_tensor_tensor(an[:], tn[:], -c2, an[:], ALU.mult, ALU.add))
                    step(nc.vector.scalar_tensor_tensor(an[:], tn[:], -c3, an[:], ALU.mult, ALU.add))
                    step(nc.vector.tensor_scalar(an[:, 0], an[:, 0], math.pi / 2, None, ALU.add))
                    step(nc.vector.tensor_scalar(tn[:], an[:], math.pi, -TWO_PI, ALU.is_gt, ALU.mult))
                    step(nc.vector.tensor_tensor(an[:], an[:], tn[:], ALU.add))
                    step(nc.vector.tensor_scalar(tn[:], an[:], -math.pi, TWO_PI, ALU.is_lt, ALU.mult))
                    step(nc.vector.tensor_tensor(an[:], an[:], tn[:], ALU.add))
                    edge = 3.14159250
                    nc.vector.tensor_scalar(an[:], an[:], edge, -edge, ALU.min, ALU.max).then_inc(an_ready.h, 1)

                @block.scalar
                def _(act):
                    act.wait_ge(an_ready.h, 1)
                    nc.scalar.activation(trig[:], an[:], ACT.Sin)

        def rope_beside(t1, t2, buf, heads):
            free0 = out_free.n

            def run(pool):
                step = Chain(pool, pool_step)
                for c in range(-(-heads // 8)):
                    nh = min(8, heads - 8 * c)
                    pool.wait_ge(out_free.h, free0 + 2 * c + 2)
                    for m in range(M):
                        v = buf[:, m, c * NB:c * NB + nh * HD].rearrange("p (h c e) -> p h c e", c=2, e=32)
                        cos = trig[:, 0, m].unsqueeze(1).broadcast_to([P, nh, 32])
                        sin = trig[:, 1, m].unsqueeze(1).broadcast_to([P, nh, 32])
                        e = nc.gpsimd
                        step(e.tensor_tensor(t1[:, 0:nh], v[:, :, 0], sin, ALU.mult))
                        step(e.tensor_tensor(t2[:, 0:nh], v[:, :, 1], sin, ALU.mult))
                        step(e.tensor_tensor(v[:, :, 0], v[:, :, 0], cos, ALU.mult))
                        step(e.tensor_tensor(v[:, :, 1], v[:, :, 1], cos, ALU.mult))
                        step(e.tensor_tensor(v[:, :, 0], v[:, :, 0], t2[:, 0:nh], ALU.subtract))
                        step(e.tensor_tensor(v[:, :, 1], v[:, :, 1], t1[:, 0:nh], ALU.add))
            return run

        lam_landed, lam_exp, sink_landed = sem("lam_landed"), sem("lam_exp"), sem("sink_landed")
        for layer in range(4):
            kind, inst = layer % 3, layer // 3
            s_in2, s_out2, s_ffn = second[layer]
            gain = layer * 4 * K8
            with ExitStack() as ctx:
                width = s_in2.n * NB if kind != 2 else 10 * P
                qkv = sb(ctx, "qkv", [P, M, width])
                beside = None
                if kind != 1:
                    t1 = sb(ctx, "rope_a", [P, 8, 32])
                    t2 = sb(ctx, "rope_b", [P, 8, 32])
                    beside = rope_beside(t1, t2, qkv, 4 * 8 if kind == 0 else 18)
                with ExitStack() as ctx2:
                    pre = Pre(ctx2)
                    if layer:
                        pre.add_normed((layer - 1, 3))
                    pre.norm(lambda k: featC[:, gain + k:gain + k + 1])
                    project(s_in2, hT, evac_act=to_sbuf(qkv, width), beside=beside, pre=pre)
                o = sb(ctx, "o", [P, M, D])
                qT = sb(ctx, "qT", [P, K8, S])
                scale = None
                if kind == 0:
                    lam_init = 0.8 - 0.6 * math.exp(-0.3 * layer)
                    kT = sb(ctx, "kT", [P, K8, S])
                    mask, mask_pool = make_masks(ctx, False)
                    lp = sb(ctx, "lam_params", [P, 4, HD])
                    lt = sb(ctx, "lam_terms", [P, 4])
                    pe_part, act_part = heads_to_feature(
                        [(qT[:, t], lambda m, t=t: qkv[:, m, t * P:(t + 1) * P]) for t in range(K8)] +
                        [(kT[:, t], lambda m, t=t: qkv[:, m, D + t * P:D + (t + 1) * P]) for t in range(K8)])
                    with nc.Block() as block:
                        block.tensor(pe_part)
                        block.gpsimd(mask_pool)

                        @block.sync
                        def _(sp):
                            sp.dma_start(lp[:].rearrange("p a b -> p (a b)"),
                                         a["a_lambda_2"][inst:inst + 1].rearrange("i a b -> i (a b)")
                                         .broadcast_to([P, 4 * HD])).then_inc(lam_landed.h, 16)

                        @block.vector
                        def _(dve):
                            step = Chain(dve, dve_step)
                            dve.wait_ge(lam_landed.h, lam_landed.n + 16)
                            for c in range(2):
                                step(nc.vector.tensor_tensor(lp[:, 2 * c], lp[:, 2 * c], lp[:, 2 * c + 1], ALU.mult))
                                step(nc.vector.reduce_sum(lt[:, c:c + 1], lp[:, 2 * c], AX))
                            nc.vector.tensor_copy(lt[:, 2:4], lt[:, 0:2]).then_inc(lam_exp.h, 1)
                            dve.wait_ge(lam_exp.h, lam_exp.n + 2)
                            step(nc.vector.tensor_tensor(lt[:, 2:3], lt[:, 1:2], lt[:, 0:1], ALU.subtract))
                            step(nc.vector.tensor_scalar(lt[:, 3:4], lt[:, 2:3], -lam_init, None, ALU.add))

                        @block.scalar
                        def _(act):
                            act.wait_ge(lam_exp.h, lam_exp.n + 1)
                            nc.scalar.activation(lt[:, 0:2], lt[:, 2:4], ACT.Exp).then_inc(lam_exp.h, 1)
                            act_part(act)
                    lam_landed.n += 16
                    lam_exp.n += 2
                    softmax_attention(qT, lambda t: kT[:, t],
                                      lambda t, c, j: qkv[:, j, 2 * D + t * P:2 * D + (t + 1) * P], o, mask,
                                      lam=lt[:, 3:4], vw=P)
                    with ExitStack() as ctx2, nc.Block() as block:
                        sq = sb(ctx2, "o_sq", [P, M, D])
                        hs = sb(ctx2, "head_ss", [P, 3, M, K8])
                        hs_ready = sem("head_ss_ready")

                        @block.vector
                        def _(dve):
                            step = Chain(dve, dve_step)
                            step(nc.vector.tensor_tensor(sq[:], o[:], o[:], ALU.mult))
                            nc.vector.reduce_sum(hs[:, 0], sq[:].rearrange("p m (h e) -> p m h e", e=P), AX) \
                                .then_inc(hs_ready.h, 1)
                            dve.wait_ge(hs_ready.h, hs_ready.n + 2)
                            step(nc.vector.reciprocal(hs[:, 2], hs[:, 1]))
                            step(nc.vector.tensor_scalar(hs[:, 2], hs[:, 2], 1.0 - lam_init, None, ALU.mult))
                            for m in range(M):
                                r = hs[:, 2, m].unsqueeze(2).broadcast_to([P, K8, P])
                                ov = o[:, m].rearrange("p (h e) -> p h e", e=P)
                                step(nc.vector.tensor_tensor(ov, ov, r, ALU.mult))

                        @block.scalar
                        def _(act):
                            act.wait_ge(hs_ready.h, hs_ready.n + 1)
                            nc.scalar.activation(hs[:, 1], hs[:, 0], ACT.Sqrt, scale=1.0 / P, bias=eps_of[RMS_EPS]) \
                                .then_inc(hs_ready.h, 1)
                    hs_ready.n += 2
                    sub = featB[:, B_SUB + inst:B_SUB + inst + 1]
                    scale = lambda k: sub
                elif kind == 1:
                    kT = sb(ctx, "kT", [P, K8, S])
                    stick_breaking(nc, sb, sem, ctx, qkv, qT, kT, o, heads_to_feature, K8, M, D, S,
                                   psG, psT, psA, dve_step, pool_step)
                else:
                    kd = sb(ctx, "k_twice", [P, M, 4, HD])
                    kT = sb(ctx, "kT2", [P, 2, S])
                    sinks = sb(ctx, "sinks", [P, 16])
                    mask, mask_pool = make_masks(ctx, True)
                    with nc.Block() as block:
                        block.gpsimd(mask_pool)

                        @block.sync
                        def _(sp):
                            sp.dma_start(sinks[:], a["c_sinks_2"][inst:inst + 1].broadcast_to([P, 16])) \
                                .then_inc(sink_landed.h, 16)
                            sp.wait_ge(sink_landed.h, sink_landed.n + 16)

                        @block.vector
                        def _(dve):
                            for m in range(M):
                                for r in range(4):
                                    o0 = D + (r // 2) * HD
                                    nc.vector.tensor_copy(kd[:, m, r], qkv[:, m, o0:o0 + HD])
                    sink_landed.n += 16
                    pe_part, act_part = heads_to_feature(
                        [(qT[:, t], lambda m, t=t: qkv[:, m, t * P:(t + 1) * P]) for t in range(K8)] +
                        [(kT[:, t], lambda m, t=t: kd[:, m, 2 * t:2 * t + 2].rearrange("p r e -> p (r e)"))
                         for t in range(2)])
                    with nc.Block() as block:
                        block.tensor(pe_part)
                        block.scalar(act_part)
                    softmax_attention(qT, lambda t: kT[:, t // 4],
                                      lambda t, c, j: qkv[:, j, D + 2 * HD + (t // 4) * HD:D + 2 * HD + (t // 4 + 1) * HD],
                                      o, mask, window=True, sink=sinks)
                out_projection(s_out2, o, scale)
            if stop == f"mix{layer}":
                add_alone(lambda pre: pre.add_normed((layer, 1)))
                return finish()
            gain2 = gain + 2 * K8
            with ExitStack() as ctx:
                pre = Pre(ctx)
                pre.add_normed((layer, 1))
                pre.norm(lambda k: featC[:, gain2 + k:gain2 + k + 1])
                gated_units(s_ffn, pre=pre)
            if stop == f"ffn{layer}" or layer == 3:
                add_alone(lambda pre: pre.add_normed((layer, 3)))
                return finish()


def stick_breaking(nc, sb, sem, ctx, qkv, qT, kT, o, heads_to_feature, K8, M, D, S, psG, psT, psA, dve_step, pool_step):
    W = 3 * P
    see = sb(ctx, "seen", [P, W])
    later = sb(ctx, "later", [P, P])
    allk = sb(ctx, "all_ones", [P, P])
    pe_part, act_part = heads_to_feature(
        [(qT[:, t], lambda m, t=t: qkv[:, m, t * P:(t + 1) * P]) for t in range(K8)] +
        [(kT[:, t], lambda m, t=t: qkv[:, m, D + t * P:D + (t + 1) * P]) for t in range(K8)])
    with nc.Block() as block:
        block.tensor(pe_part)
        block.scalar(act_part)

        @block.gpsimd
        def _(pool):
            step = Chain(pool, pool_step)
            nc.gpsimd.memset(allk[:], 1.0)
            step(nc.gpsimd.memset(see[:], 1.0))
            step(nc.gpsimd.memset(later[:], 1.0))
            for s in (slice(0, P), slice(2 * P, W)):
                nc.gpsimd.affine_select(out=see[:, s], in_=see[:, s], compare_op=ALU.is_gt, fill=0.0, base=0,
                                        pattern=[[1, P]], channel_multiplier=-1)
            step(nc.gpsimd.affine_select(out=later[:], in_=later[:], compare_op=ALU.is_gt, fill=0.0, base=0,
                                         pattern=[[-1, P]], channel_multiplier=1))
    z_ready, az_ready, ln_ready, L_ready, suf_ready, t_ready, e_ready, a_ready, so_ready, so_taken = (
        sem(n) for n in ("z_ready", "abs_z_ready", "log1p_ready", "log_rest_ready", "suffix_ready",
                         "log_a_ready", "exp_a_ready", "a_ready", "stick_o_ready", "stick_o_taken"))
    with ExitStack() as c2, nc.Block() as block:
        az = sb(c2, "abs_z", [P, 2, W])
        ez = sb(c2, "exp_z", [P, 2, W])
        rl = sb(c2, "relu_z", [P, 2, W])
        Lm = sb(c2, "log_rest", [P, 2, W])
        tt = sb(c2, "log_a", [P, 2, W])
        NH = 2 * K8

        @block.tensor
        def _(pe):
            def scores(n):
                t, b = n // 2, n % 2
                r = slice(HD * (n % 2), HD * (n % 2 + 1))
                if n >= 2:
                    pe.wait_ge(L_ready.h, 2 * (n - 1))
                nc.tensor.matmul(psG[:, b, 0:2 * P], kT[r, t, 0:P], qT[r, t, :], start=True, stop=True)
                nc.tensor.matmul(psG[:, b, 2 * P:W], kT[r, t, P:2 * P], qT[r, t, P:2 * P], start=True, stop=True) \
                    .then_inc(z_ready.h, 1)

            def suffix(n):
                b = n % 2
                pe.wait_ge(L_ready.h, 2 * n + 2)
                if n >= 2:
                    pe.wait_ge(t_ready.h, n - 1)
                nc.tensor.matmul(psT[:, b, 0:W], later[:], Lm[:, b], start=True, stop=False)
                nc.tensor.matmul(psT[:, b, P:2 * P], allk[:], Lm[:, b, 2 * P:W], start=False, stop=True) \
                    .then_inc(suf_ready.h, 1)

            def values(n):
                b = n % 2
                pe.wait_ge(a_ready.h, n + 1)
                if n >= 2:
                    pe.wait_ge(so_taken.h, n - 1)
                v = [qkv[:, j, 2 * D + n * HD:2 * D + (n + 1) * HD] for j in range(2)]
                nc.tensor.matmul(psA[:, b, 0:HD], tt[:, b, 0:P], v[0], start=True, stop=True)
                nc.tensor.matmul(psA[:, b, HD:2 * HD], tt[:, b, P:2 * P], v[0], start=True, stop=False)
                nc.tensor.matmul(psA[:, b, HD:2 * HD], tt[:, b, 2 * P:W], v[1], start=False, stop=True) \
                    .then_inc(so_ready.h, 1)
            scores(0)
            for n in range(NH + 2):
                if 1 <= n <= NH:
                    suffix(n - 1)
                if n + 1 < NH:
                    scores(n + 1)
                if n >= 2:
                    values(n - 2)

        @block.scalar
        def _(act):
            def absolute(n):
                b = n % 2
                act.wait_ge(z_ready.h, n + 1)
                if n >= 2:
                    act.wait_ge(L_ready.h, 2 * (n - 1))
                nc.scalar.activation(az[:, b], psG[:, b, 0:W], ACT.Abs).then_inc(az_ready.h, 1)

            def logs(n):
                b = n % 2
                act.wait_ge(az_ready.h, n + 1)
                nc.scalar.activation(ez[:, b], az[:, b], ACT.Exp, scale=-ATT_SCALE).then_inc(ln_ready.h, 1)
                act.wait_ge(ln_ready.h, 2 * n + 1)
                nc.scalar.activation(ez[:, b], ez[:, b], ACT.Ln, bias=1.0).then_inc(ln_ready.h, 1)

            def exps(n):
                b = n % 2
                act.wait_ge(t_ready.h, n + 1)
                nc.scalar.activation(tt[:, b], tt[:, b], ACT.Exp).then_inc(e_ready.h, 1)
            for n in range(NH + 1):
                if n < NH:
                    absolute(n)
                    logs(n)
                if n >= 1:
                    exps(n - 1)

        @block.vector
        def _(dve):
            step = Chain(dve, dve_step)

            def front(n):
                b = n % 2
                z = psG[:, b, 0:W]
                dve.wait_ge(az_ready.h, n + 1)
                step(nc.vector.tensor_scalar(rl[:, b], z, 0.0, ATT_SCALE, ALU.max, ALU.mult))
                dve.wait_ge(ln_ready.h, 2 * n + 2)
                step(nc.vector.scalar_tensor_tensor(rl[:, b], ez[:, b], -1.0, rl[:, b], ALU.mult, ALU.subtract))
                nc.vector.tensor_tensor(Lm[:, b], rl[:, b], see[:], ALU.mult).then_inc(L_ready.h, 1)
                if n >= 2:
                    dve.wait_ge(so_ready.h, n - 1)
                nc.vector.scalar_tensor_tensor(tt[:, b], z, ATT_SCALE, rl[:, b], ALU.mult, ALU.add) \
                    .then_inc(L_ready.h, 1)

            def middle(n):
                b = n % 2
                dve.wait_ge(suf_ready.h, n + 1)
                nc.vector.tensor_tensor(tt[:, b], tt[:, b], psT[:, b, 0:W], ALU.add).then_inc(t_ready.h, 1)

            def late(n):
                b = n % 2
                dve.wait_ge(e_ready.h, n + 1)
                nc.vector.tensor_tensor(tt[:, b], tt[:, b], see[:], ALU.mult).then_inc(a_ready.h, 1)

            def back(n):
                b = n % 2
                dve.wait_ge(so_ready.h, n + 1)
                nc.vector.tensor_copy(o[:, :, n * HD:(n + 1) * HD],
                                      psA[:, b, 0:2 * HD].rearrange("p (m e) -> p m e", m=2)) \
                    .then_inc(so_taken.h, 1)
            for n in range(NH + 2):
                if n >= 2:
                    late(n - 2)
                if 1 <= n <= NH:
                    middle(n - 1)
                if n < NH:
                    front(n)
                if n >= 2:
                    back(n - 2)


_INS = ["x", "c", "ada_w", "ada_b", "norm_mix", "norm_ffn", "a_w_in", "a_b_in", "a_ln_g", "a_ln_b", "a_w_s", "a_b_s",
        "a_w_out", "kv_norm", "kv_ada_w", "kv_ada_b", "kv_w_k", "kv_w_v", "b_w_q", "b_w_o", "moe_router", "moe_bias",
        "moe_w_gate", "moe_w_up", "moe_w_down", "sh_w_gate", "sh_w_up", "sh_w_down", "final_norm", "positions_2",
        "norm_gains_2", "a_w_in_2", "a_w_out_2", "a_lambda_2", "a_subln_2", "b_w_in_2", "b_w_out_2", "c_w_in_2",
        "c_w_out_2", "c_sinks_2", "ffn_w_gate_2", "ffn_w_up_2", "ffn_w_down_2"]
STOP = None


def kernel(**inputs):
    import numpy as np
    import concourse.bacc as bacc
    from concourse.bass_utils import run_bass_kernel_spmd

    nc = bacc.Bacc("TRN2", target_bir_lowering=False, num_devices=1)
    freq = (ROPE_THETA ** (-np.arange(0, HD, 2, dtype=np.float32) / np.float32(HD))).astype(np.float32)
    arrays, args = {}, {}
    for name in _INS + ["rope_freq"]:
        arr = freq[None] if name == "rope_freq" else np.ascontiguousarray(inputs[name])
        arrays[f"in_{name}"] = arr
        args[name] = nc.dram_tensor(f"in_{name}", arr.shape, mybir.dt.from_np(arr.dtype), kind="ExternalInput").ap()
    out = nc.dram_tensor("out", inputs["x"].shape, F32, kind="ExternalOutput").ap()
    build(nc, args, out, STOP)
    r = run_bass_kernel_spmd(nc, [arrays], core_ids=[0])
    return r.results[0]["out"]
```

```python
import math
from contextlib import ExitStack

import concourse.bass as bass
from concourse import mybir

F32 = mybir.dt.float32
F32R = mybir.dt.float32r
I32 = mybir.dt.int32
ALU = mybir.AluOpType
ACT = mybir.ActivationFunctionType
AX = mybir.AxisListType.X

P = 128
NEG = -1e30
RMS_EPS = 1e-6
LN_EPS = 1e-5
ROUTED_SCALE = 2.5
ROPE_THETA = 10000.0
HD = 64
ATT_SCALE = HD ** -0.5


def at(base, i, step):
    return base if i is None else base + i * step


class Sem:

    def __init__(self, ctx, nc, name):
        self.h = ctx.enter_context(nc.semaphore(name))
        self.n = 0


class Chain:

    def __init__(self, eng, sem):
        self.eng, self.sem, self.i, self.step = eng, sem, None, 0

    def __call__(self, ins):
        self.sem.n += 1
        ins.then_inc(self.sem.h, 1)
        self.eng.wait_ge(self.sem.h, at(self.sem.n, self.i, self.step))


def build(nc, a, out, stop=None):
    S, D = a["x"].shape[1:]
    M = S // P
    K8 = D // P
    NB = 512
    HALF = K8 // 2
    E = a["moe_router"].shape[2]
    EH = a["moe_w_gate"].shape[3]
    AW = a["a_w_out"].shape[1]
    NG = a["a_w_s"].shape[1]
    FFN = a["ffn_w_gate_2"].shape[2]
    assert M == 2 and K8 == 8 and EH == 2 * P and FFN % EH == 0

    with ExitStack() as top:
        names = {}

        def sb(ctx, name, shape, dt=F32):
            names[name] = names.get(name, 0) + 1
            return ctx.enter_context(nc.sbuf_tensor(f"{name}_{names[name]}", shape, dt))

        sems = {}

        def sem(name):
            if name not in sems:
                sems[name] = Sem(top, nc, name)
            return sems[name]

        x = sb(top, "x", [P, M, D])
        gu_raw = sb(top, "gu_raw", [P, 2, K8, NB])
        gu_hi = sb(top, "gu_hi", [P, K8, NB], F32R)
        gu_lo = sb(top, "gu_lo", [P, K8, NB], F32R)
        dn_raw = sb(top, "dn_raw", [P, 2, 2, D])
        dn_hi = sb(top, "dn_hi", [P, 2, D], F32R)
        dn_lo = sb(top, "dn_lo", [P, 2, D], F32R)
        hT_both = sb(top, "hT", [P, 2, K8, S], F32R)
        hT_hi, hT_lo = hT_both[:, 0], hT_both[:, 1]
        ident = sb(top, "ident", [P, P])
        ones = sb(top, "ones", [P, P])
        featA = sb(top, "featA", [P, P])
        featB = sb(top, "featB", [P, P])
        featC = sb(top, "featC", [P, P])
        mods = sb(top, "mods", [P, P])
        cs = sb(top, "cs", [P, K8])
        gates = sb(top, "gates", [P, 2, D])
        gateval = sb(top, "gateval", [P, M, E])
        aff = sb(top, "aff", [P, 2, K8])
        actout = sb(top, "actout", [P, D])
        consts = sb(top, "eps", [P, 2])
        eps_of = {RMS_EPS: consts[:, 0:1], LN_EPS: consts[:, 1:2]}

        psA = top.enter_context(nc.psum_tensor("psA", [P, 4, NB], F32))
        psG = top.enter_context(nc.psum_tensor("psG", [P, 2, NB], F32))
        psT = top.enter_context(nc.psum_tensor("psT", [P, 2, NB], F32))

        COL_C, COL_KVB = 112, 96

        landed = [[sem(f"gu_landed_{s}{h}") for h in range(2)] for s in range(2)]
        dn_landed = [sem(f"dn_landed_{s}") for s in range(2)]
        gu_hi_ready, gu_lo_ready, gu_used = sem("gu_hi_ready"), sem("gu_lo_ready"), sem("gu_used")
        dn_hi_ready, dn_lo_ready, dn_used = sem("dn_hi_ready"), sem("dn_lo_ready"), sem("dn_used")
        dve_step, pool_step, act_step = sem("dve_step"), sem("pool_step"), sem("act_step")

        count = {"g": 0, "d": 0}

        class Stream:

            def __init__(self, n, src, dn_src=None):
                self.n, self.src, self.dn_src = n, src, dn_src
                self.g, self.d = count["g"], count["d"]
                count["g"] += n
                if dn_src:
                    count["d"] += n

            def load_gu(self, sp, c, i=None):
                g, step = self.g + c, 0 if i is None else 2
                for h in range(2):
                    if g >= 2:
                        sp.wait_ge(gu_lo_ready.h, at(2 * g + h - 3, i, 4))
                    for q in range(2):
                        sp.dma_start(gu_raw[:, g % 2, h * HALF:(h + 1) * HALF, q * 256:(q + 1) * 256],
                                     self.src(at(c, i, step), h, q)).then_inc(landed[g % 2][h].h, 16)

            def load_dn(self, sp, c, i=None):
                d = self.d + c
                if d >= 2:
                    sp.wait_ge(dn_lo_ready.h, at(d - 1, i, 2))
                sp.dma_start(dn_raw[:, d % 2], self.dn_src(at(c, i, 2))).then_inc(dn_landed[d % 2].h, 16)

            def first_loads(self, sp):
                for c in range(min(2, self.n)):
                    self.load_gu(sp, c)
                    if self.dn_src:
                        self.load_dn(sp, c)

            def hi(self, act, c, h, i=None):
                g = self.g + c
                act.wait_ge(landed[g % 2][h].h, at(32 * (g // 2 + 1), i, 32))
                if g >= 1:
                    act.wait_ge(gu_used.h, at(2 * g + h - 1, i, 4))
                nc.scalar.activation(gu_hi[:, h * HALF:(h + 1) * HALF], gu_raw[:, g % 2, h * HALF:(h + 1) * HALF],
                                     ACT.Copy).then_inc(gu_hi_ready.h, 1)

            def lo(self, dve, c, h, i=None):
                g = self.g + c
                dve.wait_ge(gu_hi_ready.h, at(2 * g + h + 1, i, 4))
                sl = slice(h * HALF, (h + 1) * HALF)
                nc.vector.tensor_tensor(gu_lo[:, sl], gu_raw[:, g % 2, sl], gu_hi[:, sl].bitcast(F32),
                                        ALU.subtract).then_inc(gu_lo_ready.h, 1)

            def dhi(self, act, c, i=None):
                d = self.d + c
                act.wait_ge(dn_landed[d % 2].h, at(16 * (d // 2 + 1), i, 16))
                if d >= 1:
                    act.wait_ge(dn_used.h, at(d, i, 2))
                nc.scalar.activation(dn_hi[:], dn_raw[:, d % 2], ACT.Copy).then_inc(dn_hi_ready.h, 1)

            def dlo(self, dve, c, i=None):
                d = self.d + c
                dve.wait_ge(dn_hi_ready.h, at(d + 1, i, 2))
                nc.vector.tensor_tensor(dn_lo[:], dn_raw[:, d % 2], dn_hi[:].bitcast(F32),
                                        ALU.subtract).then_inc(dn_lo_ready.h, 1)

        def cols(w):
            v = w.rearrange("(k p) n -> p k n", p=P)
            last = w.shape[1] // NB if w.shape[1] % NB else -1

            def src(c, h, q):
                if isinstance(c, int) and c == last:
                    q = 0
                return v[:, h * HALF:(h + 1) * HALF, bass.ds(c * NB + q * 256, 256)]
            return Stream(-(-w.shape[1] // NB), src)

        def cols_deep(w):
            v = w.rearrange("(k p) n -> p k n", p=P)
            deep = w.shape[0] // D

            def src(c, h, q):
                k0 = (c % deep) * K8 + h * HALF
                return v[:, k0:k0 + HALF, (c // deep) * NB + q * 256:(c // deep) * NB + q * 256 + 256]
            return Stream(deep * w.shape[1] // NB, src)

        def experts(layer):
            def src(c, h, q):
                one = isinstance(c, int) and c == 0
                name = ("gate", "up")[q]
                w = a[f"sh_w_{name}"][layer] if one else \
                    a[f"moe_w_{name}"][layer, bass.ds(c - 1, 1)].rearrange("e r n -> (e r) n")
                return w.rearrange("(k p) n -> p k n", p=P)[:, h * HALF:(h + 1) * HALF]

            def dn_src(c):
                one = isinstance(c, int) and c == 0
                w = a["sh_w_down"][layer] if one else \
                    a["moe_w_down"][layer, bass.ds(c - 1, 1)].rearrange("e r n -> (e r) n")
                return w.rearrange("(k p) n -> p k n", p=P)
            return Stream(E + 1, src, dn_src)

        def ffn(layer):
            def src(c, h, q):
                w = a[("ffn_w_gate_2", "ffn_w_up_2")[q]][layer].rearrange("(k p) n -> p k n", p=P)
                return w[:, h * HALF:(h + 1) * HALF, bass.ds(c * EH, EH)]

            def dn_src(c):
                return a["ffn_w_down_2"][layer].rearrange("(c k p) n -> c p k n", p=P, k=2)[bass.ds(c, 1)] \
                    .rearrange("c p k n -> (c p) k n")
            return Stream(FFN // EH, src, dn_src)

        s_in = cols(a["a_w_in"][0])
        s_out = cols_deep(a["a_w_out"][0])
        s_moe = [experts(0)]
        s_k, s_v = cols(a["kv_w_k"]), cols(a["kv_w_v"])
        s_q, s_o = cols(a["b_w_q"][0]), cols(a["b_w_o"][0])
        s_moe.append(experts(1))
        second = []
        for layer in range(4):
            kind, inst = layer % 3, layer // 3
            n = "abc"[kind]
            second.append((cols(a[f"{n}_w_in_2"][inst]), cols(a[f"{n}_w_out_2"][inst]), ffn(layer)))
        order = [s_in, s_out, s_moe[0], s_k, s_v, s_q, s_o, s_moe[1]] + [s for t in second for s in t]

        def following(stream):
            k = order.index(stream) + 1
            return order[k] if k < len(order) else None

        def first_halves(stream):
            return range(0 if stream is order[0] else 1, 2)

        def start_act(act, stream, pre):
            def split():
                for h in first_halves(stream):
                    stream.hi(act, 0, h)
            if pre:
                pre.act(act, split)
            else:
                split()

        def start_dve(dve, stream, pre):
            def split():
                for h in first_halves(stream):
                    stream.lo(dve, 0, h)
            if pre:
                pre.dve(dve, split)
            else:
                split()

        def mm3(ps, lhs, rhs, start, stop):
            (ah, al), (bh, bl) = lhs, rhs
            nc.tensor.matmul(ps, ah, bh, start=start, stop=False)
            nc.tensor.matmul(ps, ah, bl, start=False, stop=False)
            return nc.tensor.matmul(ps, al, bh, start=False, stop=stop)

        out_free = sem("out_free")

        def project(stream, lhs, evac_act=None, evac_dve=None, deep=1, keep=False, beside=None,
                    pre=None):
            n = stream.n
            pairs = 0 if deep > 1 or keep else (n - 1) // 2
            if pairs < 2:
                pairs = 0
            free0 = out_free.n
            with nc.Block() as block:
                if beside:
                    block.gpsimd(beside)

                def turns(eng, body):
                    if pairs:
                        with eng.Fori(0, pairs) as i:
                            body(0, i)
                            body(1, i)
                    for c in range(2 * pairs, n):
                        body(c, None)

                @block.sync
                def _(sp):
                    if pre:
                        pre.sp(sp)

                    def body(c, i):
                        if i is not None or c + 2 < n:
                            stream.load_gu(sp, c + 2, i)
                    if pairs:
                        done = 2 * pairs + 2 > n
                        turns_n = pairs - 1 if done else pairs
                        with sp.Fori(0, turns_n) as i:
                            body(0, i)
                            body(1, i)
                        for c in range(2 * turns_n, n):
                            body(c, None)
                    else:
                        for c in range(n):
                            body(c, None)
                    nxt = following(stream)
                    if nxt:
                        nxt.first_loads(sp)

                @block.tensor
                def _(pe):
                    def body(c, i):
                        g, o = stream.g + c, c // deep
                        bank = 2 * (o % 2)
                        for h in range(2):
                            pe.wait_ge(gu_lo_ready.h, at(2 * g + h + 1, i, 4))
                            if h == 0 and c % deep == 0 and (o >= 2 or i is not None) and not keep:
                                pe.wait_ge(out_free.h, at(free0 + 2 * (o - 1), i, 4))
                            for k in range(h * HALF, (h + 1) * HALF):
                                if pre and c < deep and i is None:
                                    pre.wait_turned(pe, c * K8 + k)
                                for m in range(M):
                                    hi, lo = lhs(m, (c % deep) * K8 + k)
                                    dst = psA[:, 2 * m + o % 2] if keep else psA[:, bank + m]
                                    last = mm3(dst, (hi, lo), (gu_hi[:, k], gu_lo[:, k]),
                                               k == 0 and c % deep == 0, k == K8 - 1 and c % deep == deep - 1)
                            last.then_inc(gu_used.h, 1)
                    if pre:
                        pre.pe(pe)
                    if pairs:
                        body(0, None)
                        body(1, None)
                        with pe.Fori(1, pairs) as i:
                            body(0, i)
                            body(1, i)
                    for c in range(2 * pairs, n):
                        body(c, None)

                @block.scalar
                def _(act):
                    start_act(act, stream, pre)

                    def body(c, i):
                        if i is not None or c + 1 < n:
                            for h in range(2):
                                stream.hi(act, c + 1, h, i)
                        elif following(stream):
                            following(stream).hi(act, 0, 0)
                        if evac_act and c % deep == deep - 1:
                            act.wait_ge(gu_used.h, at(2 * (stream.g + c) + 2, i, 4))
                            for ins in evac_act(c // deep, i, 2 * (c // deep % 2)):
                                ins.then_inc(out_free.h, 1)
                    turns(act, body)

                @block.vector
                def _(dve):
                    start_dve(dve, stream, pre)

                    def body(c, i):
                        if i is not None or c + 1 < n:
                            for h in range(2):
                                stream.lo(dve, c + 1, h, i)
                        elif following(stream):
                            following(stream).lo(dve, 0, 0)
                        if evac_dve and c % deep == deep - 1:
                            dve.wait_ge(gu_used.h, at(2 * (stream.g + c) + 2, i, 4))
                            for ins in evac_dve(c // deep, i, 2 * (c // deep % 2)):
                                ins.then_inc(out_free.h, 1)
                    turns(dve, body)
            if not keep:
                out_free.n += 2 * (n // deep)

        def to_sbuf(dst, n_cols):
            def evac(c, i, bank):
                w = min(NB, n_cols - c * NB) if i is None else NB
                for m in range(M):
                    yield nc.scalar.activation(dst[:, m, bass.ds(at(c, i, 2) * NB, w)], psA[:, bank + m, 0:w],
                                               ACT.Copy)
            return evac

        def hT(m, k):
            return hT_hi[:, k, m * P:(m + 1) * P], hT_lo[:, k, m * P:(m + 1) * P]

        ss_ready, root_ready, gain_landed = sem("ss_ready"), sem("root_ready"), sem("gain_landed")
        x_added, diag_ready = sem("x_added"), sem("diag_ready")
        turned, turned_out, turned_hi, turned_lo = sem("turned"), sem("turned_out"), sem("turned_hi"), sem("turned_lo")

        def as_banks(ap):
            return ap.rearrange("p (c n) -> p c n", c=2)

        acc = psA[:].rearrange("p (m c) n -> p m c n", m=M)

        def root_parts(sums, src, n, eps, ready=None):
            s0, r0 = ss_ready.n, root_ready.n
            ss_ready.n += M
            root_ready.n += M

            def act_part(act):
                for m in range(M):
                    if ready is not None:
                        act.wait_ge(x_added.h, ready + m + 1)
                    sink = actout[:] if len(src(m).shape) == 2 else as_banks(actout[:])
                    nc.scalar.activation(sink, src(m), ACT.Square, accum_out=sums[:, 0, m:m + 1]) \
                        .then_inc(ss_ready.h, 1)
                    act.wait_ge(ss_ready.h, s0 + m + 1)
                    nc.scalar.activation(sums[:, 1, m:m + 1], sums[:, 0, m:m + 1], ACT.Sqrt, scale=1.0 / n,
                                         bias=eps_of[eps]).then_inc(root_ready.h, 1)

            def reciprocal(dve, step, m):
                dve.wait_ge(root_ready.h, r0 + m + 1)
                step(nc.vector.reciprocal(sums[:, 2, m:m + 1], sums[:, 1, m:m + 1]))
                return sums[:, 2, m:m + 1]
            return act_part, reciprocal

        class Pre:

            def __init__(self, ctx, banks=psT):
                self.banks = banks
                self.ctx, self.sps, self.acts, self.dves, self.pes = ctx, [], [], [], []
                self.x_from, self.lo_from = None, None

            def sp(self, sp):
                for part in self.sps:
                    part(sp)

            def pe(self, pe):
                for part in self.pes:
                    part(pe)

            def act(self, act, split):
                if len(self.acts) > 1:
                    self.acts[0](act)
                split()
                for part in self.acts[1 if len(self.acts) > 1 else 0:]:
                    part(act)

            def dve(self, dve, split):
                for part in self.dves[:-1]:
                    part(dve)
                if self.lo_from is None:
                    self.dves[-1](dve)
                    split()
                else:
                    self.dves[-1](dve, split)

            def wait_turned(self, pe, k):
                if k % 2 == 0:
                    pe.wait_ge(turned_lo.h, self.lo_from + k // 2 + 1)

            def alone(self):
                with nc.Block() as block:
                    block.sync(self.sp)
                    block.tensor(self.pe)
                    block.scalar(lambda act: self.act(act, lambda: None))
                    block.vector(lambda dve: self.dve(dve, lambda: None))

            def add_gated(self, gate):
                t = sb(self.ctx, "gated", [P, M, D])
                self.x_from = x_added.n
                x_added.n += M

                def dve_part(dve):
                    step = Chain(dve, dve_step)
                    for m in range(M):
                        step(nc.vector.tensor_tensor(as_banks(t[:, m]), acc[:, m], as_banks(gates[:, gate]),
                                                     ALU.mult))
                        nc.vector.tensor_tensor(x[:, m], x[:, m], t[:, m], ALU.add).then_inc(x_added.h, 1)
                self.dves.append(dve_part)

            def add_normed(self, row):
                t = sb(self.ctx, "normed", [P, M, D])
                gain = sb(self.ctx, "gain", [P, D])
                sums = sb(self.ctx, "out_sums", [P, 3, M])
                g0 = gain_landed.n
                gain_landed.n += 16
                self.x_from = x_added.n
                x_added.n += M
                act_part, reciprocal = root_parts(sums, lambda m: acc[:, m], D, RMS_EPS)

                def sp_part(sp):
                    sp.dma_start(gain[:], a["norm_gains_2"][row[0], row[1]:row[1] + 1].broadcast_to([P, D])) \
                        .then_inc(gain_landed.h, 16)

                def dve_part(dve):
                    step = Chain(dve, dve_step)
                    dve.wait_ge(gain_landed.h, g0 + 16)
                    for m in range(M):
                        r = reciprocal(dve, step, m)
                        step(nc.vector.scalar_tensor_tensor(as_banks(t[:, m]), acc[:, m], r, as_banks(gain[:]),
                                                            ALU.mult, ALU.mult))
                        nc.vector.tensor_tensor(x[:, m], x[:, m], t[:, m], ALU.add).then_inc(x_added.h, 1)
                self.sps.append(sp_part)
                self.acts.append(act_part)
                self.dves.append(dve_part)

            def turn(self, src, kt, hi, lo, scale=None, shift=None, moving=None, full=None):
                R = kt // 2
                tmp = full[:].rearrange("p (r k) s -> p r k s", k=2) if full else \
                    sb(self.ctx, "turned_full", [P, 2, 2, S])
                slots = R if full else 2
                b0 = turned.n
                for s in (turned, turned_out, turned_hi, turned_lo):
                    s.n += R
                self.lo_from = b0

                def pe_part(pe):
                    for r in range(R):
                        if r >= 2:
                            pe.wait_ge(turned_out.h, b0 + r - 1)
                        for k in range(2):
                            for m in range(M):
                                dst = self.banks[:, r % 2, k * S + m * P:k * S + (m + 1) * P]
                                if moving:
                                    last = nc.tensor.matmul(dst, src(m, 2 * r + k), moving(m), start=True, stop=True)
                                else:
                                    last = nc.tensor.transpose(dst, src(m, 2 * r + k), ident[:])
                        last.then_inc(turned.h, 1)

                def act_part(act):
                    for r in range(R):
                        act.wait_ge(turned_out.h, b0 + r + 1)
                        nc.scalar.activation(hi[:, 2 * r:2 * r + 2], tmp[:, r % slots], ACT.Copy) \
                            .then_inc(turned_hi.h, 1)

                def dve_part(dve, split):
                    def out(r):
                        dve.wait_ge(turned.h, b0 + r + 1)
                        if r >= slots:
                            dve.wait_ge(turned_lo.h, b0 + r - 1)
                        if scale is None:
                            ins = nc.vector.tensor_copy(tmp[:, r % slots].rearrange("p k s -> p (k s)"),
                                                        self.banks[:, r % 2])
                        for k in range(0 if scale is None else 2):
                            f, part, dst = 2 * r + k, self.banks[:, r % 2, k * S:(k + 1) * S], tmp[:, r % slots, k]
                            if shift is None:
                                ins = nc.vector.tensor_scalar(dst, part, scale(f), None, ALU.mult)
                            else:
                                ins = nc.vector.tensor_scalar(dst, part, scale(f), shift(f), ALU.mult, ALU.add)
                        ins.then_inc(turned_out.h, 1)

                    def low(r):
                        dve.wait_ge(turned_hi.h, b0 + r + 1)
                        nc.vector.tensor_tensor(lo[:, 2 * r:2 * r + 2], tmp[:, r % slots],
                                                hi[:, 2 * r:2 * r + 2].bitcast(F32),
                                                ALU.subtract).then_inc(turned_lo.h, 1)
                    for r in range(R + 1):
                        if r < R:
                            out(r)
                        if r >= 1:
                            low(r - 1)
                        if r == 2:
                            split()
                self.pes.append(pe_part)
                self.acts.append(act_part)
                self.dves.append(dve_part)

            def norm(self, scale, shift=None, before_dve=None, full=None):
                sums = sb(self.ctx, "x_sums", [P, 3, M])
                diag = sb(self.ctx, "diag", [P, M, P])
                act_part, reciprocal = root_parts(sums, lambda m: x[:, m], D, RMS_EPS, self.x_from)
                d0 = diag_ready.n
                diag_ready.n += M

                def dve_part(dve):
                    step = Chain(dve, dve_step)
                    if before_dve:
                        before_dve(step)
                    for m in range(M):
                        r = reciprocal(dve, step, m)
                        nc.vector.tensor_scalar(diag[:, m], ident[:], r, None, ALU.mult).then_inc(diag_ready.h, 1)
                self.acts.append(act_part)
                self.dves.append(dve_part)
                self.pes.append(lambda pe: pe.wait_ge(diag_ready.h, d0 + M))
                self.turn(lambda m, k: x[:, m, k * P:(k + 1) * P], K8, hT_hi, hT_lo, scale, shift,
                          lambda m: diag[:, m], full)

            def modulate(self, norm_col, shift_col, scale_col, full=None):
                def before(step):
                    step(nc.vector.scalar_tensor_tensor(aff[:, 0], mods[:, scale_col:scale_col + K8], 1.0,
                                                        featB[:, norm_col:norm_col + K8], ALU.add, ALU.mult))
                self.norm(lambda k: aff[:, 0, k:k + 1], lambda k: mods[:, shift_col + k:shift_col + k + 1], before,
                          full)

        gate_low, gate_sum, up_low, up_sum = (sem(n) for n in ("gate_low", "gate_sum", "up_low", "up_sum"))
        h_ready, up_ready, silu_ready = sem("unit_h_ready"), sem("unit_up_ready"), sem("unit_silu_ready")
        hu_hi_ready, hu_lo_ready = sem("unit_h_hi"), sem("unit_h_lo")
        w_landed = [sem("weight_landed_0"), sem("weight_landed_1")]
        w_turned, w_copied, w_stored = sem("weights_turned"), sem("weights_copied"), sem("weights_stored")

        def gated_units(stream, weight=None, w_dram=None, beside=None, pre=None):
            U = stream.n
            n = (U - 1) // 2 - 1
            assert U == 2 * n + 3
            q = {s: s.n for s in (gate_low, gate_sum, up_low, up_sum, h_ready, up_ready, silu_ready, hu_hi_ready,
                                  hu_lo_ready, w_turned, w_copied, w_stored, *w_landed)}
            g0, d0 = stream.g, stream.d
            weighted = weight is not None
            with ExitStack() as ctx:
                sg = sb(ctx, "silu_g", [P, 2, S])
                gl = sb(ctx, "gate_low", [P, 2, S])
                ul = sb(ctx, "up_low", [P, 2, S])
                hf = sb(ctx, "unit_h", [P, 2, S])
                huh = sb(ctx, "unit_h_hi", [P, 2, S], F32R)
                hul = sb(ctx, "unit_h_lo", [P, 2, S], F32R)
                if weighted:
                    wT = sb(ctx, "weights_T", [U - 1, S])
                    wrow = sb(ctx, "weight_row", [P, 2, S])
                with nc.Block() as block:
                    if beside:
                        block.gpsimd(beside)

                    def turns(eng, body):
                        for j in range(3):
                            body(j, None)
                        with eng.Fori(1, n) as i:
                            body(1, i)
                            body(2, i)
                        body(U - 2, None)
                        body(U - 1, None)

                    @block.sync
                    def _(sp):
                        if pre:
                            pre.sp(sp)
                        if weighted:
                            sp.wait_ge(w_copied.h, q[w_copied] + 1)
                            sp.dma_start(w_dram, wT[:]).then_inc(w_stored.h, 16)

                        def body(j, i):
                            if i is not None or j + 2 < U:
                                stream.load_gu(sp, j + 2, i)
                                stream.load_dn(sp, j + 2, i)
                        turns(sp, body)
                        nxt = following(stream)
                        if nxt:
                            nxt.first_loads(sp)

                    @block.tensor
                    def _(pe):
                        if pre:
                            pre.pe(pe)
                        if weighted:
                            for m in range(M):
                                last = nc.tensor.transpose(psA[0:U - 1, 0, m * P:(m + 1) * P], weight[:, m], ident[:])
                            last.then_inc(w_turned.h, 1)

                        def down(j, i):
                            pe.wait_ge(dn_lo_ready.h, at(d0 + j + 1, i, 2))
                            pe.wait_ge(hu_lo_ready.h, at(q[hu_lo_ready] + j + 1, i, 2))
                            for k in range(2):
                                for m in range(M):
                                    lhs = huh[:, k, m * P:(m + 1) * P], hul[:, k, m * P:(m + 1) * P]
                                    for c in range(2):
                                        first = j == 0 and i is None and k == 0
                                        final = j == U - 1 and k == 1
                                        cs_ = slice(c * NB, (c + 1) * NB)
                                        last = mm3(psA[:, 2 * m + c], lhs, (dn_hi[:, k, cs_], dn_lo[:, k, cs_]),
                                                   first, final)
                            last.then_inc(dn_used.h, 1)

                        def body(j, i):
                            for h in range(2):
                                pe.wait_ge(gu_lo_ready.h, at(2 * (g0 + j) + h + 1, i, 4))
                                if h == 0 and j > 0:
                                    pe.wait_ge(up_sum.h, at(q[up_sum] + j, i, 2))
                                for k in range(h * HALF, (h + 1) * HALF):
                                    if pre and j == 0:
                                        pre.wait_turned(pe, k)
                                    for b in range(4):
                                        f = slice(b * P, (b + 1) * P)
                                        bank = (psG, psT)[b // 2][:, b % 2]

                                        whole, low = ((bank.rearrange("p (c s) -> p c s", c=2), gu_hi[:, k, f],
                                                       hT_both[:, :, k]), (bank[:, 0:S], gu_lo[:, k, f], hT_hi[:, k]))
                                        if k < K8 - 1:
                                            nc.tensor.matmul(*whole, start=k == 0, stop=False)
                                            last = nc.tensor.matmul(*low, start=False, stop=False)
                                        else:
                                            nc.tensor.matmul(*low, start=False, stop=False)
                                            last = nc.tensor.matmul(*whole, start=False, stop=True)
                                last.then_inc(gu_used.h, 1)
                            if j > 0:
                                down(j - 1, i)
                        turns(pe, body)
                        down(U - 1, None)

                    @block.scalar
                    def _(act):
                        start_act(act, stream, pre)
                        if weighted:
                            act.wait_ge(w_turned.h, q[w_turned] + 1)
                            nc.scalar.activation(wT[:], psA[0:U - 1, 0, 0:S], ACT.Copy).then_inc(w_copied.h, 1)

                        def body(j, i):
                            if j < U - 1:
                                stream.hi(act, j + 1, 0, i)
                            elif following(stream):
                                following(stream).hi(act, 0, 0)
                            act.wait_ge(gu_used.h, at(2 * (g0 + j) + 2, i, 4))
                            if j > 0:
                                act.wait_ge(h_ready.h, at(q[h_ready] + j, i, 2))
                            nc.scalar.activation(gl[:], psG[:, :, S:2 * S], ACT.Copy).then_inc(gate_low.h, 1)
                            nc.scalar.activation(ul[:], psT[:, :, S:2 * S], ACT.Copy).then_inc(up_low.h, 1)
                            act.wait_ge(gate_sum.h, at(q[gate_sum] + j + 1, i, 2))
                            nc.scalar.activation(sg[:], gl[:], ACT.Silu).then_inc(silu_ready.h, 1)
                            if weighted and j < U - 1:
                                if j == 0:
                                    act.wait_ge(w_stored.h, q[w_stored] + 16)
                                act.dma_start(wrow[:, (j + 1) % 2], w_dram[bass.ds(at(j, i, 2), 1)]
                                              .broadcast_to([P, S])).then_inc(w_landed[(j + 1) % 2].h, 16)
                            if j < U - 1:
                                stream.hi(act, j + 1, 1, i)
                            act.wait_ge(h_ready.h, at(q[h_ready] + j + 1, i, 2))
                            if d0 + j > 0:
                                act.wait_ge(dn_used.h, at(d0 + j, i, 2))
                            nc.scalar.activation(huh[:], hf[:], ACT.Copy).then_inc(hu_hi_ready.h, 1)
                            stream.dhi(act, j, i)
                        turns(act, body)

                    @block.vector
                    def _(dve):
                        start_dve(dve, stream, pre)

                        def body(j, i):
                            if j < U - 1:
                                stream.lo(dve, j + 1, 0, i)
                            elif following(stream):
                                following(stream).lo(dve, 0, 0)
                            if j > 0:
                                dve.wait_ge(hu_lo_ready.h, at(q[hu_lo_ready] + j, i, 2))
                            dve.wait_ge(gate_low.h, at(q[gate_low] + j + 1, i, 2))
                            nc.vector.tensor_tensor(gl[:], gl[:], psG[:, :, 0:S], ALU.add).then_inc(gate_sum.h, 1)
                            dve.wait_ge(up_low.h, at(q[up_low] + j + 1, i, 2))
                            nc.vector.tensor_tensor(ul[:], ul[:], psT[:, :, 0:S], ALU.add).then_inc(up_sum.h, 1)
                            dve.wait_ge(up_sum.h, at(q[up_sum] + j + 1, i, 2))
                            dve.wait_ge(silu_ready.h, at(q[silu_ready] + j + 1, i, 2))
                            ins = nc.vector.tensor_tensor(hf[:], sg[:], ul[:], ALU.mult)
                            if weighted and j > 0:
                                ins.then_inc(up_ready.h, 1)
                                dve.wait_ge(up_ready.h, at(q[up_ready] + j, i, 2))
                                dve.wait_ge(w_landed[j % 2].h, at(q[w_landed[j % 2]] + 16 * ((j + 1) // 2), i, 16))
                                ins = nc.vector.tensor_tensor(hf[:], hf[:], wrow[:, j % 2].unsqueeze(1)
                                                              .broadcast_to([P, 2, S]), ALU.mult)
                            ins.then_inc(h_ready.h, 1)
                            if j < U - 1:
                                stream.lo(dve, j + 1, 1, i)
                            dve.wait_ge(hu_hi_ready.h, at(q[hu_hi_ready] + j + 1, i, 2))
                            nc.vector.tensor_tensor(hul[:], hf[:], huh[:].bitcast(F32), ALU.subtract) \
                                .then_inc(hu_lo_ready.h, 1)
                            stream.dlo(dve, j, i)
                        turns(dve, body)
            for s in (gate_low, gate_sum, up_low, up_sum, h_ready, silu_ready, hu_hi_ready, hu_lo_ready):
                s.n += U
            if weighted:
                up_ready.n += U - 1
                w_turned.n += 1
                w_copied.n += 1
                w_stored.n += 16
                for s in w_landed:
                    s.n += 16 * ((U - 1) // 2)

        x_landed, vec_landed = sem("x_landed"), sem("vec_landed")
        const_ready, vec_turned, vec_ready = sem("const_ready"), sem("vec_turned"), sem("vec_ready")

        def rows(ap):
            return ap.rearrange("(r p) -> r p", p=P)

        B_MIX, B_FFN, B_KV, B_BS, B_SUB = 0, 16, 32, 40, 48
        with ExitStack() as ctx:
            stage = sb(ctx, "vec_rows", [P, 3, P])
            with nc.Block() as block:
                @block.sync
                def _(sp):
                    sp.dma_start(x[:], a["x"][0].rearrange("(m p) d -> p m d", p=P)).then_inc(x_landed.h, 16)
                    vecs = [(0, 0, a["ada_b"].rearrange("l (r p) -> (l r) p", p=P)), (0, COL_KVB, rows(a["kv_ada_b"])),
                            (0, COL_C, rows(a["c"][0])),
                            (1, B_MIX, a["norm_mix"].rearrange("l (r p) -> (l r) p", p=P)),
                            (1, B_FFN, a["norm_ffn"].rearrange("l (r p) -> (l r) p", p=P)),
                            (1, B_KV, rows(a["kv_norm"])), (1, B_BS, a["a_b_s"][0]), (1, B_SUB, a["a_subln_2"]),
                            (2, 0, a["norm_gains_2"].rearrange("l g (r p) -> (l g r) p", p=P))]
                    sp.wait_ge(const_ready.h, 1)
                    for t, r, src in vecs:
                        sp.dma_start(stage[r:r + src.shape[0], t], src).then_inc(vec_landed.h, 16)
                    vec_landed.n = 16 * len(vecs)
                    sp.wait_ge(x_landed.h, 16)

                @block.gpsimd
                def _(pool):
                    step = Chain(pool, pool_step)
                    nc.gpsimd.memset(stage[:], 0.0).then_inc(const_ready.h, 1)
                    nc.gpsimd.memset(consts[:, 0:1], RMS_EPS)
                    nc.gpsimd.memset(consts[:, 1:2], LN_EPS)
                    step(nc.gpsimd.memset(ones[:], 1.0))
                    step(nc.gpsimd.memset(ident[:], 0.0))
                    nc.gpsimd.affine_select(out=ident[:], in_=ident[:], compare_op=ALU.not_equal, fill=1.0, base=0,
                                            pattern=[[-1, P]], channel_multiplier=1).then_inc(const_ready.h, 1)

                @block.tensor
                def _(pe):
                    pe.wait_ge(const_ready.h, 2)
                    pe.wait_ge(vec_landed.h, vec_landed.n)
                    for t in range(3):
                        last = nc.tensor.transpose(psT[:, 0, t * P:(t + 1) * P], stage[:, t], ident[:])
                    last.then_inc(vec_turned.h, 1)

                @block.vector
                def _(dve):
                    step = Chain(dve, dve_step)
                    dve.wait_ge(vec_turned.h, 1)
                    for t, dst in enumerate((featA, featB, featC)):
                        step(nc.vector.tensor_copy(dst[:], psT[:, 0, t * P:(t + 1) * P]))
                    nc.vector.tensor_copy(featA[:], featA[:]).then_inc(vec_ready.h, 1)

                @block.scalar
                def _(act):
                    act.wait_ge(vec_ready.h, 1)
                    nc.scalar.activation(cs[:], featA[:, COL_C:COL_C + K8], ACT.Silu)

        ada_landed = [sem(f"ada_landed_{s}") for s in range(4)]
        side_landed = [sem("side_landed_0"), sem("side_landed_1")]
        ada_used, ada_mm, gate_out = sem("ada_used"), sem("ada_mm"), sem("gate_out")
        gate_landed = sem("gate_landed")
        AC = 256

        def ada_view(w):
            return w.rearrange("(k p) n -> p k n", p=P)

        def ada_now(w, n, row, ring, brow, bias_landed):
            wv = ada_view(w)
            R = len(ada_landed)
            assert n % R == 0
            with nc.Block() as block:
                @block.sync
                def _(sp):
                    for s in range(R):
                        sp.dma_start(ring[:, s], wv[:, :, s * AC:(s + 1) * AC]).then_inc(ada_landed[s].h, 16)
                    with sp.Fori(0, n // R - 1) as i:
                        for s in range(R):
                            sp.wait_ge(ada_used.h, at(s + 1, i, R))
                            sp.dma_start(ring[:, s], wv[:, :, bass.ds(i * (R * AC) + (R + s) * AC, AC)]) \
                                .then_inc(ada_landed[s].h, 16)
                    s_in.first_loads(sp)
                    sp.dma_start(brow[:], a["a_b_in"].broadcast_to([P, 2 * AW])).then_inc(bias_landed.h, 16)

                @block.vector
                def _(dve):
                    step0 = dve_step.n
                    with dve.Fori(0, n // R) as i:
                        step = Chain(dve, dve_step)
                        step.i, step.step = i, R * (K8 - 1)
                        for s in range(R):
                            dve.wait_ge(ada_landed[s].h, at(16, i, 16))
                            dst = row[:, bass.ds(i * (R * AC) + s * AC, AC)]
                            for k in range(K8):
                                if k == 0:
                                    ins = nc.vector.tensor_scalar(dst, ring[:, s, k], cs[:, k:k + 1], None, ALU.mult)
                                else:
                                    ins = nc.vector.scalar_tensor_tensor(dst, ring[:, s, k], cs[:, k:k + 1], dst,
                                                                         ALU.mult, ALU.add)
                                if k < K8 - 1:
                                    step(ins)
                                else:
                                    ins.then_inc(ada_used.h, 1)
                    dve_step.n = step0 + (K8 - 1) * n

        def ada_beside(pool, w, first, n, row, ring):
            wv = ada_view(w)
            step0 = pool_step.n
            l0 = [s.n for s in side_landed]

            def load(s, col):
                pool.dma_start(ring(s), wv[:, :, col]).then_inc(side_landed[s].h, 16)
            for s in range(2):
                load(s, slice((first + s) * AC, (first + s + 1) * AC))

            def piece(s, i, more):
                step = Chain(pool, pool_step)
                if i is not None:
                    step.i, step.step = i, 8
                r = ring(s)
                pool.wait_ge(side_landed[s].h, at(l0[s] + 16, i, 16))
                step(nc.gpsimd.tensor_tensor(r, r, cs[:].unsqueeze(2).broadcast_to([P, K8, AC]), ALU.mult))
                step(nc.gpsimd.tensor_tensor(r[:, 0:4], r[:, 0:4], r[:, 4:8], ALU.add))
                step(nc.gpsimd.tensor_tensor(r[:, 0:2], r[:, 0:2], r[:, 2:4], ALU.add))
                base = 0 if i is None else i * (2 * AC)
                step(nc.gpsimd.tensor_tensor(row[:, bass.ds(base + s * AC, AC)], r[:, 0], r[:, 1], ALU.add))
                if more:
                    load(s, bass.ds(base + (first + 2 + s) * AC, AC))
            with pool.Fori(0, n // 2 - 1) as i:
                for s in range(2):
                    piece(s, i, True)
            pool_step.n = step0 + 4 * (n - 2)
            for s in range(2):
                l0[s] += 16 * (n // 2 - 1)
            last = row[:, (n - 2) * AC:n * AC]
            for s in range(2):
                step = Chain(pool, pool_step)
                r = ring(s)
                pool.wait_ge(side_landed[s].h, l0[s] + 16)
                step(nc.gpsimd.tensor_tensor(r, r, cs[:].unsqueeze(2).broadcast_to([P, K8, AC]), ALU.mult))
                step(nc.gpsimd.tensor_tensor(r[:, 0:4], r[:, 0:4], r[:, 4:8], ALU.add))
                step(nc.gpsimd.tensor_tensor(r[:, 0:2], r[:, 0:2], r[:, 2:4], ALU.add))
                step(nc.gpsimd.tensor_tensor(last[:, s * AC:(s + 1) * AC], r[:, 0], r[:, 1], ALU.add))
            for s in range(2):
                side_landed[s].n += 16 * (n // 2)

        def ada_finish(row, bias_col, mods_col, gates_at=None, layer=0, wait_sp=None):
            nt = row.shape[1] // P
            of_gates = [t for o in (gates_at or {}).values() for t in range(o // P, o // P + K8)]
            wanted = [t for t in range(nt) if t not in of_gates]
            runs = [(t, t + K8) for t in wanted if t % K8 == 0]
            with nc.Block() as block:
                @block.sync
                def _(sp):
                    if wait_sp:
                        wait_sp(sp)
                    if gates_at:
                        for k in gates_at:
                            sp.dma_start(gates[:, k], a["ada_b"][layer:layer + 1, (2 + 3 * k) * D:(3 + 3 * k) * D]
                                         .broadcast_to([P, D])).then_inc(gate_landed.h, 16)

                @block.tensor
                def _(pe):
                    for t in wanted:
                        last = nc.tensor.matmul(psT[:, 0, t:t + 1], row[:, t * P:(t + 1) * P], ones[:, 0:1],
                                                start=True, stop=True)
                    if wanted:
                        last.then_inc(ada_mm.h, 1)
                    if gates_at:
                        for j, k in enumerate(gates_at):
                            if j:
                                pe.wait_ge(gate_out.h, gate_out.n + j)
                            for c in range(2):
                                o = gates_at[k] + c * NB
                                last = nc.tensor.matmul(psG[:, c], ones[:], row[:, o:o + NB], start=True, stop=True)
                            last.then_inc(ada_mm.h, 1)

                @block.vector
                def _(dve):
                    if wanted:
                        dve.wait_ge(ada_mm.h, ada_mm.n + 1)
                    for t0, t1 in runs:
                        nc.vector.tensor_tensor(mods[:, mods_col + t0:mods_col + t1], psT[:, 0, t0:t1],
                                                featA[:, bias_col + t0:bias_col + t1], ALU.add)
                    if gates_at:
                        dve.wait_ge(gate_landed.h, gate_landed.n + 16 * len(gates_at))
                        for j, k in enumerate(gates_at):
                            dve.wait_ge(ada_mm.h, ada_mm.n + bool(wanted) + 1 + j)
                            nc.vector.tensor_tensor(as_banks(gates[:, k]), psG[:], as_banks(gates[:, k]),
                                                    ALU.add).then_inc(gate_out.h, 1)
            ada_mm.n += bool(wanted)
            if gates_at:
                gate_landed.n += 16 * len(gates_at)
                gate_out.n += len(gates_at)
                ada_mm.n += len(gates_at)

        def finish():
            stored = sem("stored")
            with nc.Block() as block:
                @block.sync
                def _(sp):
                    sp.dma_start(out[0].rearrange("(m p) d -> p m d", p=P), x[:]).then_inc(stored.h, 16)
                    sp.wait_ge(stored.h, 16)

        bias_landed, ws_masked = sem("bias_landed"), sem("ws_masked")
        zg, v_ready, ws_turned, ws_ready = sem("gelu_done"), sem("v_ready"), sem("ws_turned"), sem("ws_ready")
        sv_ready, y_ready, mu_ready = sem("sv_ready"), sem("y_ready"), sem("mu_ready")
        with ExitStack() as ctx:
            z = sb(ctx, "z", [P, M, 2 * AW])
            with ExitStack() as ctx2:
                brow = sb(ctx2, "b_in", [P, 2 * AW])
                row = sb(ctx2, "ada_row", [P, 2 * D])
                ada_now(a["ada_w"][0], 2 * D // AC, row,
                        z[:].rearrange("p m (s k n) -> p (m s) k n", k=K8, n=AC), brow, bias_landed)
                ada_finish(row, 0, 0, wait_sp=lambda sp: sp.wait_ge(bias_landed.h, 16))

                def evac_z(c, i, bank):
                    for m in range(M):
                        o = at(c, i, 2) * NB
                        yield nc.vector.tensor_tensor(z[:, m, bass.ds(o, NB)], psA[:, bank + m],
                                                      brow[:, bass.ds(o, NB)], ALU.add)
                pre = Pre(ctx2)
                pre.modulate(B_MIX, 0, 8)
                project(s_in, hT, evac_dve=evac_z, pre=pre, beside=lambda pool: ada_beside(
                    pool, a["ada_w"][0], 3 * D // AC, 2 * D // AC, row,
                    lambda s: dn_raw[:, s].rearrange("p a (b n) -> p (a b) n", n=AC)))
                ada_finish(row, 24, 24)
            with ExitStack() as ctx2:
                lng = sb(ctx2, "ln_g", [P, AW])
                lnb = sb(ctx2, "ln_b", [P, AW])
                ws = sb(ctx2, "w_s", [P, NG, P])
                wsT = sb(ctx2, "w_sT", [P, NG, P])
                st = sb(ctx2, "ln_stats", [P, 4, M])
                sink = sb(ctx2, "ln_sink", [P, AW])
                with nc.Block() as block:
                    @block.sync
                    def _(sp):
                        sp.dma_start(ws[:], a["a_w_s"][0].rearrange("g t s -> t g s")).then_inc(bias_landed.h, 16)
                        sp.wait_ge(bias_landed.h, 32)
                        sp.dma_start(lng[:], a["a_ln_g"].broadcast_to([P, AW])).then_inc(bias_landed.h, 16)
                        sp.dma_start(lnb[:], a["a_ln_b"].broadcast_to([P, AW])).then_inc(bias_landed.h, 16)

                    @block.gpsimd
                    def _(pool):
                        pool.wait_ge(bias_landed.h, 32)
                        nc.gpsimd.affine_select(out=ws[:], in_=ws[:], compare_op=ALU.is_ge, fill=0.0, base=0,
                                                pattern=[[0, NG], [-1, P]], channel_multiplier=1) \
                            .then_inc(ws_masked.h, 1)
                        pool.wait_ge(mu_ready.h, 2)
                        nc.gpsimd.tensor_scalar(st[:, 1], st[:, 0], -1.0 / AW, None, ALU.mult) \
                            .then_inc(mu_ready.h, 1)

                    @block.scalar
                    def _(act):
                        for m in range(M):
                            nc.scalar.activation(z[:, m, AW:], z[:, m, AW:], ACT.Gelu_apprx_tanh,
                                                 accum_out=st[:, 0, m:m + 1]).then_inc(mu_ready.h, 1)
                        act.wait_ge(mu_ready.h, 3)
                        for m in range(M):
                            nc.scalar.activation(sink[:], z[:, m, AW:], ACT.Square, bias=st[:, 1, m:m + 1],
                                                 accum_out=st[:, 2, m:m + 1]).then_inc(mu_ready.h, 1)
                            act.wait_ge(mu_ready.h, m + 4)
                        nc.scalar.activation(st[:, 3], st[:, 2], ACT.Sqrt, scale=1.0 / AW, bias=eps_of[LN_EPS]) \
                            .then_inc(mu_ready.h, 1)
                        for m in range(M):
                            nc.scalar.activation(z[:, m, 0:AW], z[:, m, 0:AW], ACT.Gelu_apprx_tanh).then_inc(zg.h, 1)

                    @block.tensor
                    def _(pe):
                        pe.wait_ge(ws_masked.h, 1)
                        for g in range(NG):
                            last = nc.tensor.transpose(psT[:, g // 4, (g % 4) * P:(g % 4 + 1) * P], ws[:, g], ident[:])
                        last.then_inc(ws_turned.h, 1)
                        pe.wait_ge(ws_ready.h, 1)
                        W = AW // NG
                        for m in range(M):
                            pe.wait_ge(v_ready.h, m + 1)
                            for g in range(NG):
                                r = m * NG + g
                                if r >= 8 and r % 2 == 0:
                                    pe.wait_ge(y_ready.h, r - 6)
                                last = nc.tensor.matmul(psA[:, (r // 2) % 4, (r % 2) * W:(r % 2 + 1) * W], wsT[:, g],
                                                        z[:, m, AW + g * W:AW + (g + 1) * W], start=True, stop=True)
                                if r % 2:
                                    last.then_inc(sv_ready.h, 1)

                    @block.vector
                    def _(dve):
                        step = Chain(dve, dve_step)
                        dve.wait_ge(ws_turned.h, 1)
                        nc.vector.tensor_copy(wsT[:].rearrange("p (b g) t -> p b (g t)", b=2), psT[:]) \
                            .then_inc(ws_ready.h, 1)
                        dve.wait_ge(bias_landed.h, 64)
                        dve.wait_ge(mu_ready.h, 6)
                        step(nc.vector.reciprocal(st[:, 2], st[:, 3]))
                        for m in range(M):
                            v = z[:, m, AW:]
                            step(nc.vector.tensor_scalar(v, v, st[:, 1, m:m + 1], st[:, 2, m:m + 1], ALU.add, ALU.mult))
                            step(nc.vector.tensor_tensor(v, v, lng[:], ALU.mult))
                            nc.vector.tensor_tensor(v, v, lnb[:], ALU.add).then_inc(v_ready.h, 1)
                        W = AW // NG
                        dve.wait_ge(zg.h, 2)
                        for m in range(M):
                            for g in range(NG):
                                r = m * NG + g
                                dve.wait_ge(sv_ready.h, r // 2 + 1)
                                u = z[:, m, g * W:(g + 1) * W]
                                nc.vector.scalar_tensor_tensor(u, psA[:, (r // 2) % 4, (r % 2) * W:(r % 2 + 1) * W],
                                                               featB[:, B_BS + g:B_BS + g + 1], u, ALU.add, ALU.mult) \
                                    .then_inc(y_ready.h, 1)
            yT_hi = sb(ctx, "yT_hi", [P, AW // P, S], F32R)
            yT_lo = sb(ctx, "yT_lo", [P, AW // P, S], F32R)
            ring = z[:, :, AW:AW + K8 * AC].rearrange("p s (k n) -> p s k n", n=AC)
            g1_row = gates[:, 1]
            pre = Pre(ctx)
            pre.turn(lambda m, k: z[:, m, k * P:(k + 1) * P], AW // P, yT_hi, yT_lo)
            project(s_out, lambda m, k: (yT_hi[:, k, m * P:(m + 1) * P], yT_lo[:, k, m * P:(m + 1) * P]),
                    deep=AW // D, keep=True, pre=pre, beside=lambda pool: ada_beside(
                        pool, a["ada_w"][0], 2 * D // AC, D // AC, g1_row,
                        lambda s: ring[:, s]))
            ada_finish(g1_row, 16, 16, {0: 0}, 0)

        def add_alone(add):
            with ExitStack() as ctx:
                pre = Pre(ctx)
                add(pre)
                pre.alone()

        if stop == "gmlp":
            add_alone(lambda pre: pre.add_gated(0))
        if stop == "gmlp":
            return finish()

        router_landed, router_mm, router_sig = sem("router_landed"), sem("router_mm"), sem("router_sig")
        weights_dram = [nc.dram_tensor(f"token_weights_{layer}", [E, S], F32, kind="Internal").ap()
                        for layer in range(2)]
        G8 = 8
        GE = E // G8

        def moe(layer):
            with ExitStack() as ctx:
                hf = sb(ctx, "hT_full", [P, K8, S])
                with ExitStack() as ctx2:
                    pre = Pre(ctx2)
                    pre.add_gated(0)
                    pre.modulate(B_FFN + 8 * layer, 48 * layer + 24, 48 * layer + 32, hf)
                    pre.alone()
                wr = sb(ctx, "w_router", [P, K8, E])
                eb = sb(ctx, "e_bias", [P, E])
                sc = sb(ctx, "scores", [P, M, E])
                ch = sb(ctx, "choice", [P, M, E])
                ch2 = sb(ctx, "choice_cut", [P, M, E])
                t8 = sb(ctx, "group_top", [P, M, G8, 8])
                gs = sb(ctx, "group_score", [P, M, G8])
                c1 = sb(ctx, "better", [P, M, G8, G8])
                c2 = sb(ctx, "equal_before", [P, M, G8, G8])
                tri = sb(ctx, "before", [P, G8, G8])
                rk = sb(ctx, "group_rank", [P, M, G8])
                em = sb(ctx, "group_mask", [P, M, G8])
                sm = sb(ctx, "weight_sum", [P, M])
                with nc.Block() as block:
                    @block.sync
                    def _(sp):
                        sp.dma_start(wr[:], a["moe_router"][layer].rearrange("(k p) e -> p k e", p=P)) \
                            .then_inc(router_landed.h, 16)
                        sp.dma_start(eb[:], a["moe_bias"][layer:layer + 1].broadcast_to([P, E])) \
                            .then_inc(router_landed.h, 16)

                    @block.gpsimd
                    def _(pool):
                        step = Chain(pool, pool_step)
                        step(nc.gpsimd.memset(tri[:], 1.0))
                        step(nc.gpsimd.affine_select(out=tri[:], in_=tri[:], compare_op=ALU.is_gt, fill=0.0, base=0,
                                                     pattern=[[1, G8], [-1, G8]], channel_multiplier=0))

                    @block.tensor
                    def _(pe):
                        pe.wait_ge(router_landed.h, router_landed.n + 32)
                        for m in range(M):
                            for k in range(K8):
                                last = nc.tensor.matmul(psT[:, m, 0:E], hf[:, k, m * P:(m + 1) * P], wr[:, k],
                                                        start=k == 0, stop=k == K8 - 1)
                        last.then_inc(router_mm.h, 1)

                    @block.scalar
                    def _(act):
                        act.wait_ge(router_mm.h, router_mm.n + 1)
                        nc.scalar.activation(sc[:], psT[:, :, 0:E], ACT.Sigmoid).then_inc(router_sig.h, 1)

                    pool_steps = pool_step.n

                    @block.vector
                    def _(dve):
                        step = Chain(dve, dve_step)
                        dve.wait_ge(router_sig.h, router_sig.n + 1)
                        dve.wait_ge(pool_step.h, pool_steps)
                        def both(op):
                            for m in range(M):
                                ins = op(m)
                            step(ins)
                        groups = [ch[:, m].rearrange("p (g e) -> p g e", g=G8) for m in range(M)]
                        other = [gs[:, m].unsqueeze(1).broadcast_to([P, G8, G8]) for m in range(M)]
                        own = [gs[:, m].unsqueeze(2).broadcast_to([P, G8, G8]) for m in range(M)]
                        v = nc.vector
                        both(lambda m: v.tensor_tensor(ch[:, m], sc[:, m], eb[:], ALU.add))
                        for g in range(G8 - 1):
                            for m in range(M):
                                v.max(t8[:, m, g], ch[:, m, g * GE:(g + 1) * GE])
                        both(lambda m: v.max(t8[:, m, G8 - 1], ch[:, m, (G8 - 1) * GE:]))
                        step(v.tensor_tensor(gs[:], t8[:, :, :, 0], t8[:, :, :, 1], ALU.add))
                        for m in range(M):
                            v.tensor_tensor(c1[:, m], other[m], own[m], ALU.is_gt)
                        both(lambda m: v.tensor_tensor(c2[:, m], other[m], own[m], ALU.is_equal))
                        both(lambda m: v.tensor_tensor(c2[:, m], c2[:, m], tri[:], ALU.mult))
                        both(lambda m: v.tensor_tensor(c1[:, m], c1[:, m], c2[:, m], ALU.add))
                        step(v.reduce_sum(rk[:], c1[:], AX))
                        step(v.tensor_scalar(em[:], rk[:], 4.0, None, ALU.is_lt))
                        v.tensor_scalar(rk[:], em[:], -1.0, -NEG, ALU.add, ALU.mult)
                        both(lambda m: v.tensor_tensor(groups[m], groups[m],
                                                       em[:, m].unsqueeze(2).broadcast_to([P, G8, GE]), ALU.mult))
                        both(lambda m: v.tensor_tensor(groups[m], groups[m],
                                                       rk[:, m].unsqueeze(2).broadcast_to([P, G8, GE]), ALU.add))
                        both(lambda m: v.max(t8[:, m, 0], ch[:, m]))
                        both(lambda m: v.match_replace(ch2[:, m], t8[:, m, 0], ch[:, m], 4 * NEG))
                        both(lambda m: v.tensor_tensor(ch2[:, m], ch2[:, m], ch[:, m], ALU.not_equal))
                        both(lambda m: v.tensor_tensor(ch2[:, m], ch2[:, m], sc[:, m], ALU.mult))
                        step(nc.vector.reduce_sum(sm[:], ch2[:], AX))
                        step(nc.vector.reciprocal(sm[:], sm[:]))
                        for m in range(M):
                            step(nc.vector.tensor_scalar(gateval[:, m], ch2[:, m], sm[:, m:m + 1],
                                                         ROUTED_SCALE, ALU.mult, ALU.mult))
                router_landed.n += 32
                router_mm.n += 1
                router_sig.n += 1
            if layer == 0:
                with ExitStack() as ctx:
                    rows_ = [sb(ctx, "ada_row", [P, 6 * D]), sb(ctx, "ada_row", [P, 2 * D])]
                    row_g2 = sb(ctx, "ada_row", [P, D])
                    ring = sb(ctx, "ada_ring", [P, 2, K8, AC])

                    def beside(pool):
                        ada_beside(pool, a["ada_w"][0], 5 * D // AC, D // AC, row_g2, lambda s: ring[:, s])
                        ada_beside(pool, a["ada_w"][1], 0, 6 * D // AC, rows_[0], lambda s: ring[:, s])
                        ada_beside(pool, a["kv_ada_w"], 0, 2 * D // AC, rows_[1], lambda s: ring[:, s])
                    gated_units(s_moe[layer], gateval, weights_dram[layer], beside)
                    ada_finish(row_g2, 40, 40, {1: 0}, 0)
                    add_alone(lambda pre: pre.add_gated(1))
                    ada_finish(rows_[0], 48, 48, {0: 2 * D, 1: 5 * D}, 1)
                    ada_finish(rows_[1], COL_KVB, 96)
            else:
                gated_units(s_moe[layer], gateval, weights_dram[layer])
                add_alone(lambda pre: pre.add_gated(1))

        moe(0)
        if stop == "moe0":
            return finish()

        masks_ready = sem("masks_ready")

        def make_masks(ctx, window):
            mk = sb(ctx, "mask", [P, 2 * P])

            def pool_part(pool):
                step = Chain(pool, pool_step)
                step(nc.gpsimd.memset(mk[:], 0.0))
                if window:
                    step(nc.gpsimd.affine_select(out=mk[:, 0:P], in_=mk[:, 0:P], compare_op=ALU.is_gt, fill=NEG,
                                                 base=0, pattern=[[1, P]], channel_multiplier=-1))
                nc.gpsimd.affine_select(out=mk[:, P:2 * P], in_=mk[:, P:2 * P], compare_op=ALU.is_ge, fill=NEG, base=0,
                                        pattern=[[-1, P]], channel_multiplier=1).then_inc(masks_ready.h, 1)
            return mk, pool_part

        qk_turned, qk_copied = sem("qk_turned"), sem("qk_copied")

        def heads_to_feature(pairs):
            n0 = qk_copied.n
            R = len(pairs) // 2

            def pe_part(pe):
                for r in range(R):
                    if r >= 2:
                        pe.wait_ge(qk_copied.h, n0 + r - 1)
                    for k in range(2):
                        for m in range(M):
                            last = nc.tensor.transpose(psT[:, r % 2, k * S + m * P:k * S + (m + 1) * P],
                                                       pairs[2 * r + k][1](m), ident[:])
                    last.then_inc(qk_turned.h, 1)

            def act_part(act):
                for r in range(R):
                    act.wait_ge(qk_turned.h, n0 + r + 1)
                    for k in range(2):
                        ins = nc.scalar.activation(pairs[2 * r + k][0], psT[:, r % 2, k * S:(k + 1) * S], ACT.Copy)
                    ins.then_inc(qk_copied.h, 1)
            qk_copied.n += R
            return pe_part, act_part

        sq_ready = sem("out_square_ready")
        scores_ready, s_taken, bias_ready, p_ready = (sem(n) for n in
                                                      ("scores_ready", "scores_taken", "bias_ready", "probs_ready"))
        w_ready, p_turned, p_copied, o_ready, o_taken = (sem(n) for n in
                                                         ("weights_ready", "probs_turned", "probs_copied",
                                                          "o_ready", "o_taken"))

        def softmax_attention(qT, kT, v, o, mask, window=False, lam=None, sink=None, vw=HD, squares=None):
            items = [(t, m) for t in range(K8) for m in range(M)]
            q = {s: s.n for s in (scores_ready, s_taken, bias_ready, p_ready, w_ready, p_turned, p_copied,
                                  o_ready, o_taken)}
            nh = 1 if lam is not None else 2
            banks = (psG[:, 0:2], psA[:, 2:4])
            with ExitStack() as ctx:
                sm = sb(ctx, "scores_m", [P, 2, 2, 2 * P])
                pr = sb(ctx, "probs", [P, 2, 2, 2 * P])
                pT = sb(ctx, "probsT", [P, 2, 4, P])
                mx = sb(ctx, "row_max", [P, 2, 2])
                nm = sb(ctx, "neg_max", [P, 2, 2])
                su = sb(ctx, "row_sum", [P, 2, 2])
                rc = sb(ctx, "row_rec", [P, 2, 2])
                es = sb(ctx, "sink_term", [P, 2, 2])
                with nc.Block() as block:
                    @block.tensor
                    def _(pe):
                        def scores(n):
                            t, m = items[n]
                            b, L = n % 2, (m + 1) * P
                            if n >= 2:
                                pe.wait_ge(s_taken.h, q[s_taken] + n - 1)
                            for c in range(2):
                                r = slice(HD * c, HD * (c + 1))
                                last = nc.tensor.matmul(banks[b][:, c, 0:L], qT[r, t, m * P:(m + 1) * P],
                                                        kT(t)[r, 0:L], start=True, stop=True)
                            last.then_inc(scores_ready.h, 1)

                        def turn(n):
                            t, m = items[n]
                            b = n % 2
                            pe.wait_ge((w_ready if lam is not None else p_ready).h,
                                       q[w_ready] + n + 1 if lam is not None else q[p_ready] + 2 * n + 2)
                            for c in range(nh):
                                for j in range(m + 1):
                                    last = nc.tensor.transpose(psT[:, b, (2 * c + j) * P:(2 * c + j + 1) * P],
                                                               pr[:, b, c, j * P:(j + 1) * P], ident[:])
                            last.then_inc(p_turned.h, 1)

                        def values(n):
                            t, m = items[n]
                            b = n % 2
                            pe.wait_ge(p_copied.h, q[p_copied] + n + 1)
                            if n >= 2:
                                pe.wait_ge(o_taken.h, q[o_taken] + n - 1)
                            for c in range(nh):
                                for j in range(m + 1):
                                    last = nc.tensor.matmul(psA[:, b, c * vw:(c + 1) * vw], pT[:, b, 2 * c + j],
                                                            v(t, c, j), start=j == 0, stop=j == m)
                            last.then_inc(o_ready.h, 1)
                        N = len(items)
                        scores(0)
                        for n in range(N + 2):
                            if n + 1 < N:
                                scores(n + 1)
                            if n >= 2:
                                values(n - 2)
                            if 1 <= n <= N:
                                turn(n - 1)

                    @block.vector
                    def _(dve):
                        def mark(ins):
                            dve_step.n += 1
                            ins.then_inc(dve_step.h, 1)
                            return dve_step.n

                        def after(count):
                            dve.wait_ge(dve_step.h, count)

                        def masked(n):
                            t, m = items[n]
                            b, L = n % 2, (m + 1) * P
                            dve.wait_ge(scores_ready.h, q[scores_ready] + n + 1)
                            if n >= 2:
                                dve.wait_ge(p_ready.h, q[p_ready] + 2 * (n - 1))
                            mk = mask[:, 2 * P - L:].unsqueeze(1).broadcast_to([P, 2, L])
                            nc.vector.tensor_tensor(sm[:, b, :, 0:L], banks[b][:, :, 0:L], mk, ALU.add) \
                                .then_inc(s_taken.h, 1)

                        def maximum(n):
                            b, L = n % 2, (items[n][1] + 1) * P
                            dve.wait_ge(s_taken.h, q[s_taken] + n + 1)
                            return mark(nc.vector.reduce_max(mx[:, b], sm[:, b, :, 0:L], AX))

                        def bias(n, done):
                            t, b = items[n][0], n % 2
                            after(done)
                            if sink is None:
                                nc.vector.tensor_scalar(nm[:, b], mx[:, b], -ATT_SCALE, None, ALU.mult) \
                                    .then_inc(bias_ready.h, 1)
                                return
                            after(mark(nc.vector.scalar_tensor_tensor(mx[:, b], mx[:, b], ATT_SCALE,
                                                                      sink[:, 2 * t:2 * t + 2], ALU.mult, ALU.max)))
                            nc.vector.tensor_tensor(es[:, b], sink[:, 2 * t:2 * t + 2], mx[:, b], ALU.subtract)
                            nc.vector.tensor_scalar(nm[:, b], mx[:, b], -1.0, None, ALU.mult).then_inc(bias_ready.h, 1)

                        def total(n):
                            b = n % 2
                            dve.wait_ge(p_ready.h, q[p_ready] + 2 * n + 2)
                            if n >= 2:
                                dve.wait_ge(o_taken.h, q[o_taken] + n - 1)
                            if sink is not None:
                                after(mark(nc.vector.tensor_tensor(su[:, b], su[:, b], es[:, b], ALU.add)))
                            return mark(nc.vector.reciprocal(rc[:, b], su[:, b]))

                        def times_lambda(n, done):
                            b = n % 2
                            after(done)
                            return mark(nc.vector.tensor_tensor(rc[:, b, 1:2], rc[:, b, 1:2], lam, ALU.mult))

                        def first_weights(n):
                            b, L = n % 2, (items[n][1] + 1) * P
                            return mark(nc.vector.tensor_scalar(pr[:, b, 0, 0:L], pr[:, b, 0, 0:L], rc[:, b, 0:1], None,
                                                                ALU.mult))

                        def both_weights(n, done):
                            b, L = n % 2, (items[n][1] + 1) * P
                            after(done)
                            nc.vector.scalar_tensor_tensor(pr[:, b, 0, 0:L], pr[:, b, 1, 0:L], rc[:, b, 1:2],
                                                           pr[:, b, 0, 0:L], ALU.mult, ALU.add).then_inc(w_ready.h, 1)

                        reciprocal_done = {}

                        def back(n):
                            t, m = items[n]
                            b = n % 2
                            after(reciprocal_done[n])
                            dve.wait_ge(o_ready.h, q[o_ready] + n + 1)
                            w = nh * vw
                            dst = o[:, m, t * w:(t + 1) * w]
                            if lam is not None:
                                nc.vector.tensor_copy(dst, psA[:, b, 0:w]).then_inc(o_taken.h, 1)
                            else:
                                r = rc[:, b].unsqueeze(2).broadcast_to([P, 2, vw])
                                nc.vector.tensor_tensor(dst.rearrange("p (c e) -> p c e", c=2),
                                                        psA[:, b, 0:w].rearrange("p (c e) -> p c e", c=2), r,
                                                        ALU.mult).then_inc(o_taken.h, 1)
                        N = len(items)
                        for n in range(N + 2):
                            if n < N:
                                masked(n)
                            if 1 <= n <= N:
                                done = reciprocal_done[n - 1] = total(n - 1)
                            if n < N:
                                max_done = maximum(n)
                            if lam is not None and 1 <= n <= N:
                                done = times_lambda(n - 1, done)
                                weights_done = first_weights(n - 1)
                            if n < N:
                                bias(n, max_done)
                            if lam is not None and 1 <= n <= N:
                                after(done)
                                both_weights(n - 1, weights_done)
                            if n >= 2:
                                back(n - 2)

                    @block.scalar
                    def _(act):
                        def exps(n):
                            t, m = items[n]
                            b, L = n % 2, (m + 1) * P
                            act.wait_ge(bias_ready.h, q[bias_ready] + n + 1)
                            if n >= 2:
                                act.wait_ge(p_turned.h, q[p_turned] + n - 1)
                            for c in range(2):
                                nc.scalar.activation(pr[:, b, c, 0:L], sm[:, b, c, 0:L], ACT.Exp,
                                                     bias=nm[:, b, c:c + 1], scale=ATT_SCALE,
                                                     accum_out=su[:, b, c:c + 1]).then_inc(p_ready.h, 1)

                        def copy(n):
                            t, m = items[n]
                            b = n % 2
                            act.wait_ge(p_turned.h, q[p_turned] + n + 1)
                            if n >= 2:
                                act.wait_ge(o_ready.h, q[o_ready] + n - 1)
                            src = psT[:, b].rearrange("p (c j k) -> p c j k", c=2, j=2)[:, 0:nh, 0:m + 1]
                            dst = pT[:, b].rearrange("p (c j) k -> p c j k", c=2)[:, 0:nh, 0:m + 1]
                            nc.scalar.activation(dst, src, ACT.Copy).then_inc(p_copied.h, 1)
                        N = len(items)

                        def square(n):
                            t, m = items[n]
                            act.wait_ge(o_taken.h, q[o_taken] + n + 1)
                            if n:
                                act.wait_ge(sq_ready.h, sq_ready.n)
                            sq_ready.n += 1
                            nc.scalar.activation(actout[:, 0:vw], o[:, m, t * vw:(t + 1) * vw], ACT.Square,
                                                 accum_out=squares(t, m)).then_inc(sq_ready.h, 1)
                        for n in range(N + (3 if squares else 1)):
                            if squares and n >= 3:
                                square(n - 3)
                            if n < N:
                                if sink is not None:
                                    act.wait_ge(bias_ready.h, q[bias_ready] + n + 1)
                                    nc.scalar.activation(es[:, n % 2], es[:, n % 2], ACT.Exp)
                                exps(n)
                            if 1 <= n <= N:
                                copy(n - 1)
                        if squares:
                            square(N - 1)
            N = len(items)
            for s in (scores_ready, s_taken, bias_ready, p_turned, p_copied, o_ready, o_taken):
                s.n += N
            p_ready.n += 2 * N
            if lam is not None:
                w_ready.n += N

        def out_projection(stream, o, scale=None):
            with ExitStack() as ctx:
                pre = Pre(ctx)
                pre.turn(lambda m, k: o[:, m, k * P:(k + 1) * P], K8, hT_hi, hT_lo, scale)
                project(stream, hT, keep=True, pre=pre)

        with ExitStack() as ctx:
            qkv = sb(ctx, "qkv", [P, M, 3 * D])
            with ExitStack() as ctx2:
                pre = Pre(ctx2)
                pre.modulate(B_KV, 96, 104)
                project(s_k, hT, evac_act=to_sbuf(qkv[:, :, D:2 * D], D), pre=pre)
            project(s_v, hT, evac_act=to_sbuf(qkv[:, :, 2 * D:], D))
            with ExitStack() as ctx2:
                pre = Pre(ctx2)
                pre.modulate(B_MIX + 8, 48, 56)
                project(s_q, hT, evac_act=to_sbuf(qkv[:, :, 0:D], D), pre=pre)
            o = sb(ctx, "o", [P, M, D])
            qT = sb(ctx, "qT", [P, K8, S])
            kT = sb(ctx, "kT", [P, K8, S])
            mask, mask_pool = make_masks(ctx, False)
            pe_part, act_part = heads_to_feature(
                [(qT[:, t], lambda m, t=t: qkv[:, m, t * P:(t + 1) * P]) for t in range(K8)] +
                [(kT[:, t], lambda m, t=t: qkv[:, m, D + t * P:D + (t + 1) * P]) for t in range(K8)])
            with nc.Block() as block:
                block.tensor(pe_part)
                block.scalar(act_part)
                block.gpsimd(mask_pool)
            softmax_attention(qT, lambda t: kT[:, t],
                              lambda t, c, j: qkv[:, j, 2 * D + (2 * t + c) * HD:2 * D + (2 * t + c + 1) * HD], o, mask)
            out_projection(s_o, o)
        if stop == "moba":
            add_alone(lambda pre: pre.add_gated(0))
            return finish()
        moe(1)
        if stop == "moe1":
            return finish()
        final_landed = sem("final_gain_landed")

        def norm_x():
            with ExitStack() as ctx:
                gain = sb(ctx, "final_gain", [P, D])
                sums = sb(ctx, "final_sums", [P, 3, M])
                act_part, reciprocal = root_parts(sums, lambda m: x[:, m], D, RMS_EPS)
                with nc.Block() as block:
                    @block.sync
                    def _(sp):
                        sp.dma_start(gain[:], a["final_norm"].rearrange("(o d) -> o d", o=1).broadcast_to([P, D])) \
                            .then_inc(final_landed.h, 16)
                    block.scalar(act_part)

                    @block.vector
                    def _(dve):
                        step = Chain(dve, dve_step)
                        dve.wait_ge(final_landed.h, 16)
                        for m in range(M):
                            r = reciprocal(dve, step, m)
                            nc.vector.scalar_tensor_tensor(x[:, m], x[:, m], r, gain[:], ALU.mult, ALU.mult)
        norm_x()
        if stop == "first":
            return finish()

        trig = sb(top, "trig", [P, 2, M, 32])
        with ExitStack() as ctx:
            pos = sb(ctx, "pos", [P, M], I32)
            posf = sb(ctx, "posf", [P, M])
            fr = sb(ctx, "freq", [P, 32])
            an = sb(ctx, "angle", [P, 2, M, 32])
            tn = sb(ctx, "turns", [P, 2, M, 32])
            ti = sb(ctx, "turns_i", [P, 2, M, 32], I32)
            pos_landed, an_ready = sem("pos_landed"), sem("angle_ready")
            with nc.Block() as block:
                @block.sync
                def _(sp):
                    for m in range(M):
                        sp.dma_start(pos[:, m:m + 1], a["positions_2"][0:1, m * P:(m + 1) * P]
                                     .rearrange("o (p q) -> (o p) q", q=1)).then_inc(pos_landed.h, 16)
                    sp.dma_start(fr[:], a["rope_freq"].broadcast_to([P, 32])).then_inc(pos_landed.h, 16)

                @block.vector
                def _(dve):
                    step = Chain(dve, dve_step)
                    dve.wait_ge(pos_landed.h, 48)
                    step(nc.vector.tensor_copy(posf[:], pos[:]))
                    for m in range(M):
                        step(nc.vector.tensor_scalar(an[:, 1, m], fr[:], posf[:, m:m + 1], None, ALU.mult))
                    TWO_PI = 2 * math.pi
                    step(nc.vector.tensor_scalar(tn[:, 1], an[:, 1], 1 / TWO_PI, None, ALU.mult))
                    step(nc.vector.tensor_scalar(tn[:, 0], an[:, 1], 1 / TWO_PI, 0.25, ALU.mult, ALU.add))
                    step(nc.vector.tensor_copy(ti[:], tn[:]))
                    step(nc.vector.tensor_copy(tn[:], ti[:]))
                    c1 = 6.28125
                    c2 = math.floor((TWO_PI - c1) * 2 ** 21) / 2 ** 21
                    c3 = TWO_PI - c1 - c2
                    step(nc.vector.scalar_tensor_tensor(an[:, 0], tn[:, 0], -c1, an[:, 1], ALU.mult, ALU.add))
                    step(nc.vector.scalar_tensor_tensor(an[:, 1], tn[:, 1], -c1, an[:, 1], ALU.mult, ALU.add))
                    step(nc.vector.scalar_tensor_tensor(an[:], tn[:], -c2, an[:], ALU.mult, ALU.add))
                    step(nc.vector.scalar_tensor_tensor(an[:], tn[:], -c3, an[:], ALU.mult, ALU.add))
                    step(nc.vector.tensor_scalar(an[:, 0], an[:, 0], math.pi / 2, None, ALU.add))
                    step(nc.vector.tensor_scalar(tn[:], an[:], math.pi, -TWO_PI, ALU.is_gt, ALU.mult))
                    step(nc.vector.tensor_tensor(an[:], an[:], tn[:], ALU.add))
                    step(nc.vector.tensor_scalar(tn[:], an[:], -math.pi, TWO_PI, ALU.is_lt, ALU.mult))
                    step(nc.vector.tensor_tensor(an[:], an[:], tn[:], ALU.add))
                    edge = 3.14159250
                    nc.vector.tensor_scalar(an[:], an[:], edge, -edge, ALU.min, ALU.max).then_inc(an_ready.h, 1)

                @block.scalar
                def _(act):
                    act.wait_ge(an_ready.h, 1)
                    nc.scalar.activation(trig[:], an[:], ACT.Sin)

        def rope_beside(t1, t2, buf, heads):
            free0 = out_free.n

            def run(pool):
                step = Chain(pool, pool_step)
                for c in range(-(-heads // 8)):
                    nh = min(8, heads - 8 * c)
                    pool.wait_ge(out_free.h, free0 + 2 * c + 2)
                    for m in range(M):
                        v = buf[:, m, c * NB:c * NB + nh * HD].rearrange("p (h c e) -> p h c e", c=2, e=32)
                        cos = trig[:, 0, m].unsqueeze(1).broadcast_to([P, nh, 32])
                        sin = trig[:, 1, m].unsqueeze(1).broadcast_to([P, nh, 32])
                        e = nc.gpsimd
                        step(e.tensor_tensor(t1[:, 0:nh], v[:, :, 0], sin, ALU.mult))
                        step(e.tensor_tensor(t2[:, 0:nh], v[:, :, 1], sin, ALU.mult))
                        step(e.tensor_tensor(v[:, :, 0], v[:, :, 0], cos, ALU.mult))
                        step(e.tensor_tensor(v[:, :, 1], v[:, :, 1], cos, ALU.mult))
                        step(e.tensor_tensor(v[:, :, 0], v[:, :, 0], t2[:, 0:nh], ALU.subtract))
                        step(e.tensor_tensor(v[:, :, 1], v[:, :, 1], t1[:, 0:nh], ALU.add))
            return run

        lam_landed, lam_exp, sink_landed = sem("lam_landed"), sem("lam_exp"), sem("sink_landed")
        for layer in range(4):
            kind, inst = layer % 3, layer // 3
            s_in2, s_out2, s_ffn = second[layer]
            gain = layer * 4 * K8
            with ExitStack() as ctx:
                width = s_in2.n * NB if kind != 2 else 10 * P
                qkv = sb(ctx, "qkv", [P, M, width])
                beside = None
                if kind != 1:
                    t1 = sb(ctx, "rope_a", [P, 8, 32])
                    t2 = sb(ctx, "rope_b", [P, 8, 32])
                    beside = rope_beside(t1, t2, qkv, 4 * 8 if kind == 0 else 18)
                with ExitStack() as ctx2:
                    pre = Pre(ctx2)
                    if layer:
                        pre.add_normed((layer - 1, 3))
                    pre.norm(lambda k: featC[:, gain + k:gain + k + 1])
                    project(s_in2, hT, evac_act=to_sbuf(qkv, width), beside=beside, pre=pre)
                o = sb(ctx, "o", [P, M, D])
                qT = sb(ctx, "qT", [P, K8, S])
                scale = None
                if kind == 0:
                    lam_init = 0.8 - 0.6 * math.exp(-0.3 * layer)
                    kT = sb(ctx, "kT", [P, K8, S])
                    mask, mask_pool = make_masks(ctx, False)
                    lp = sb(ctx, "lam_params", [P, 4, HD])
                    lt = sb(ctx, "lam_terms", [P, 4])
                    pe_part, act_part = heads_to_feature(
                        [(qT[:, t], lambda m, t=t: qkv[:, m, t * P:(t + 1) * P]) for t in range(K8)] +
                        [(kT[:, t], lambda m, t=t: qkv[:, m, D + t * P:D + (t + 1) * P]) for t in range(K8)])
                    with nc.Block() as block:
                        block.tensor(pe_part)
                        block.gpsimd(mask_pool)

                        @block.sync
                        def _(sp):
                            sp.dma_start(lp[:].rearrange("p a b -> p (a b)"),
                                         a["a_lambda_2"][inst:inst + 1].rearrange("i a b -> i (a b)")
                                         .broadcast_to([P, 4 * HD])).then_inc(lam_landed.h, 16)

                        @block.vector
                        def _(dve):
                            step = Chain(dve, dve_step)
                            dve.wait_ge(lam_landed.h, lam_landed.n + 16)
                            for c in range(2):
                                step(nc.vector.tensor_tensor(lp[:, 2 * c], lp[:, 2 * c], lp[:, 2 * c + 1], ALU.mult))
                                step(nc.vector.reduce_sum(lt[:, c:c + 1], lp[:, 2 * c], AX))
                            nc.vector.tensor_copy(lt[:, 2:4], lt[:, 0:2]).then_inc(lam_exp.h, 1)
                            dve.wait_ge(lam_exp.h, lam_exp.n + 2)
                            step(nc.vector.tensor_tensor(lt[:, 2:3], lt[:, 1:2], lt[:, 0:1], ALU.subtract))
                            step(nc.vector.tensor_scalar(lt[:, 3:4], lt[:, 2:3], -lam_init, None, ALU.add))

                        @block.scalar
                        def _(act):
                            act_part(act)
                            act.wait_ge(lam_exp.h, lam_exp.n + 1)
                            nc.scalar.activation(lt[:, 0:2], lt[:, 2:4], ACT.Exp).then_inc(lam_exp.h, 1)
                    lam_landed.n += 16
                    lam_exp.n += 2
                    hs = sb(ctx, "head_ss", [P, 3, M, K8])
                    softmax_attention(qT, lambda t: kT[:, t],
                                      lambda t, c, j: qkv[:, j, 2 * D + t * P:2 * D + (t + 1) * P], o, mask,
                                      lam=lt[:, 3:4], vw=P, squares=lambda t, m: hs[:, 0, m, t:t + 1])
                    with nc.Block() as block:
                        hs_ready = sem("head_ss_ready")

                        @block.vector
                        def _(dve):
                            step = Chain(dve, dve_step)
                            dve.wait_ge(hs_ready.h, hs_ready.n + 1)
                            step(nc.vector.reciprocal(hs[:, 2], hs[:, 1]))
                            step(nc.vector.tensor_scalar(hs[:, 2], hs[:, 2], 1.0 - lam_init, None, ALU.mult))
                            for m in range(M):
                                r = hs[:, 2, m].unsqueeze(2).broadcast_to([P, K8, P])
                                ov = o[:, m].rearrange("p (h e) -> p h e", e=P)
                                step(nc.vector.tensor_tensor(ov, ov, r, ALU.mult))

                        @block.scalar
                        def _(act):
                            nc.scalar.activation(hs[:, 1], hs[:, 0], ACT.Sqrt, scale=1.0 / P, bias=eps_of[RMS_EPS]) \
                                .then_inc(hs_ready.h, 1)
                    hs_ready.n += 1
                    sub = featB[:, B_SUB + inst:B_SUB + inst + 1]
                    scale = lambda k: sub
                elif kind == 1:
                    kT = sb(ctx, "kT", [P, K8, S])
                    stick_breaking(nc, sb, sem, ctx, qkv, qT, kT, o, heads_to_feature, K8, M, D, S,
                                   psG, psT, psA, dve_step, pool_step)
                else:
                    kd = sb(ctx, "k_twice", [P, M, 4, HD])
                    kT = sb(ctx, "kT2", [P, 2, S])
                    sinks = sb(ctx, "sinks", [P, 16])
                    mask, mask_pool = make_masks(ctx, True)
                    with nc.Block() as block:
                        block.gpsimd(mask_pool)

                        @block.sync
                        def _(sp):
                            sp.dma_start(sinks[:], a["c_sinks_2"][inst:inst + 1].broadcast_to([P, 16])) \
                                .then_inc(sink_landed.h, 16)
                            sp.wait_ge(sink_landed.h, sink_landed.n + 16)

                        @block.vector
                        def _(dve):
                            for m in range(M):
                                for r in range(4):
                                    o0 = D + (r // 2) * HD
                                    nc.vector.tensor_copy(kd[:, m, r], qkv[:, m, o0:o0 + HD])
                    sink_landed.n += 16
                    pe_part, act_part = heads_to_feature(
                        [(qT[:, t], lambda m, t=t: qkv[:, m, t * P:(t + 1) * P]) for t in range(K8)] +
                        [(kT[:, t], lambda m, t=t: kd[:, m, 2 * t:2 * t + 2].rearrange("p r e -> p (r e)"))
                         for t in range(2)])
                    with nc.Block() as block:
                        block.tensor(pe_part)
                        block.scalar(act_part)
                    softmax_attention(qT, lambda t: kT[:, t // 4],
                                      lambda t, c, j: qkv[:, j, D + 2 * HD + (t // 4) * HD:D + 2 * HD + (t // 4 + 1) * HD],
                                      o, mask, window=True, sink=sinks)
                out_projection(s_out2, o, scale)
            if stop == f"mix{layer}":
                add_alone(lambda pre: pre.add_normed((layer, 1)))
                return finish()
            gain2 = gain + 2 * K8
            with ExitStack() as ctx:
                pre = Pre(ctx, psA)
                pre.add_normed((layer, 1))
                pre.norm(lambda k: featC[:, gain2 + k:gain2 + k + 1])
                gated_units(s_ffn, pre=pre)
            if stop == f"ffn{layer}" or layer == 3:
                add_alone(lambda pre: pre.add_normed((layer, 3)))
                return finish()


def stick_breaking(nc, sb, sem, ctx, qkv, qT, kT, o, heads_to_feature, K8, M, D, S, psG, psT, psA, dve_step, pool_step):
    W = 3 * P
    see = sb(ctx, "seen", [P, W])
    later = sb(ctx, "later", [P, P])
    allk = sb(ctx, "all_ones", [P, P])
    pe_part, act_part = heads_to_feature(
        [(qT[:, t], lambda m, t=t: qkv[:, m, t * P:(t + 1) * P]) for t in range(K8)] +
        [(kT[:, t], lambda m, t=t: qkv[:, m, D + t * P:D + (t + 1) * P]) for t in range(K8)])
    with nc.Block() as block:
        block.tensor(pe_part)
        block.scalar(act_part)

        @block.gpsimd
        def _(pool):
            step = Chain(pool, pool_step)
            nc.gpsimd.memset(allk[:], 1.0)
            step(nc.gpsimd.memset(see[:], 1.0))
            step(nc.gpsimd.memset(later[:], 1.0))
            for s in (slice(0, P), slice(2 * P, W)):
                nc.gpsimd.affine_select(out=see[:, s], in_=see[:, s], compare_op=ALU.is_gt, fill=0.0, base=0,
                                        pattern=[[1, P]], channel_multiplier=-1)
            step(nc.gpsimd.affine_select(out=later[:], in_=later[:], compare_op=ALU.is_gt, fill=0.0, base=0,
                                         pattern=[[-1, P]], channel_multiplier=1))
    s_ready = sem("s_ready")
    z_ready, az_ready, ln_ready, L_ready, suf_ready, t_ready, e_ready, a_ready, so_ready, so_taken = (
        sem(n) for n in ("z_ready", "abs_z_ready", "log1p_ready", "log_rest_ready", "suffix_ready",
                         "log_a_ready", "exp_a_ready", "a_ready", "stick_o_ready", "stick_o_taken"))
    with ExitStack() as c2, nc.Block() as block:
        az, Lm = (qkv[:, m, 0:4 * W].rearrange("p (b c w) -> p b c w", b=2, c=2) for m in range(2))
        rl = sb(c2, "relu_z", [P, 2, 2, W])
        tt = sb(c2, "log_a", [P, 3, 2, W])
        zbanks = (psG[:, :, 0:W], psA[:, 2:4, 0:W])

        @block.tensor
        def _(pe):
            def scores(n):
                if n >= 2:
                    pe.wait_ge(s_ready.h, n - 1)
                for c in range(2):
                    r = slice(HD * c, HD * (c + 1))
                    z = zbanks[n % 2][:, c]
                    nc.tensor.matmul(z[:, 0:2 * P], kT[r, n, 0:P], qT[r, n, :], start=True, stop=True)
                    last = nc.tensor.matmul(z[:, 2 * P:W], kT[r, n, P:2 * P], qT[r, n, P:2 * P], start=True, stop=True)
                last.then_inc(z_ready.h, 1)

            def suffix(n):
                pe.wait_ge(L_ready.h, 2 * n + 1)
                if n >= 1:
                    pe.wait_ge(t_ready.h, n)
                for c in range(2):
                    nc.tensor.matmul(psT[:, c, 0:W], later[:], Lm[:, n % 2, c], start=True, stop=False)
                    last = nc.tensor.matmul(psT[:, c, P:2 * P], allk[:], Lm[:, n % 2, c, 2 * P:W],
                                            start=False, stop=True)
                last.then_inc(suf_ready.h, 1)

            def values(n):
                pe.wait_ge(a_ready.h, n + 1)
                if n >= 2:
                    pe.wait_ge(so_taken.h, n - 1)
                for c in range(2):
                    v = [qkv[:, j, 2 * D + (2 * n + c) * HD:2 * D + (2 * n + c + 1) * HD] for j in range(2)]
                    p = tt[:, n % 3, c]
                    first, second = (psA[:, n % 2, (2 * c + m) * HD:(2 * c + m + 1) * HD] for m in range(2))
                    nc.tensor.matmul(first, p[:, 0:P], v[0], start=True, stop=True)
                    nc.tensor.matmul(second, p[:, P:2 * P], v[0], start=True, stop=False)
                    last = nc.tensor.matmul(second, p[:, 2 * P:W], v[1], start=False, stop=True)
                last.then_inc(so_ready.h, 1)
            scores(0)
            for n in range(K8 + 2):
                if n + 1 < K8:
                    scores(n + 1)
                if 1 <= n <= K8:
                    suffix(n - 1)
                if n >= 2:
                    values(n - 2)

        @block.scalar
        def _(act):
            def logs(n):
                b = n % 2
                act.wait_ge(az_ready.h, n + 1)
                if n >= 3:
                    act.wait_ge(so_ready.h, n - 2)
                nc.scalar.activation(tt[:, n % 3], zbanks[b], ACT.Copy, scale=ATT_SCALE).then_inc(s_ready.h, 1)
                nc.scalar.activation(az[:, b], az[:, b], ACT.Exp, scale=-ATT_SCALE).then_inc(ln_ready.h, 1)
                act.wait_ge(ln_ready.h, 2 * n + 1)
                nc.scalar.activation(az[:, b], az[:, b], ACT.Ln, bias=1.0).then_inc(ln_ready.h, 1)

            def exps(n):
                act.wait_ge(t_ready.h, n + 1)
                nc.scalar.activation(tt[:, n % 3], tt[:, n % 3], ACT.Exp).then_inc(e_ready.h, 1)
            for n in range(K8 + 1):
                if n < K8:
                    logs(n)
                if n >= 1:
                    exps(n - 1)

        @block.vector
        def _(dve):
            step = Chain(dve, dve_step)

            def absolute(n):
                b, z = n % 2, zbanks[n % 2]
                if n >= 2:
                    dve.wait_ge(L_ready.h, 2 * (n - 1))
                dve.wait_ge(z_ready.h, n + 1)
                step(nc.vector.tensor_scalar(rl[:, b], z, 0.0, None, ALU.max))
                nc.vector.scalar_tensor_tensor(az[:, b], rl[:, b], 2.0, z, ALU.mult, ALU.subtract) \
                    .then_inc(az_ready.h, 1)

            def front(n):
                b = n % 2
                dve.wait_ge(az_ready.h, n + 1)
                dve.wait_ge(ln_ready.h, 2 * n + 2)
                step(nc.vector.scalar_tensor_tensor(rl[:, b], rl[:, b], -ATT_SCALE, az[:, b], ALU.mult, ALU.subtract))
                nc.vector.tensor_tensor(Lm[:, b], rl[:, b], see[:].unsqueeze(1).broadcast_to([P, 2, W]), ALU.mult) \
                    .then_inc(L_ready.h, 1)
                nc.vector.tensor_tensor(tt[:, n % 3], tt[:, n % 3], rl[:, b], ALU.add).then_inc(L_ready.h, 1)

            def middle(n):
                dve.wait_ge(L_ready.h, 2 * n + 2)
                dve.wait_ge(suf_ready.h, n + 1)
                nc.vector.tensor_tensor(tt[:, n % 3], tt[:, n % 3], psT[:, :, 0:W], ALU.add).then_inc(t_ready.h, 1)

            def late(n):
                dve.wait_ge(e_ready.h, n + 1)
                nc.vector.tensor_tensor(tt[:, n % 3], tt[:, n % 3], see[:].unsqueeze(1).broadcast_to([P, 2, W]),
                                        ALU.mult).then_inc(a_ready.h, 1)

            def back(n):
                dve.wait_ge(so_ready.h, n + 1)
                nc.vector.tensor_copy(o[:, :, n * P:(n + 1) * P].rearrange("p m (c e) -> p c m e", c=2),
                                      psA[:, n % 2, 0:4 * HD].rearrange("p (c m e) -> p c m e", c=2, m=2)) \
                    .then_inc(so_taken.h, 1)
            absolute(0)
            for n in range(K8 + 2):
                if n + 1 < K8:
                    absolute(n + 1)
                if n >= 2:
                    late(n - 2)
                if 1 <= n <= K8:
                    middle(n - 1)
                if n < K8:
                    front(n)
                if n >= 2:
                    back(n - 2)


_INS = ["x", "c", "ada_w", "ada_b", "norm_mix", "norm_ffn", "a_w_in", "a_b_in", "a_ln_g", "a_ln_b", "a_w_s", "a_b_s",
        "a_w_out", "kv_norm", "kv_ada_w", "kv_ada_b", "kv_w_k", "kv_w_v", "b_w_q", "b_w_o", "moe_router", "moe_bias",
        "moe_w_gate", "moe_w_up", "moe_w_down", "sh_w_gate", "sh_w_up", "sh_w_down", "final_norm", "positions_2",
        "norm_gains_2", "a_w_in_2", "a_w_out_2", "a_lambda_2", "a_subln_2", "b_w_in_2", "b_w_out_2", "c_w_in_2",
        "c_w_out_2", "c_sinks_2", "ffn_w_gate_2", "ffn_w_up_2", "ffn_w_down_2"]
STOP = None


def kernel(**inputs):
    import numpy as np
    import concourse.bacc as bacc
    from concourse.bass_utils import run_bass_kernel_spmd

    nc = bacc.Bacc("TRN2", target_bir_lowering=False, num_devices=1)
    freq = (ROPE_THETA ** (-np.arange(0, HD, 2, dtype=np.float32) / np.float32(HD))).astype(np.float32)
    arrays, args = {}, {}
    for name in _INS + ["rope_freq"]:
        arr = freq[None] if name == "rope_freq" else np.ascontiguousarray(inputs[name])
        arrays[f"in_{name}"] = arr
        args[name] = nc.dram_tensor(f"in_{name}", arr.shape, mybir.dt.from_np(arr.dtype), kind="ExternalInput").ap()
    out = nc.dram_tensor("out", inputs["x"].shape, F32, kind="ExternalOutput").ap()
    build(nc, args, out, STOP)
    r = run_bass_kernel_spmd(nc, [arrays], core_ids=[0])
    return r.results[0]["out"]
```
